# Optimizing a Trainium2 kernel written in Bass

```python
import math
import jax, jax.numpy as jnp
from jax import lax
import numpy as np
import jax
import jax.numpy as jnp

D_MODEL = 2048
BATCH = 1
SEQ = 256
DEPTH = 1

HEAD_DIM = 128
N_MEM = 256
GRID_W = 64
DIL_PAIRS = ((128, 1), (512, 4), (2048, 16))
A_HEADS_PER_GROUP = 2
A_HEADS = A_HEADS_PER_GROUP * len(DIL_PAIRS)
A_BLOCK = 64
B_Q_HEADS = 6
B_KV_HEADS = 2
B_QBLOCK = 128
ROPE_THETA = 10000.0
C_HEADS = 4
N_BRANCH = 3
REL_BUCKETS = 32
REL_MAX_DIST = 1024
D_FF = -(-8 * D_MODEL // (3 * 256)) * 256
EPS = 1e-6
NEG = -1e30

A_W = A_HEADS * HEAD_DIM
A_OUT_W = A_HEADS_PER_GROUP * HEAD_DIM
B_QW = B_Q_HEADS * HEAD_DIM
B_KVW = B_KV_HEADS * HEAD_DIM
C_W = C_HEADS * HEAD_DIM
IN_SPLITS = (A_W, A_W, A_W, B_QW, B_KVW, B_KVW, C_W, N_BRANCH * D_MODEL)
IN_W = sum(IN_SPLITS)


def rms_norm(x, g):
    xf = x.astype(jnp.float32)
    y = xf * lax.rsqrt(jnp.mean(xf * xf, axis=-1, keepdims=True) + EPS)
    return (y * g.astype(jnp.float32)).astype(x.dtype)

def split_heads(t, h):
    return t.reshape(t.shape[0], t.shape[1], h, HEAD_DIM)

def t5_bucket(rel):
    nb = REL_BUCKETS // 2
    ret = jnp.where(rel > 0, nb, 0)
    n = jnp.abs(rel)
    max_exact = nb // 2
    large = max_exact + (jnp.log(jnp.maximum(n, 1).astype(jnp.float32) / max_exact)
                         / math.log(REL_MAX_DIST / max_exact) * (nb - max_exact)).astype(jnp.int32)
    large = jnp.minimum(large, nb - 1)
    return ret + jnp.where(n < max_exact, n, large)

def dilated_group(q, k, v, bias_tab, window, dil):
    b, s, h, dh = q.shape
    L = s // dil
    radius = window // (2 * dil)
    n = b * dil

    def to_res(t):
        return t.reshape(b, L, dil, h, dh).transpose(0, 2, 1, 3, 4).reshape(n, L, h, dh)

    qr, kr, vr = to_res(q), to_res(k), to_res(v)
    nb = -(-L // A_BLOCK)
    lp = nb * A_BLOCK
    side = -(-radius // A_BLOCK)
    pad = side * A_BLOCK
    wk = (2 * side + 1) * A_BLOCK
    qb = jnp.pad(qr, ((0, 0), (0, lp - L), (0, 0), (0, 0))).reshape(n, nb, A_BLOCK, h, dh)

    def band(t):
        tp = jnp.pad(t, ((0, 0), (pad, lp - L + pad), (0, 0), (0, 0))).reshape(n, nb + 2 * side, A_BLOCK, h, dh)
        return jnp.concatenate([tp[:, i:i + nb] for i in range(2 * side + 1)], axis=2)

    kb, vb = band(kr), band(vr)
    rel = (jnp.arange(wk) - pad)[None, :] - jnp.arange(A_BLOCK)[:, None]
    bias = bias_tab[t5_bucket(rel * dil)].transpose(2, 0, 1).astype(jnp.float32)
    k_pos = jnp.arange(nb)[:, None] * A_BLOCK - pad + jnp.arange(wk)[None, :]
    valid = (jnp.abs(rel) <= radius)[None] & ((k_pos >= 0) & (k_pos < L))[:, None, :]
    sc = jnp.einsum('nbqhd,nbkhd->nbhqk', qb, kb, preferred_element_type=jnp.float32) / math.sqrt(dh)
    sc = jnp.where(valid[None, :, None], sc + bias[None, None], NEG)
    m = jnp.max(sc, axis=-1, keepdims=True)
    p = jnp.exp(sc - m)
    l = jnp.sum(p, axis=-1, keepdims=True)
    o = jnp.einsum('nbhqk,nbkhd->nbqhd', p, vb.astype(jnp.float32))
    o = o / l[..., 0].transpose(0, 1, 3, 2)[..., None]
    lse = (m + jnp.log(l))[..., 0].transpose(0, 1, 3, 2)
    o = o.reshape(n, lp, h, dh)[:, :L]
    lse = lse.reshape(n, lp, h)[:, :L]
    o = o.reshape(b, dil, L, h, dh).transpose(0, 2, 1, 3, 4).reshape(b, s, h, dh)
    lse = lse.reshape(b, dil, L, h).transpose(0, 2, 1, 3).reshape(b, s, h)
    return o, lse

def axial_rope_tables(s):
    rows = s // GRID_W
    r = jnp.repeat(jnp.arange(rows), GRID_W).astype(jnp.float32)
    c = jnp.tile(jnp.arange(GRID_W), rows).astype(jnp.float32)
    nf = HEAD_DIM // 4
    inv = ROPE_THETA ** (-jnp.arange(nf, dtype=jnp.float32) / nf)
    ang = jnp.concatenate([r[:, None] * inv, c[:, None] * inv], axis=-1)
    return jnp.cos(ang), jnp.sin(ang)

def apply_rope(x, cos, sin):
    b, s, h, dh = x.shape
    xf = x.astype(jnp.float32).reshape(b, s, h, dh // 2, 2)
    x0, x1 = xf[..., 0], xf[..., 1]
    c, sn = cos[None, :, None, :], sin[None, :, None, :]
    out = jnp.stack([x0 * c - x1 * sn, x0 * sn + x1 * c], axis=-1)
    return out.reshape(b, s, h, dh).astype(x.dtype)

def gqa_blocks(q, k, v):
    b, s, hq, dh = q.shape
    g = hq // B_KV_HEADS
    nblk = s // B_QBLOCK
    qb = q.reshape(b, nblk, B_QBLOCK, B_KV_HEADS, g, dh).transpose(1, 0, 2, 3, 4, 5)

    def one_block(qq):
        sc = jnp.einsum('bqkgd,bskd->bkgqs', qq, k, preferred_element_type=jnp.float32) / math.sqrt(dh)
        p = jax.nn.softmax(sc, axis=-1)
        return jnp.einsum('bkgqs,bskd->bqkgd', p, v.astype(jnp.float32)).astype(q.dtype)

    o = lax.map(one_block, qb)
    return o.transpose(1, 0, 2, 3, 4, 5).reshape(b, s, hq * dh)

def first_inputs(seed: int = 0) -> dict:
    key = jax.random.key(seed)
    ks = jax.random.split(key, 24)
    f32 = jnp.float32

    def w(k, shape, fan_in):
        return jax.random.normal(k, shape, f32) * (fan_in ** -0.5)

    def gain(k, shape):
        return 1.0 + 0.05 * jax.random.normal(k, shape, f32)

    Dp = DEPTH
    return {
        "x": jax.random.normal(ks[0], (BATCH, SEQ, D_MODEL), f32),
        "mem": jax.random.normal(ks[1], (BATCH, N_MEM, D_MODEL), f32),
        "rel_bias": 0.5 * jax.random.normal(ks[2], (REL_BUCKETS, A_HEADS), f32),
        "g_mix": gain(ks[3], (Dp, D_MODEL)),
        "w_in": w(ks[4], (Dp, D_MODEL, IN_W), D_MODEL),
        "g_qa": gain(ks[5], (Dp, HEAD_DIM)),
        "g_ka": gain(ks[6], (Dp, HEAD_DIM)),
        "g_qb": gain(ks[7], (Dp, HEAD_DIM)),
        "g_kb": gain(ks[8], (Dp, HEAD_DIM)),
        "g_mem": gain(ks[9], (Dp, D_MODEL)),
        "w_mem_kv": w(ks[10], (Dp, D_MODEL, 2 * C_W), D_MODEL),
        "g_qc": gain(ks[11], (Dp, HEAD_DIM)),
        "g_kc": gain(ks[12], (Dp, HEAD_DIM)),
        "w_br_a": w(ks[13], (Dp, A_OUT_W, D_MODEL), A_OUT_W),
        "w_br_b": w(ks[14], (Dp, B_QW, D_MODEL), B_QW),
        "w_br_c": w(ks[15], (Dp, C_W, D_MODEL), C_W),
        "w_o": w(ks[16], (Dp, D_MODEL, D_MODEL), D_MODEL),
        "g_ffn": gain(ks[17], (Dp, D_MODEL)),
        "w_ffn_in": w(ks[18], (Dp, D_MODEL, 2 * D_FF), D_MODEL),
        "w_ffn_out": w(ks[19], (Dp, D_FF, D_MODEL), D_FF),
    }

def first_block(x, mem, rel_bias, g_mix, w_in, g_qa, g_ka, g_qb, g_kb, g_mem, w_mem_kv,
              g_qc, g_kc, w_br_a, w_br_b, w_br_c, w_o, g_ffn, w_ffn_in, w_ffn_out):
    b, s, _ = x.shape
    cos, sin = axial_rope_tables(s)
    offs = np.cumsum((0,) + IN_SPLITS)
    for layer in range(DEPTH):
        h = rms_norm(x, g_mix[layer])
        proj = h @ w_in[layer]
        qa, ka, va, qb, kb, vb, qc, gt = [proj[..., offs[i]:offs[i + 1]] for i in range(len(IN_SPLITS))]

        qa = rms_norm(split_heads(qa, A_HEADS), g_qa[layer])
        ka = rms_norm(split_heads(ka, A_HEADS), g_ka[layer])
        va = split_heads(va, A_HEADS)
        outs, lses = [], []
        for gi, (win, dil) in enumerate(DIL_PAIRS):
            sl = slice(gi * A_HEADS_PER_GROUP, (gi + 1) * A_HEADS_PER_GROUP)
            o, lse = dilated_group(qa[:, :, sl], ka[:, :, sl], va[:, :, sl], rel_bias[:, sl], win, dil)
            outs.append(o)
            lses.append(lse)
        wgt = jax.nn.softmax(jnp.stack(lses), axis=0)
        oa = jnp.sum(wgt[..., None] * jnp.stack(outs), axis=0).reshape(b, s, A_OUT_W).astype(x.dtype)

        qb = apply_rope(rms_norm(split_heads(qb, B_Q_HEADS), g_qb[layer]), cos, sin)
        kb = apply_rope(rms_norm(split_heads(kb, B_KV_HEADS), g_kb[layer]), cos, sin)
        ob = gqa_blocks(qb, kb, split_heads(vb, B_KV_HEADS))

        mkv = rms_norm(mem, g_mem[layer]) @ w_mem_kv[layer]
        kc = rms_norm(split_heads(mkv[..., :C_W], C_HEADS), g_kc[layer])
        vc = split_heads(mkv[..., C_W:], C_HEADS)
        qc = rms_norm(split_heads(qc, C_HEADS), g_qc[layer])
        sc = jnp.einsum('bqhd,bmhd->bhqm', qc, kc, preferred_element_type=jnp.float32) / math.sqrt(HEAD_DIM)
        pc = jax.nn.softmax(sc, axis=-1)
        oc = jnp.einsum('bhqm,bmhd->bqhd', pc, vc.astype(jnp.float32)).reshape(b, s, C_W).astype(x.dtype)

        gates = jax.nn.sigmoid(gt.astype(jnp.float32)).reshape(b, s, N_BRANCH, D_MODEL)
        merged = (gates[:, :, 0] * (oa @ w_br_a[layer]).astype(jnp.float32)
                  + gates[:, :, 1] * (ob @ w_br_b[layer]).astype(jnp.float32)
                  + gates[:, :, 2] * (oc @ w_br_c[layer]).astype(jnp.float32)).astype(x.dtype)
        x = x + merged @ w_o[layer]

        hf = rms_norm(x, g_ffn[layer]) @ w_ffn_in[layer]
        x = x + (jax.nn.silu(hf[..., :D_FF]) * hf[..., D_FF:]) @ w_ffn_out[layer]
    return x


NSA_HEADS = 16
NSA_KV_GROUPS = 4
HEADS_PER_GROUP = NSA_HEADS // NSA_KV_GROUPS
NSA_WIDTH = NSA_HEADS * HEAD_DIM
KV_WIDTH = NSA_KV_GROUPS * HEAD_DIM
CMP_LEN = 32
CMP_STRIDE = 16
SLC_LEN = 64
SLC_TOP_N = 16
SLC_LOCAL = 2
FORCE_BONUS = 1e4
WINDOW = 512
WIN_Q_BLOCK = 128
SLC_Q_BLOCK = 32

LRU_WIDTH = 2048
LRU_BLOCKS = 16
LRU_BLOCK_DIM = LRU_WIDTH // LRU_BLOCKS
LRU_C = 8.0
LRU_CONV = 4

D_FF_2 = 3 * D_MODEL
FFN_CONV = 3

IN_WIDTH = NSA_WIDTH + 6 * KV_WIDTH + 3 * NSA_HEADS + 2 * LRU_WIDTH + 2 * D_MODEL
NORM_EPS = 1e-6


def rmsnorm(x, g):
    x32 = x.astype(jnp.float32)
    inv = lax.rsqrt(jnp.mean(x32 * x32, axis=-1, keepdims=True) + NORM_EPS)
    return (x32 * inv).astype(x.dtype) * g

def causal_dwconv(x, w, b):
    k = w.shape[0]
    t = x.shape[1]
    xp = jnp.pad(x, ((0, 0), (k - 1, 0), (0, 0)))
    out = b
    for j in range(k):
        out = out + xp[:, j:j + t] * w[j]
    return out

def masked_softmax(s, mask):
    s = jnp.where(mask, s.astype(jnp.float32), -jnp.inf)
    m = jnp.max(s, axis=-1, keepdims=True)
    m = jnp.where(jnp.isfinite(m), m, 0.0)
    p = jnp.exp(s - m)
    return p / jnp.maximum(jnp.sum(p, axis=-1, keepdims=True), 1e-30)

def _split_points():
    sizes = (NSA_WIDTH,) + (KV_WIDTH,) * 6 + (3 * NSA_HEADS, LRU_WIDTH, LRU_WIDTH, D_MODEL, D_MODEL)
    return [int(v) for v in np.cumsum(sizes)[:-1]]

def compress_blocks(kv, pos, w1, w2):
    t = kv.shape[1]
    n_cmp = (t - CMP_LEN) // CMP_STRIDE + 1
    idx = jnp.arange(n_cmp)[:, None] * CMP_STRIDE + jnp.arange(CMP_LEN)[None, :]
    blocks = kv[:, idx] + pos[None, None, :, None, :]
    hid = jax.nn.gelu(jnp.einsum('bnlgd,lde->bnge', blocks, w1))
    return jnp.einsum('bnge,ef->bngf', hid, w2)

def selected_attention(q, k, v, sel):
    bn, t, g, hg, hd = q.shape
    n_slc = t // SLC_LEN
    n_top = sel.shape[-1]
    nc = t // SLC_Q_BLOCK
    kb = k.reshape(bn, n_slc, SLC_LEN, g, hd).transpose(0, 3, 1, 2, 4)
    vb = v.reshape(bn, n_slc, SLC_LEN, g, hd).transpose(0, 3, 1, 2, 4)
    b_ix = jnp.arange(bn)[:, None, None, None]
    g_ix = jnp.arange(g)[None, :, None, None]
    off = jnp.arange(SLC_LEN)
    m_tok = n_top * SLC_LEN

    def chunk(args):
        q_c, sel_c, start = args
        k_g = kb[b_ix, g_ix, sel_c].reshape(bn, g, SLC_Q_BLOCK, m_tok, hd)
        v_g = vb[b_ix, g_ix, sel_c].reshape(bn, g, SLC_Q_BLOCK, m_tok, hd)
        key_pos = (sel_c[..., None] * SLC_LEN + off).reshape(bn, g, SLC_Q_BLOCK, m_tok)
        q_pos = start + jnp.arange(SLC_Q_BLOCK)
        mask = key_pos <= q_pos[None, None, :, None]
        s = jnp.einsum('bqghd,bgqmd->bghqm', q_c, k_g)
        p = masked_softmax(s, mask[:, :, None])
        return jnp.einsum('bghqm,bgqmd->bqghd', p.astype(v_g.dtype), v_g)

    q_chunks = jnp.moveaxis(q.reshape(bn, nc, SLC_Q_BLOCK, g, hg, hd), 1, 0)
    sel_chunks = jnp.moveaxis(sel.reshape(bn, g, nc, SLC_Q_BLOCK, n_top), 2, 0)
    starts = jnp.arange(nc) * SLC_Q_BLOCK
    out = lax.map(chunk, (q_chunks, sel_chunks, starts))
    return jnp.moveaxis(out, 0, 1).reshape(bn, t, g, hg, hd)

def window_attention(q, k, v):
    bn, t, g, hg, hd = q.shape
    nb = t // WIN_Q_BLOCK
    n_prev = WINDOW // WIN_Q_BLOCK

    def band(z):
        zp = jnp.pad(z, ((0, 0), (WINDOW, 0), (0, 0), (0, 0)))
        zb = zp.reshape(bn, nb + n_prev, WIN_Q_BLOCK, g, hd)
        return jnp.concatenate([zb[:, j:j + nb] for j in range(n_prev + 1)], axis=2)

    kb, vb = band(k), band(v)
    qb = q.reshape(bn, nb, WIN_Q_BLOCK, g, hg, hd)
    q_pos = jnp.arange(t).reshape(nb, WIN_Q_BLOCK)
    k_pos = q_pos[:, :1] - WINDOW + jnp.arange((n_prev + 1) * WIN_Q_BLOCK)[None, :]
    diff = q_pos[:, :, None] - k_pos[:, None, :]
    mask = (diff >= 0) & (diff < WINDOW) & (k_pos[:, None, :] >= 0)
    s = jnp.einsum('bnqghd,bnmgd->bnghqm', qb, kb)
    p = masked_softmax(s, mask[None, :, None, None])
    o = jnp.einsum('bnghqm,bnmgd->bnqghd', p.astype(vb.dtype), vb)
    return o.reshape(bn, t, g, hg, hd)

def nsa_attention(q, kc, vc, ks, vs, kw, vw, gates, pos_k, w1_k, w2_k, pos_v, w1_v, w2_v):
    bn, t, _ = q.shape
    g, hg, hd = NSA_KV_GROUPS, HEADS_PER_GROUP, HEAD_DIM
    q = q.reshape(bn, t, g, hg, hd) * (hd ** -0.5)
    kc, vc = kc.reshape(bn, t, g, hd), vc.reshape(bn, t, g, hd)
    ks, vs = ks.reshape(bn, t, g, hd), vs.reshape(bn, t, g, hd)
    kw, vw = kw.reshape(bn, t, g, hd), vw.reshape(bn, t, g, hd)
    t_pos = jnp.arange(t)

    k_cmp = compress_blocks(kc, pos_k, w1_k, w2_k)
    v_cmp = compress_blocks(vc, pos_v, w1_v, w2_v)
    n_cmp = k_cmp.shape[1]
    cmp_start = jnp.arange(n_cmp) * CMP_STRIDE
    cmp_mask = (cmp_start + CMP_LEN - 1)[None, :] <= t_pos[:, None]
    s_cmp = jnp.einsum('btghd,bngd->bghtn', q, k_cmp)
    p_cmp = masked_softmax(s_cmp, cmp_mask)
    o_cmp = jnp.einsum('bghtn,bngd->btghd', p_cmp.astype(v_cmp.dtype), v_cmp)

    n_slc = t // SLC_LEN
    slc_start = jnp.arange(n_slc) * SLC_LEN
    overlap = ((cmp_start[:, None] < slc_start[None, :] + SLC_LEN)
               & (cmp_start[:, None] + CMP_LEN > slc_start[None, :])).astype(jnp.float32)
    imp = jnp.einsum('bghtn,nj->bgtj', p_cmp, overlap)
    blk = jnp.arange(n_slc)[None, :]
    cur = (t_pos // SLC_LEN)[:, None]
    valid = blk <= cur
    forced = (blk == 0) | (valid & (blk > cur - SLC_LOCAL))
    score = jnp.where(forced, imp + FORCE_BONUS, jnp.where(valid, imp, -1.0))
    n_top = min(SLC_TOP_N, n_slc)
    _, sel = lax.top_k(score, n_top)
    o_slc = selected_attention(q, ks, vs, sel)

    o_win = window_attention(q, kw, vw)

    gt = jax.nn.sigmoid(gates.reshape(bn, t, g, hg, 3))
    o = gt[..., 0:1] * o_cmp + gt[..., 1:2] * o_slc + gt[..., 2:3] * o_win
    return o.reshape(bn, t, NSA_WIDTH)

def rg_lru(x, w_a, b_a, w_i, b_i, lam):
    bn, t, w = x.shape
    xb = x.reshape(bn, t, LRU_BLOCKS, LRU_BLOCK_DIM)
    r = jax.nn.sigmoid(jnp.einsum('btnd,nde->btne', xb, w_a).reshape(bn, t, w) + b_a)
    i = jax.nn.sigmoid(jnp.einsum('btnd,nde->btne', xb, w_i).reshape(bn, t, w) + b_i)
    log_a = (LRU_C * r.astype(jnp.float32)) * jax.nn.log_sigmoid(lam.astype(jnp.float32))
    a = jnp.exp(log_a)
    b = jnp.sqrt(-jnp.expm1(2.0 * log_a)) * (i * x).astype(jnp.float32)

    def combine(left, right):
        a1, b1 = left
        a2, b2 = right
        return a1 * a2, a2 * b1 + b2

    _, h = lax.associative_scan(combine, (a, b), axis=1)
    return h.astype(x.dtype)

def token_mixer(h, w_in, pos_k, w1_k, w2_k, pos_v, w1_v, w2_v, conv_w, conv_b,
                w_a, b_a, w_i, b_i, lam, proj_a, proj_b, w_out):
    z = h @ w_in
    q, kc, vc, ks, vs, kw, vw, g_nsa, lx, ly, ga, gb = jnp.split(z, _split_points(), axis=-1)
    o_a = nsa_attention(q, kc, vc, ks, vs, kw, vw, g_nsa, pos_k, w1_k, w2_k, pos_v, w1_v, w2_v)
    u = causal_dwconv(lx, conv_w, conv_b)
    o_b = jax.nn.gelu(ly) * rg_lru(u, w_a, b_a, w_i, b_i, lam)
    merged = jax.nn.sigmoid(ga) * (o_a @ proj_a) + jax.nn.sigmoid(gb) * (o_b @ proj_b)
    return merged @ w_out

def conv_glu_ffn(h, w_up, conv_w, conv_b, w_down):
    gate, val = jnp.split(h @ w_up, 2, axis=-1)
    gate = causal_dwconv(gate, conv_w, conv_b)
    return (jax.nn.gelu(gate) * val) @ w_down

def second_inputs(seed: int = 0) -> dict:
    key = jax.random.key(seed)
    ks = iter(jax.random.split(key, 40))

    def nrm(shape, fan_in, scale=1.0):
        return jax.random.normal(next(ks), shape, jnp.float32) * (scale * fan_in ** -0.5)

    def small(shape, s=0.02):
        return jax.random.normal(next(ks), shape, jnp.float32) * s

    x = jax.random.normal(next(ks), (BATCH, SEQ, D_MODEL), jnp.float32)
    c = jax.random.normal(next(ks), (BATCH, D_MODEL), jnp.float32)
    ada_w = nrm((DEPTH, D_MODEL, 6 * D_MODEL), D_MODEL, 0.5)
    ada_b = small((DEPTH, 6 * D_MODEL))
    norm1_g = 1.0 + small((DEPTH, D_MODEL))
    w_in = nrm((DEPTH, D_MODEL, IN_WIDTH), D_MODEL)
    cmp_pos_k = small((DEPTH, CMP_LEN, HEAD_DIM), 0.1)
    cmp_w1_k = nrm((DEPTH, CMP_LEN, HEAD_DIM, HEAD_DIM), CMP_LEN * HEAD_DIM)
    cmp_w2_k = nrm((DEPTH, HEAD_DIM, HEAD_DIM), HEAD_DIM)
    cmp_pos_v = small((DEPTH, CMP_LEN, HEAD_DIM), 0.1)
    cmp_w1_v = nrm((DEPTH, CMP_LEN, HEAD_DIM, HEAD_DIM), CMP_LEN * HEAD_DIM)
    cmp_w2_v = nrm((DEPTH, HEAD_DIM, HEAD_DIM), HEAD_DIM)
    lru_conv_w = nrm((DEPTH, LRU_CONV, LRU_WIDTH), LRU_CONV)
    lru_conv_b = small((DEPTH, LRU_WIDTH))
    lru_wa = nrm((DEPTH, LRU_BLOCKS, LRU_BLOCK_DIM, LRU_BLOCK_DIM), LRU_BLOCK_DIM)
    lru_ba = small((DEPTH, LRU_WIDTH))
    lru_wi = nrm((DEPTH, LRU_BLOCKS, LRU_BLOCK_DIM, LRU_BLOCK_DIM), LRU_BLOCK_DIM)
    lru_bi = small((DEPTH, LRU_WIDTH))
    u = jax.random.uniform(next(ks), (DEPTH, LRU_WIDTH), jnp.float32)
    rad = jnp.sqrt(u * (0.999 ** 2 - 0.9 ** 2) + 0.9 ** 2)
    lru_lambda = jnp.log(rad) - jnp.log1p(-rad)
    proj_a = nrm((DEPTH, NSA_WIDTH, D_MODEL), NSA_WIDTH)
    proj_b = nrm((DEPTH, LRU_WIDTH, D_MODEL), LRU_WIDTH)
    w_out = nrm((DEPTH, D_MODEL, D_MODEL), D_MODEL)
    norm2_g = 1.0 + small((DEPTH, D_MODEL))
    ffn_up = nrm((DEPTH, D_MODEL, 2 * D_FF_2), D_MODEL)
    ffn_conv_w = nrm((DEPTH, FFN_CONV, D_FF_2), FFN_CONV)
    ffn_conv_b = small((DEPTH, D_FF_2))
    ffn_down = nrm((DEPTH, D_FF_2, D_MODEL), D_FF_2)
    final_g = 1.0 + small((D_MODEL,))
    return {"x": x, "c": c, "ada_w": ada_w, "ada_b": ada_b, "norm1_g": norm1_g, "w_in": w_in,
            "cmp_pos_k": cmp_pos_k, "cmp_w1_k": cmp_w1_k, "cmp_w2_k": cmp_w2_k,
            "cmp_pos_v": cmp_pos_v, "cmp_w1_v": cmp_w1_v, "cmp_w2_v": cmp_w2_v,
            "lru_conv_w": lru_conv_w, "lru_conv_b": lru_conv_b, "lru_wa": lru_wa, "lru_ba": lru_ba,
            "lru_wi": lru_wi, "lru_bi": lru_bi, "lru_lambda": lru_lambda,
            "proj_a": proj_a, "proj_b": proj_b, "w_out": w_out, "norm2_g": norm2_g,
            "ffn_up": ffn_up, "ffn_conv_w": ffn_conv_w, "ffn_conv_b": ffn_conv_b, "ffn_down": ffn_down,
            "final_g": final_g}

def second_block(x, c, ada_w, ada_b, norm1_g, w_in, cmp_pos_k, cmp_w1_k, cmp_w2_k, cmp_pos_v, cmp_w1_v,
              cmp_w2_v, lru_conv_w, lru_conv_b, lru_wa, lru_ba, lru_wi, lru_bi, lru_lambda, proj_a, proj_b,
              w_out, norm2_g, ffn_up, ffn_conv_w, ffn_conv_b, ffn_down, final_g):
    c_act = jax.nn.silu(c)
    for l in range(DEPTH):
        mod = (c_act @ ada_w[l] + ada_b[l])[:, None, :]
        sh1, sc1, g1, sh2, sc2, g2 = jnp.split(mod, 6, axis=-1)
        h = rmsnorm(x, norm1_g[l]) * (1.0 + sc1) + sh1
        y = token_mixer(h, w_in[l], cmp_pos_k[l], cmp_w1_k[l], cmp_w2_k[l], cmp_pos_v[l], cmp_w1_v[l],
                        cmp_w2_v[l], lru_conv_w[l], lru_conv_b[l], lru_wa[l], lru_ba[l], lru_wi[l],
                        lru_bi[l], lru_lambda[l], proj_a[l], proj_b[l], w_out[l])
        x = x + g1 * y
        h = rmsnorm(x, norm2_g[l]) * (1.0 + sc2) + sh2
        x = x + g2 * conv_glu_ffn(h, ffn_up[l], ffn_conv_w[l], ffn_conv_b[l], ffn_down[l])
    return rmsnorm(x, final_g)


def setup_inputs(seed=0):
    out = dict(first_inputs(seed))
    for name, value in second_inputs(seed + 1).items():
        if name != "x":
            out[name + "_2"] = value
    return out


def reference(
    x, mem, rel_bias, g_mix, w_in, g_qa, g_ka, g_qb, g_kb, g_mem, w_mem_kv, g_qc, g_kc, w_br_a,
    w_br_b, w_br_c, w_o, g_ffn, w_ffn_in, w_ffn_out, c_2, ada_w_2, ada_b_2, norm1_g_2, w_in_2,
    cmp_pos_k_2, cmp_w1_k_2, cmp_w2_k_2, cmp_pos_v_2, cmp_w1_v_2, cmp_w2_v_2, lru_conv_w_2,
    lru_conv_b_2, lru_wa_2, lru_ba_2, lru_wi_2, lru_bi_2, lru_lambda_2, proj_a_2, proj_b_2,
    w_out_2, norm2_g_2, ffn_up_2, ffn_conv_w_2, ffn_conv_b_2, ffn_down_2, final_g_2,
):
    x = first_block(
        x, mem, rel_bias, g_mix, w_in, g_qa, g_ka, g_qb, g_kb, g_mem, w_mem_kv, g_qc, g_kc,
        w_br_a, w_br_b, w_br_c, w_o, g_ffn, w_ffn_in, w_ffn_out,
    )
    return second_block(
        x, c_2, ada_w_2, ada_b_2, norm1_g_2, w_in_2, cmp_pos_k_2, cmp_w1_k_2, cmp_w2_k_2,
        cmp_pos_v_2, cmp_w1_v_2, cmp_w2_v_2, lru_conv_w_2, lru_conv_b_2, lru_wa_2, lru_ba_2,
        lru_wi_2, lru_bi_2, lru_lambda_2, proj_a_2, proj_b_2, w_out_2, norm2_g_2, ffn_up_2,
        ffn_conv_w_2, ffn_conv_b_2, ffn_down_2, final_g_2,
    )


_drawn_inputs = setup_inputs


def setup_inputs(seed=0):
    import zlib

    import numpy as np

    out = dict(_drawn_inputs(seed))
    spreads = {}
    factors = {'g_mix': 6.054,
     'g_qa': 8.0,
     'g_ka': 8.0,
     'g_qb': 8.0,
     'g_kb': 8.0,
     'g_mem': 8.0,
     'g_qc': 8.0,
     'g_kc': 8.0,
     'ada_b_2': 3.202,
     'norm1_g_2': 8.0,
     'cmp_pos_k_2': 8.0,
     'cmp_w1_k_2': 5.49,
     'cmp_w2_k_2': 5.489,
     'cmp_pos_v_2': 45.026,
     'lru_conv_b_2': 8.0,
     'lru_wa_2': 3.602,
     'lru_ba_2': 52.824,
     'lru_bi_2': 25.143,
     'norm2_g_2': 8.0,
     'ffn_conv_b_2': 27.75,
     'final_g_2': 7.397,
     'g_ffn': 2.787}
    for name, (base, spread) in spreads.items():
        noise = np.random.default_rng([zlib.crc32(name.encode()), seed]).standard_normal(out[name].shape)
        drawn = base * np.exp(spread * noise) if base else spread * noise
        out[name] = jnp.asarray(drawn.astype(out[name].dtype))
    for name, factor in factors.items():
        out[name] = (out[name] * factor).astype(out[name].dtype)
    return out
```

```python
from contextlib import ExitStack

import numpy as np

import concourse.bass as bass
from concourse import mybir

F32 = mybir.dt.float32
F32R = mybir.dt.float32r
ALU = mybir.AluOpType
ACT = mybir.ActivationFunctionType
AX = mybir.AxisListType

P = 128
S = 256
NT = S // P
D = 2048
KD = D // P
NW = 512
EPS = 1e-6
HD = 128
SCALE = float(HD) ** -0.5
NEG = -1e30

FF1 = 5632
KF1 = FF1 // P
FF2 = 6144
KF2 = FF2 // P
A_GROUPS, A_PER = 3, 2
ADA_CHUNKS = 6 * D // NW

VECTORS = [("c_2", 16), ("g_mem", 16), ("g_mix", 16), ("g_ffn", 16), ("norm1_g_2", 16), ("norm2_g_2", 16),
           ("g_qa", 1), ("g_ka", 1), ("g_qc", 1), ("g_kc", 1),
           ("lru_lambda_2", 16), ("lru_ba_2", 16), ("lru_bi_2", 16), ("lru_conv_b_2", 16), ("lru_conv_w_2", 64),
           ("ffn_conv_w_2", 144), ("ffn_conv_b_2", 48), ("cmp_pos_k_2", 32), ("cmp_pos_v_2", 32)]
COL = {}
_at = 0
for _n, _k in VECTORS:
    COL[_n] = _at
    _at += _k
NCOL = _at


READY = {"mem": 4, "qkv": 8, "gates": 8, "branch": 11, "w_o": 15, "ffn_in": 19, "mix2": 23,
         "proj_a": 27, "proj_b": 31, "w_out": 35, "ffn_up": 39}


TURN = {0: 0, 1: 1, "m1": 2, 2: 3, 3: 4, "m2": 5, 4: 6}


class At:

    def __init__(self, base, per=0, i=0):
        self.base, self.per, self.i = base, per, i

    def val(self, scale=1, offset=0):
        const = scale * self.base + offset
        step = scale * self.per
        if isinstance(self.i, int):
            return const + step * self.i
        if step == 0:
            return const
        return self.i * step + const


K16 = [(0, 4), (4, 4), (8, 4), (12, 4)]
BRANCH = [[(0, 2)], [(2, 3), (5, 3)], [(8, 4)]]


def body_of(chunks, ada):
    out, q = [], 0
    for j, tiles in enumerate(chunks):
        for t, (k0, nk) in enumerate(tiles):
            out.append(("g", j, t, k0, nk))
            if ada and t % 2 == 0:
                out.append(("a", q, 0, 0, 0))
                q += 1
    return out


class Phase:
    def __init__(self, name, iters, chunks, ada=False):
        self.name, self.iters, self.chunks, self.ada = name, iters, chunks, ada
        self.body = body_of(chunks, ada)


def plan():
    two = [K16, K16]
    phases = [Phase("mem", 1, two, True), Phase("qkv", 4, two, True), Phase("gates", 6, two, True),
              Phase("branch", 4, BRANCH), Phase("w_o", 2, two, True), Phase("ffn_in", 11, two, True),
              Phase("ffn_out", KF1 // 4, [[(0, 1)] * 4]),
              Phase("q2", 2, two), Phase("kv2", 3, two), Phase("g48", 1, [K16]),
              Phase("lru_in", 4, two), Phase("gates2", 4, two), Phase("proj_a", 2, two), Phase("proj_b", 2, two),
              Phase("w_out", 2, two), Phase("ffn_up", 12, two), Phase("ffn_down", KF2 // 4, [[(0, 1)] * 4])]
    t = h = c = a = 0
    for p in phases:
        p.T0, p.H0, p.C0, p.A0 = t, h, c, a
        p.tpi = len(p.body)
        p.hpi = 2 * sum(b[0] == "g" for b in p.body)
        p.cpi = 0 if p.name in ("ffn_out", "ffn_down") else len(p.chunks)
        t += p.tpi * p.iters
        h += p.hpi * p.iters
        c += p.cpi * p.iters
        a += p.iters if p.ada else 0
        assert p.T0 % 4 == 0 and p.tpi % 4 == 0, p.name
    assert a == ADA_CHUNKS
    return {p.name: p for p in phases}


def two_block_program(nc, t, out, stop=99):
    PH = plan()
    ctx = ExitStack()
    with ctx:
        def sb(name, shape, dt):
            return ctx.enter_context(nc.sbuf_tensor(name, shape, dt))

        sems = {}

        def sem(name):
            if name not in sems:
                sems[name] = ctx.enter_context(nc.semaphore(name))
            return sems[name]

        raw = sb("raw", [P, 4, 4, NW], F32)
        WH = sb("WH", [P, 4, 2, NW], F32R)
        WL = sb("WL", [P, 4, 2, NW], F32R)
        XH = sb("XH", [P, KD, S], F32R)
        XL = sb("XL", [P, KD, S], F32R)
        X = sb("X", [P, NT, D], F32)
        KB = 256
        arena = sb("arena", [P, 92 * KB], F32)
        cols = sb("cols", [P, NCOL], F32)
        ident = sb("ident", [P, P], F32)
        small = sb("small", [P, 290], F32)
        acc = [ctx.enter_context(nc.psum_tensor(f"acc{i}", [P, 2, NW], F32)) for i in range(4)]

        def at(kb, n):
            return arena[:, int(kb * KB):int(kb * KB) + n]

        XF = at(0, KD * S).rearrange("p (k s) -> p k s", k=KD)
        XN = at(16, NT * D).rearrange("p (t n) -> p t n", t=NT)
        Z = at(16, NT * 4096).rearrange("p (t n) -> p t n", t=NT)
        QK = at(48, 28 * S).rearrange("p (h s) -> p h s", h=28)
        VC = at(76, NT * NW).rearrange("p (t n) -> p t n", t=NT)
        BI = at(80, 12 * S).rearrange("p (j t g s) -> p j t g s", j=2, t=2, g=3)
        SG = at(16, NT * 6144).rearrange("p (t n) -> p t n", t=NT)
        M = at(64, NT * D).rearrange("p (t n) -> p t n", t=NT)
        AT = at(16, 48 * S).rearrange("p (k s) -> p k s", k=48)
        GT = at(64, 2 * 4 * S).rearrange("p (b m s) -> p b m s", b=2, m=4)
        CV = at(72, 2 * 4 * S).rearrange("p (b m s) -> p b m s", b=2, m=4)

        def ada_place(name):
            kb = 0 if name in ("mem", "qkv") else 80
            return at(kb, 2 * NW).rearrange("p (b n) -> p b n", b=2), at(kb + 4, NW), at(kb + 6, NW)

        def col(name, n=None, first=0):
            n = dict(VECTORS)[name] if n is None else n
            return cols[:, COL[name] + first:COL[name] + first + n]

        def bc(ap, shape):
            return ap.unsqueeze(2).broadcast_to(shape)

        zero1 = small[:, 0:1]
        one1 = small[:, 1:2]
        cact = small[:, 2:18]
        stat = small[:, 18:34]
        gq = small[:, 34:62]
        smx = small[:, 62:94]
        mod = small[:, 94:158]
        lamc = small[:, 158:190]
        G48 = small[:, 190:286].rearrange("p (t n) -> p t n", t=NT)

        XT = lambda kb, n: at(kb, n * S).rearrange("p (k s) -> p k s", k=n)
        Q2, LX, LY = XT(16, 16), XT(32, 16), XT(48, 16)
        KC2, VC2, KS2, KW2 = XT(64, 4), XT(68, 4), XT(72, 4), XT(76, 4)
        VS2 = at(80, NT * NW).rearrange("p (t n) -> p t n", t=NT)
        VW2 = at(84, NT * NW).rearrange("p (t n) -> p t n", t=NT)
        KCMP = at(88, 64)
        VCMP = at(89, 512)
        SG2 = at(48, NT * 4096).rearrange("p (t n) -> p t n", t=NT)

        smx1 = mod
        amax1, asum1 = smx[:, 0:4], smx[:, 4:8]
        P1 = X[:, :, :].rearrange("p t n -> p (t n)")[:, 0:3072].rearrange("p (b t n) -> p b t n", b=2, t=2)
        PT1 = Z[:, :, 0:1536].rearrange("p b (k s) -> p b k s", k=6)
        RT, IT, TT, UT, AA = XT(0, 4), XT(4, 4), XT(8, 4), XT(12, 4), XT(88, 4)
        SEG = [(0, S), (S, 2 * S), (2 * S, 2 * S + 15)]
        P2 = at(0, 4 * 527).rearrange("p (b t n) -> p b t n", b=2, t=2)
        PC2 = at(9, 2 * S).rearrange("p (b s) -> p b s", b=2)
        PT2 = X[:, 1, :].rearrange("p (b k s) -> p b k s", b=2, k=4)

        mod_dram = nc.dram_tensor("mod_scratch", (6 * D,), F32, kind="Internal").ap()
        bias_dram = nc.dram_tensor("bias_scratch", (6, P, 2 * S), F32, kind="Internal").ap()
        x_dram = nc.dram_tensor("x_scratch", (P, NT * D), F32, kind="Internal").ap()

        landed = [sem(f"tile_landed{i}") for i in range(4)]
        w_hi, w_lo = sem("weights_rounded"), sem("weights_rest")
        mm_half = sem("half_multiplied")
        acc_used = [sem("acc_used0"), sem("acc_used1")]
        ada_mac, ada_red, ada_rowed = sem("ada_multiplied"), sem("ada_reduced"), sem("ada_row_ready")
        ada_b_in, ada_stored = sem("ada_bias_landed"), sem("ada_row_stored")
        xh_ready, xl_ready = sem("acts_rounded"), sem("acts_rest")

        def run(eng, ph, body):
            body(0, True)
            if ph.iters > 1:
                with eng.Fori(1, ph.iters) as i:
                    body(i, False)

        def c_end(name, p):
            ph = PH[name]
            return (ph.C0 + ph.cpi * ph.iters + 1 - p) // 2

        def last_half(ph, n, i):
            g = sum(b[0] == "g" for b in ph.body[:n])
            return At(ph.H0 + 2 * g + 1, ph.hpi, i)

        def chunk_done(ph, j, i):
            n = max(n for n, b in enumerate(ph.body) if b[0] == "g" and b[1] == j)
            return last_half(ph, n, i).val(1, 1)

        def pair_of(ph, j, i):
            c = ph.C0 + j
            if ph.cpi == 3:
                c += 3 * i
                return c % 2, At(c // 2)
            return c % 2, At(c // 2, 1, i)

        block = ctx.enter_context(nc.Block())

        @block.sync
        def _(sp):
            tail = [None]

            def reuse(ph, n, i, first):
                if n >= 4:
                    m, before, at_i = n - 4, ph, i
                elif not first:
                    m, before, at_i = n - 4 + ph.tpi, ph, i - 1
                elif tail[0]:
                    before = tail[0]
                    m, at_i = n - 4 + before.tpi, before.iters - 1
                else:
                    return
                if before.body[m][0] == "a":
                    sp.wait_ge(ada_mac, At(before.A0, 1, at_i).val(16, 4 * before.body[m][1] + 4))
                else:
                    sp.wait_ge(w_lo, last_half(before, m, at_i).val(1, 1))

            def load(T, slot, dst, src):
                sp.dma_start(dst, src).then_inc(landed[slot], 16)

            def stream(ph, source):
                def body(i, first):
                    for n, b in enumerate(ph.body):
                        T = At(ph.T0 + n, ph.tpi, i)
                        slot = n % 4
                        reuse(ph, n, i, first)
                        if b[0] == "a":
                            column = At(ph.A0, 1, i).val(NW)
                            src = t["ada_w_2"].rearrange("(k p) n -> p k n", p=P)[
                                :, 4 * b[1]:4 * b[1] + 4, bass.ds(column, NW)]
                            load(T, slot, raw[:, slot], src)
                        else:
                            source(i, T, slot, *b[1:])
                if ph.cpi == 3:
                    for i in range(ph.iters):
                        body(i, i == 0)
                else:
                    run(sp, ph, body)
                tail[0] = ph

            def chunked(w, column):
                wv = w.rearrange("(k p) n -> p k n", p=P)

                def source(i, T, slot, j, tt, k0, nk):
                    load(T, slot, raw[:, slot, 0:nk], wv[:, k0:k0 + nk, bass.ds(column(i, j), NW)])
                return source

            def rows(w, kf):
                def source(i, T, slot, j, tt, k0, nk):
                    start = At(tt, 4, i).val(P)
                    load(T, slot, raw[:, slot].rearrange("p a n -> p (a n)"), w[bass.ds(start, P), :])
                return source

            def lin(base, per_i, per_j):
                return lambda i, j: i * per_i + (base + j * per_j)

            stream(PH["mem"], chunked(t["w_mem_kv"], lin(0, 2 * NW, NW)))
            stream(PH["qkv"], chunked(t["w_in"], lin(0, 2 * NW, NW)))
            stream(PH["gates"], chunked(t["w_in"], lin(4096, 2 * NW, NW)))
            wa = t["w_br_a"].rearrange("(k p) n -> p k n", p=P)
            wb = t["w_br_b"].rearrange("(k p) n -> p k n", p=P)
            wc = t["w_br_c"].rearrange("(k p) n -> p k n", p=P)

            def branch(i, T, slot, j, tt, k0, nk):
                w, base = ((wa, 0), (wb, 2), (wc, 8))[j]
                load(T, slot, raw[:, slot, 0:nk], w[:, k0 - base:k0 - base + nk, i * NW:(i + 1) * NW])
            stream(PH["branch"], branch)
            stream(PH["w_o"], chunked(t["w_o"], lin(0, 2 * NW, NW)))
            stream(PH["ffn_in"], chunked(t["w_ffn_in"], lin(0, NW, FF1)))
            stream(PH["ffn_out"], rows(t["w_ffn_out"], KF1))
            w2 = t["w_in_2"]
            stream(PH["q2"], chunked(w2, lin(0, 2 * NW, NW)))
            stream(PH["kv2"], chunked(w2, lin(2048, 2 * NW, NW)))
            w2v = w2.rearrange("(k p) n -> p k n", p=P)

            def g48(i, T, slot, j, tt, k0, nk):
                load(T, slot, raw[:, slot, :, 0:48], w2v[:, k0:k0 + nk, 5120:5168])
            stream(PH["g48"], g48)
            stream(PH["lru_in"], chunked(w2, lin(5168, 2 * NW, NW)))
            stream(PH["gates2"], chunked(w2, lin(9264, 2 * NW, NW)))
            stream(PH["proj_a"], chunked(t["proj_a_2"], lin(0, 2 * NW, NW)))
            stream(PH["proj_b"], chunked(t["proj_b_2"], lin(0, 2 * NW, NW)))
            stream(PH["w_out"], chunked(t["w_out_2"], lin(0, 2 * NW, NW)))
            stream(PH["ffn_up"], chunked(t["ffn_up_2"], lin(0, NW, FF2)))
            stream(PH["ffn_down"], rows(t["ffn_down_2"], KF2))

        @block.gpsimd
        def _(gp):
            gp.dma_start(cols[:, :], t["vectors"]).then_inc(sem("cols_in"), 16)
            gp.dma_start(ident[:, :], t["identity"]).then_inc(sem("ident_in"), 16)
            gp.dma_start(X[:, :, :], t["mem"].rearrange("(t p) n -> p t n", p=P)).then_inc(sem("mem_in"), 16)
            gp.dma_start(at(32, 6)[0:32], t["rel_bias"]).then_inc(sem("bias_in"), 16)
            gp.dma_start(at(33, 512)[0:32], t["one_hot"]).then_inc(sem("bias_in"), 16)
            gp.dma_start(at(36, 6 * S), t["masks_a"]).then_inc(sem("bias_in"), 16)
            gp.memset(zero1, 0.0).then_inc(sem("small_set"), 1)
            gp.memset(one1, 1.0).then_inc(sem("small_set"), 1)
            gp.memset(gq, 1.0).then_inc(sem("small_set"), 1)
            for h in range(6):
                gp.wait_ge(sem("bias_row"), h + 1)
                gp.dma_start(bias_dram[h], at(42 + 2 * (h % 2), 512)).then_inc(sem("bias_out"), 16)
                gp.wait_ge(sem("bias_out"), 16 * (h + 1))
            for h in range(6):
                g, j = h // 2, h % 2
                for tt in range(NT):
                    src = bass.AP(tensor=bias_dram.tensor, offset=h * P * 512 + 255 - tt * P, ap=[[511, P], [1, S]])
                    gp.dma_start(BI[:, j, tt, g, :], src).then_inc(sem("bias_back"), 16)
            gp.wait_ge(sem("norm_rows"), 1 * NT)
            gp.dma_start(X[:, :, :], t["x"].rearrange("(t p) n -> p t n", p=P)).then_inc(sem("x_in"), 16)
            if stop < 3:
                return
            def ada_rows(name):
                ph = PH[name]
                _, ada_row, ada_brow = ada_place(name)

                if ph.A0 == 0 or name == "qkv":
                    gp.wait_ge(xl_ready, READY[name])
                for a in range(ph.A0, ph.A0 + ph.iters):
                    gp.dma_start(ada_brow[0:1], t["ada_b_2"][:, NW * a:NW * a + NW]).then_inc(ada_b_in, 16)
                    gp.wait_ge(ada_rowed, a + 1)
                    gp.dma_start(mod_dram[NW * a:NW * a + NW].unsqueeze(0), ada_row[0:1]).then_inc(ada_stored, 16)
                    gp.wait_ge(ada_stored, 16 * a + 16)
            ada_rows("mem")
            gp.wait_ge(sem("norm_rows"), 2 * NT)
            gp.dma_start(X[:, 0, 0:256], t["rope"]).then_inc(sem("rope_in"), 16)
            gp.dma_start(X[:, 0, 256:384], t["g_qb"].partition_broadcast(P)).then_inc(sem("rope_in"), 16)
            gp.dma_start(X[:, 0, 384:512], t["g_kb"].partition_broadcast(P)).then_inc(sem("rope_in"), 16)
            ada_rows("qkv")
            if stop < 6:
                return
            gp.wait_ge(sem("attn1_out"), 12)
            ada_rows("gates")
            gp.dma_start(X[:, :, :], t["x"].rearrange("(t p) n -> p t n", p=P)).then_inc(sem("x_again"), 16)
            ada_rows("w_o")
            ada_rows("ffn_in")
            for n, part in enumerate((1, 0, 4, 3)):
                gp.dma_start(at(88, P)[16 * n:16 * n + 16], mod_dram[part * D:(part + 1) * D].rearrange(
                    "(k p) -> k p", p=P)).then_inc(sem("mod_in"), 16)
            if stop < 10:
                return
            gp.wait_ge(sem("norm_rows"), 4 * NT)
            gp.dma_start(x_dram, X[:, :, :].rearrange("p t n -> p (t n)")).then_inc(sem("x_away"), 16)
            gp.wait_ge(sem("x_away"), 16)
            gp.dma_start(X[:, 0, :].rearrange("p (n e) -> p n e", n=16),
                         t["lru_wa_2"].rearrange("n d e -> d n e")).then_inc(sem("lru_w_in"), 16)
            gp.dma_start(X[:, 1, :].rearrange("p (n e) -> p n e", n=16),
                         t["lru_wi_2"].rearrange("n d e -> d n e")).then_inc(sem("lru_w_in"), 16)
            for n, (w1, w2) in enumerate((("cmp_w1_k_2", "cmp_w2_k_2"), ("cmp_w1_v_2", "cmp_w2_v_2"))):
                if n == 0:
                    gp.wait_ge(sem("lru_out"), 4)
                else:
                    gp.wait_ge(sem("cmp_hid"), 1)
                gp.dma_start(at(0, 4096).rearrange("p (l e) -> p l e", l=32),
                             t[w1].rearrange("l d e -> d l e")).then_inc(sem("cmp_in"), 16)
                gp.dma_start(X[:, 1, 128 * n:128 * n + 128], t[w2]).then_inc(sem("cmp2_in"), 16)
            gp.wait_ge(sem("cmp_hid"), 2)
            gp.dma_start(X[:, 0, 0:2 * 527], t["masks_2"]).then_inc(sem("mask2_in"), 16)
            if stop < 14:
                return
            gp.wait_ge(sem("attn2_out"), 16)
            gp.dma_start(X[:, :, :].rearrange("p t n -> p (t n)"), x_dram).then_inc(sem("x_back"), 16)
            gp.wait_ge(xl_ready, READY["w_out"])
            gp.dma_start(at(0, D), mod_dram[2 * D:3 * D].partition_broadcast(P)).then_inc(sem("g1_in"), 16)
            gp.wait_ge(xl_ready, READY["ffn_up"])
            gp.dma_start(at(0, D), mod_dram[5 * D:6 * D].partition_broadcast(P)).then_inc(sem("g2_in"), 16)
            gp.dma_start(at(8, D), t["final_g_2"].partition_broadcast(P)).then_inc(sem("final_g_in"), 16)
            for tt in range(NT):
                gp.wait_ge(sem("final"), tt + 1)
                gp.dma_start(out[tt * P:(tt + 1) * P, :], XN[:, tt, :]).then_inc(sem("out_stored"), 16)
            gp.wait_ge(sem("out_stored"), 16 * NT)

        def halves(nk):
            a = (nk + 1) // 2
            return ((0, a), (a, nk))

        def half_at(ph, g, h, i):
            return At(ph.H0 + 2 * g + h, ph.hpi, i)

        def epilogue_of(ph, j, i, first):
            if j > 0:
                return (i, j - 1)
            return None if first else (i - 1, len(ph.chunks) - 1)

        def products(eng, ph, tile, epilogue, ada=None, straight=False, iters=None):
            def body(i, first):
                g = 0
                for n, b in enumerate(ph.body):
                    T = At(ph.T0 + n, ph.tpi, i)
                    if b[0] == "a":
                        if ada:
                            ada("tile", i, (T, n % 4, b[1]))
                        continue
                    tile(i, T, n % 4, g, *b[1:])
                    g += 1
                    if ada and not first and g == 1:
                        ada("row", i - 1, None)
                    last = epilogue_of(ph, b[1], i, first) if b[2] == 0 else None
                    if last and epilogue:
                        epilogue(*last, *pair_of(ph, last[1], last[0]))
            if straight:
                for i in range(ph.iters):
                    body(i, i == 0)
            else:
                run(eng, ph, body)
            end = (ph.iters - 1, len(ph.chunks) - 1)
            if epilogue:
                epilogue(*end, *pair_of(ph, end[1], end[0]))
            if ada:
                ada("row", ph.iters - 1, None)

        @block.scalar
        def _(act):
            def act_copy(out, in_, func=ACT.Copy, **kw):
                return nc.scalar.activation(out, in_, func, **kw)

            def tile(width=NW):
                def one(i, T, slot, g, j, tt, k0, nk):
                    ph = cur[0]
                    act.wait_ge(landed[slot], T.val(4, 16 - 4 * slot))
                    for h, (a, b) in enumerate(halves(nk)):
                        H = half_at(ph, g, h, i)
                        if not (isinstance(i, int) and H.val() < 4):
                            act.wait_ge(mm_half, H.val(1, -3))
                        act_copy(WH[:, (2 * slot_g(ph, g) + h) % 4, 0:b - a, 0:width],
                                 raw[:, slot, a:b, 0:width]).then_inc(w_hi, 1)
                return one
            cur = [None]

            def slot_g(ph, g):
                return (ph.H0 // 2 + g) % 2

            def phase(name, epilogue, straight=False, width=NW):
                cur[0] = PH[name]
                products(act, PH[name], tile(width), epilogue, straight=straight)

            def norm_part(n, src, wait):
                wait()
                for tt in range(NT):
                    act_copy(at(8 * tt, D), src[:, tt, :], ACT.Square,
                             accum_out=stat[:, tt:tt + 1]).then_inc(sem("norm_squares"), 1)
                act.wait_ge(sem("norm_mean"), n + 1)
                act_copy(stat[:, 4:6], stat[:, 2:4], ACT.Sqrt).then_inc(sem("norm_root"), 1)

            def round_acts(name, done, base):
                act.wait_ge(mm_half, PH[name].H0)
                for g in range(4):
                    act.wait_ge(done, base + g + 1)
                    act_copy(XH[:, 4 * g:4 * g + 4], XF[:, 4 * g:4 * g + 4]).then_inc(xh_ready, 1)

            act.wait_ge(sem("cols_in"), 16)
            act_copy(cact, col("c_2"), ACT.Silu).then_inc(sem("c_ready"), 1)
            for h in range(6):
                act.wait_ge(sem("bias_mm"), h + 1)
                if h >= 2:
                    act.wait_ge(sem("bias_out"), 16 * (h - 1))
                act_copy(at(42 + 2 * (h % 2), 512), acc[2 + h % 2][:, 0, :]).then_inc(sem("bias_row"), 1)
            norm_part(0, X, lambda: act.wait_ge(sem("mem_in"), 16))
            for g in range(4):
                act.wait_ge(sem("acts"), g + 1)
                act_copy(XH[:, 4 * g:4 * g + 4], XF[:, 4 * g:4 * g + 4]).then_inc(xh_ready, 1)
            if stop < 2:
                return

            def to_tokens(dst):
                def epilogue(i, j, p, used):
                    act.wait_ge(mm_half, chunk_done(cur[0], j, i))
                    act_copy(dst(i, j, 0), acc[p][:, 0, :]).then_inc(acc_used[p], 1)
                return epilogue
            if stop < 3:
                return
            phase("mem", to_tokens(lambda i, j, tt: (Z[:, tt, 0:NW], VC[:, tt, :])[j]))

            def heads_part(n):
                act.wait_ge(sem(f"heads{n}_mean"), 1)
                act_copy(smx[:, 0:32], smx[:, 0:32], ACT.Sqrt).then_inc(sem(f"heads{n}_root"), 1)

            if stop < 4:
                return
            act.wait_ge(sem("kc_mean"), 1)
            act_copy(stat[:, 8:16], stat[:, 8:16], ACT.Sqrt).then_inc(sem("kc_root"), 1)
            act.wait_ge(ada_stored, 16 * 1)
            norm_part(1, X, lambda: act.wait_ge(sem("x_in"), 16))
            round_acts("qkv", sem("acts"), 4 * TURN[1])
            if stop < 5:
                return
            phase("qkv", to_tokens(lambda i, j, tt: Z[:, tt, bass.ds(i * (2 * NW) + j * NW, NW)]))
            act.wait_ge(sem("heads_mean"), 1)
            act_copy(smx1[:, 0:48], smx1[:, 0:48], ACT.Sqrt).then_inc(sem("heads_root"), 1)
            if stop < 6:
                return
            for job in range(12):
                segs = 3 if job < 2 else 1
                n = 256 * segs
                for tt in range(NT):
                    u = 2 * job + tt
                    act.wait_ge(sem("attn1_max"), u + 1)
                    src = P1[:, job % 2, tt, 0:n] if job < 2 else acc[tt][:, 0, 0:256]
                    act_copy(P1[:, job % 2, tt, 0:n], src, ACT.Exp, bias=amax1[:, 2 * (job % 2) + tt:2 * (job % 2) + tt + 1],
                             accum_out=asum1[:, 2 * (job % 2) + tt:2 * (job % 2) + tt + 1]).then_inc(sem("attn1_exp"), 1)
                act.wait_ge(sem("attn1_turned"), job + 1)
                if job >= 2:
                    act.wait_ge(sem("attn1_mm"), job - 1)
                nb = 2 * segs
                act_copy(PT1[:, job % 2, 0:min(nb, 4), :], acc[2][:, :, :].rearrange("p a (b s) -> p (a b) s", b=2)[:, 0:min(nb, 4)]).then_inc(sem("attn1_pt"), 1)
                if nb > 4:
                    act_copy(PT1[:, job % 2, 4:6, :], acc[3][:, 0, :].rearrange("p (b s) -> p b s", b=2)).then_inc(sem("attn1_pt"), 1)
            act.wait_ge(sem("attn1_out"), 12)
            if stop < 7:
                return

            def gates(dst, width):
                def epilogue(i, j, p, used):
                    act.wait_ge(mm_half, chunk_done(cur[0], j, i))
                    for tt in range(NT):
                        act_copy(dst[:, tt, bass.ds(i * (2 * NW) + j * NW, NW)], acc[p][:, tt, :],
                                 ACT.Sigmoid).then_inc(acc_used[p], 1)
                return epilogue
            phase("gates", gates(SG, 6144))
            if stop < 8:
                return
            act.wait_ge(mm_half, PH["branch"].H0)
            for g in range(3):
                act_copy(XH[:, 4 * g:4 * g + 4], XF[:, 4 * g:4 * g + 4]).then_inc(xh_ready, 1)
            phase("branch", None, straight=True)
            act.wait_ge(mm_half, PH["w_o"].H0)
            round_acts("w_o", sem("acts"), 4 * TURN["m1"])
            phase("w_o", None)
            if stop < 9:
                return
            act.wait_ge(ada_stored, 16 * (PH["w_o"].A0 + 2))
            norm_part(2, X, lambda: [act.wait_ge(acc_used[p], 2 * c_end("w_o", p)) for p in range(2)])
            round_acts("ffn_in", sem("acts"), 4 * TURN[2])

            def used_before(ph, i):
                return pair_of(ph, 1, i)[1]

            def silu_gate(func, src_of, guard):
                def epilogue(i, j, p, used):
                    if j == 1:
                        return
                    act.wait_ge(mm_half, chunk_done(cur[0], j, i))
                    act.wait_ge(acc_used[1 - p], used_before(cur[0], i).val(2, 0))
                    act_copy(GT[:, 0], acc[p][:, :, :].rearrange("p a (b s) -> p (a b) s", b=2), func).then_inc(acc_used[p], 2)
                return epilogue
            phase("ffn_in", silu_gate(ACT.Silu, None, None))

            def k_outer(name, base):
                ph = PH[name]

                def body(i, first):
                    for j in range(4):
                        T = At(ph.T0 + j, 4, i)
                        H = At(ph.H0 + 2 * j, 8, i)
                        act.wait_ge(mm_half, ph.H0 if first else H.val(1, -6))
                        act_copy(XH[:, j], AT[:, bass.ds(i * 4 + j, 1), :] if not isinstance(i, int) else AT[:, 4 * i + j:4 * i + j + 1, :]).then_inc(sem("hidden_rounded"), 1)
                        act.wait_ge(landed[j], T.val(4, 16 - 4 * j))
                        for h in range(2):
                            act.wait_ge(mm_half, H.val(1, h - 3))
                            act_copy(WH[:, (ph.H0 + 2 * j + h) % 4], raw[:, j, 2 * h:2 * h + 2]).then_inc(w_hi, 1)
                run(act, ph, body)
            if stop < 10:
                return
            for p in range(2):
                act.wait_ge(acc_used[p], 2 * c_end("ffn_in", p))
            k_outer("ffn_out", 0)
            if stop < 11:
                return
            norm_part(3, X, lambda: act.wait_ge(sem("x2_ready"), 4))
            round_acts("q2", sem("acts"), 4 * TURN[3])

            def to_features(dst, scale=1.0):
                def epilogue(i, j, p, used):
                    act.wait_ge(mm_half, chunk_done(cur[0], j, i))
                    act_copy(dst(i, j, 0), acc[p][:, 0, :].rearrange("p (b s) -> p b s", b=2), scale=scale).then_inc(acc_used[p], 1)
                return epilogue
            phase("q2", to_features(lambda i, j, b: Q2[:, bass.ds(i * 8 + (4 * j + 2 * b), 2), :], SCALE))
            kv_dst = [(KC2, 0), (VC2, 0), (KS2, 0), (VS2, 1), (KW2, 0), (VW2, 1)]

            def kv_epilogue(i, j, p, used):
                dst, token = kv_dst[2 * i + j]
                if token:
                    to_tokens(lambda i, j, tt: dst[:, tt, :])(i, j, p, used)
                else:
                    to_features(lambda i, j, b: dst[:, 2 * b:2 * b + 2, :])(i, j, p, used)
            phase("kv2", kv_epilogue, straight=True)

            def g48_epilogue(i, j, p, used):
                act.wait_ge(mm_half, chunk_done(cur[0], j, i))
                act_copy(G48[:, :, :], acc[p][:, :, 0:48], ACT.Sigmoid).then_inc(acc_used[p], 2)
            phase("g48", g48_epilogue, width=48)
            LXY = XT(32, 32)
            phase("lru_in", to_features(lambda i, j, b: LXY[:, bass.ds(i * 8 + (4 * j + 2 * b), 2), :]))
            if stop < 12:
                return
            act_copy(lamc[:, 0:16], col("lru_lambda_2"), ACT.Abs).then_inc(sem("lam_abs"), 1)
            act.wait_ge(sem("lam_abs"), 1)
            act_copy(lamc[:, 0:16], lamc[:, 0:16], ACT.Exp, scale=-1.0).then_inc(sem("lam_exp"), 1)
            act.wait_ge(sem("lam_exp"), 1)
            act_copy(lamc[:, 0:16], lamc[:, 0:16], ACT.Ln, bias=1.0).then_inc(sem("lam_log"), 1)
            act.wait_ge(sem("lam_ready"), 1)
            for b in range(4):
                for n in range(4):
                    k = 4 * b + n
                    act.wait_ge(sem("lru_gates"), k + 1)
                    act_copy(RT[:, n], acc[2 + k % 2][:, 0, 0:S], ACT.Sigmoid, bias=col("lru_ba_2")[:, k:k + 1]).then_inc(sem("lru_r"), 1)
                    act_copy(IT[:, n], acc[2 + k % 2][:, 0, S:2 * S], ACT.Sigmoid, bias=col("lru_bi_2")[:, k:k + 1]).then_inc(sem("lru_r"), 1)
                act.wait_ge(sem("lru_scaled"), b + 1)
                act_copy(TT[:, :], RT[:, :], ACT.Tanh).then_inc(sem("lru_tanh"), 1)
                act_copy(AA[:, :], RT[:, :], ACT.Exp, scale=-1.0).then_inc(sem("lru_a"), 1)
                act.wait_ge(sem("lru_one_minus"), b + 1)
                act_copy(TT[:, :], TT[:, :], ACT.Sqrt).then_inc(sem("lru_sqrt"), 1)
                act_copy(LY[:, 4 * b:4 * b + 4], LY[:, 4 * b:4 * b + 4], ACT.Gelu_apprx_tanh).then_inc(sem("lru_gelu"), 1)
            if stop < 13:
                return
            for n in range(2):
                act.wait_ge(sem("cmp_hid"), n + 1)
                act_copy(X[:, 1, 256 + 64 * n:256 + 64 * n + 60], acc[2 + n][:, 0, 0:60], ACT.Gelu_apprx_tanh).then_inc(sem("cmp_gelu"), 1)
            act.wait_ge(sem("cmp_done"), 1)
            act_copy(KCMP[:, 0:60], acc[2][:, 1, 0:60]).then_inc(sem("cmp_kept"), 1)
            act.wait_ge(sem("cmp_done"), 2)
            act_copy(VCMP[0:15, :], acc[3][0:15, 1, :]).then_inc(sem("cmp_kept"), 1)
            if stop < 14:
                return
            for job in range(16):
                bb = job % 2
                for tt in range(NT):
                    u = 2 * job + tt
                    act.wait_ge(sem("attn2_max"), u + 1)
                    for seg in range(3):
                        lo, hi = SEG[seg]
                        st = 12 * bb + 6 * tt
                        act_copy(P2[:, bb, tt, lo:hi], P2[:, bb, tt, lo:hi], ACT.Exp, bias=smx[:, st + seg:st + seg + 1],
                                 accum_out=smx[:, st + 3 + seg:st + 4 + seg]).then_inc(sem("attn2_exp"), 1)
                act.wait_ge(sem("attn2_turned"), job + 1)
                if job >= 2:
                    act.wait_ge(sem("attn2_mm"), job - 1)
                act_copy(PT2[:, bb], acc[2][:, :, :].rearrange("p a (b s) -> p (a b) s", b=2)).then_inc(sem("attn2_pt"), 1)
                act_copy(PC2[0:15, bb], acc[3][0:15, 0, 0:S]).then_inc(sem("attn2_pt"), 1)
            act.wait_ge(sem("attn2_out"), 16)
            if stop < 15:
                return
            phase("gates2", gates(SG2, 4096))
            round_acts("proj_a", sem("acts_copied"), 0)
            phase("proj_a", None)
            round_acts("proj_b", sem("acts_copied"), 4)
            phase("proj_b", None)
            act.wait_ge(mm_half, PH["w_out"].H0)
            round_acts("w_out", sem("acts"), 4 * TURN["m2"])
            phase("w_out", None)
            if stop < 16:
                return
            norm_part(4, X, lambda: act.wait_ge(sem("x3_ready"), 4))
            round_acts("ffn_up", sem("acts"), 4 * TURN[4])

            def up_epilogue(i, j, p, used):
                if j == 1:
                    return
                act.wait_ge(acc_used[p], used.val(2, 2))
                act_copy(GT[:, 0], CV[:, 0], ACT.Gelu_apprx_tanh).then_inc(sem("gate_ready"), 1)
            phase("ffn_up", up_epilogue)
            if stop < 17:
                return
            for p in range(2):
                act.wait_ge(acc_used[p], 2 * c_end("ffn_up", p))
            k_outer("ffn_down", KF1)
            for tt in range(NT):
                act.wait_ge(sem("x4_ready"), 2 * tt + 2)
                act_copy(at(32 + 8 * tt, D), X[:, tt, :], ACT.Square, accum_out=stat[:, tt:tt + 1]).then_inc(sem("final_squares"), 1)
            act.wait_ge(sem("final_mean"), 1)
            act_copy(stat[:, 4:6], stat[:, 2:4], ACT.Sqrt).then_inc(sem("final_root"), 1)

        @block.vector
        def _(dve):
            v = nc.vector
            cur = [None]

            def tile(width=NW):
                def one(i, T, slot, g, j, tt, k0, nk):
                    ph = cur[0]
                    last = None
                    for h, (a, b) in enumerate(halves(nk)):
                        H = half_at(ph, g, h, i)
                        dve.wait_ge(w_hi, H.val(1, 1))
                        ring = (2 * ((ph.H0 // 2 + g) % 2) + h) % 4
                        last = v.tensor_tensor(WL[:, ring, 0:b - a, 0:width], raw[:, slot, a:b, 0:width],
                                               WH[:, ring, 0:b - a, 0:width].bitcast(F32), ALU.subtract)
                        last.then_inc(w_lo, 1)
                return one

            def ada(what, i, arg):
                ph = cur[0]
                ada_acc, ada_row, ada_brow = ada_place(ph.name)
                a = At(ph.A0, 1, i)
                if what == "row":
                    dve.wait_ge(ada_red, a.val(1, 1))
                    dve.wait_ge(ada_b_in, a.val(16, 16))
                    v.tensor_tensor(ada_row[0:1], acc[2][0:1, 0, :], ada_brow[0:1], ALU.add).then_inc(ada_rowed, 1)
                    return
                T, slot, q = arg
                dve.wait_ge(landed[slot], T.val(4, 16 - 4 * slot))
                for kk in range(4):
                    n = 4 * q + kk
                    count = a.val(16, n)
                    if n < 2:
                        if not (isinstance(i, int) and a.val() == 0):
                            dve.wait_ge(ada_red, a.val(1, 0))
                        v.tensor_scalar(ada_acc[:, n % 2], raw[:, slot, kk], cact[:, n:n + 1], None, ALU.mult).then_inc(ada_mac, 1)
                    else:
                        dve.wait_ge(ada_mac, a.val(16, n - 1))
                        v.scalar_tensor_tensor(ada_acc[:, n % 2], raw[:, slot, kk], cact[:, n:n + 1], ada_acc[:, n % 2],
                                               ALU.mult, ALU.add).then_inc(ada_mac, 1)

            def phase(name, epilogue, straight=False, width=NW):
                cur[0] = PH[name]
                products(dve, PH[name], tile(width), epilogue, ada=ada if PH[name].ada else None, straight=straight)

            def norm_part(n, src):
                dve.wait_ge(sem("norm_squares"), NT * (n + 1))
                v.tensor_scalar(stat[:, 2:4], stat[:, 0:2], 1.0 / D, EPS, ALU.mult, ALU.add).then_inc(sem("norm_mean"), 1)
                dve.wait_ge(sem("norm_root"), n + 1)
                v.reciprocal(stat[:, 6:8], stat[:, 4:6]).then_inc(sem("norm_inverse"), 1)
                dve.wait_ge(sem("norm_inverse"), n + 1)
                for tt in range(NT):
                    v.tensor_scalar(XN[:, tt], src[:, tt], stat[:, 6 + tt:7 + tt], None, ALU.mult).then_inc(sem("norm_rows"), 1)

            def rest(ready, g):
                dve.wait_ge(xh_ready, ready + g + 1)
                v.tensor_tensor(XL[:, 4 * g:4 * g + 4], XF[:, 4 * g:4 * g + 4], XH[:, 4 * g:4 * g + 4].bitcast(F32),
                                ALU.subtract).then_inc(xl_ready, 1)

            def turned(n, ready, gain=None, shift=None):
                for g in range(4):
                    dve.wait_ge(sem("turned"), 4 * TURN[n] + g + 1)
                    src = acc[2 + g % 2][:, :, :].rearrange("p a (b s) -> p (a b) s", b=2)
                    if gain is None:
                        v.tensor_copy(XF[:, 4 * g:4 * g + 4], src).then_inc(sem("acts"), 1)
                    elif shift is None:
                        v.tensor_tensor(XF[:, 4 * g:4 * g + 4], src, bc(gain[:, 4 * g:4 * g + 4], [P, 4, S]), ALU.mult).then_inc(sem("acts"), 1)
                    else:
                        v.tensor_tensor(XF[:, 4 * g:4 * g + 4], src, bc(gain[:, 4 * g:4 * g + 4], [P, 4, S]), ALU.mult).then_inc(sem("acts_gain"), 1)
                        dve.wait_ge(sem("acts_gain"), 4 * (TURN[n] - 4 - (TURN[n] == 6)) + g + 1)
                        v.tensor_tensor(XF[:, 4 * g:4 * g + 4], XF[:, 4 * g:4 * g + 4], bc(shift[:, 4 * g:4 * g + 4], [P, 4, S]), ALU.add).then_inc(sem("acts"), 1)
                    if g:
                        rest(ready, g - 1)
                rest(ready, 3)

            dve.wait_ge(sem("bias_in"), 48)
            v.tensor_copy(at(76, 768)[0:32].rearrange("p (h q) -> p h q", h=6), bc(at(32, 6)[0:32], [32, 6, P])).then_inc(sem("bias_wide"), 1)
            norm_part(0, X)
            turned(0, 0, col("g_mem"))
            if stop < 2:
                return
            dve.wait_ge(sem("small_set"), 3)
            dve.wait_ge(sem("cols_in"), 16)
            for dst, name, n, s in ((0, "g_qa", 6, SCALE), (6, "g_ka", 6, 1.0), (20, "g_qc", 4, SCALE), (24, "g_kc", 4, 1.0)):
                v.tensor_scalar(gq[:, dst:dst + n], col(name).broadcast_to([P, n]), s, None, ALU.mult).then_inc(sem("head_gain"), 1)
            v.tensor_scalar(gq[:, 12:18], one1.broadcast_to([P, 6]), SCALE, None, ALU.mult).then_inc(sem("head_gain"), 1)
            dve.wait_ge(sem("bias_back"), 16 * 12)
            for j in range(2):
                for tt in range(NT):
                    mk = at(36, 6 * S).rearrange("p (t g s) -> p t g s", t=2, g=3)
                    v.tensor_tensor(BI[:, j, tt], BI[:, j, tt], mk[:, tt], ALU.add).then_inc(sem("bias_ready"), 1)

            def to_tokens(dst):
                def epilogue(i, j, p, used):
                    dve.wait_ge(mm_half, chunk_done(cur[0], j, i))
                    v.tensor_copy(dst(i, j, 1), acc[p][:, 1, :]).then_inc(acc_used[p], 1)
                return epilogue
            if stop < 3:
                return
            dve.wait_ge(sem("c_ready"), 1)
            dve.wait_ge(xl_ready, 4)
            dve.wait_ge(sem("bias_ready"), 4)
            phase("mem", to_tokens(lambda i, j, tt: (Z[:, tt, 0:NW], VC[:, tt, :])[j]))
            if stop < 4:
                return

            def head_squares(view, n, dst, name, tmp, count):
                sq = tmp.rearrange("p (h d) -> p h d", h=n)
                v.tensor_tensor(sq, view, view, ALU.mult).then_inc(sem(name + "_sq"), 1)
                dve.wait_ge(sem(name + "_sq"), count)
                v.tensor_reduce(dst, sq, AX.X, ALU.add).then_inc(sem(name + "_sum"), 1)

            dve.wait_ge(acc_used[0], 2)
            kc = [Z[:, tt, 0:NW].rearrange("p (h d) -> p h d", h=4) for tt in range(NT)]
            for tt in range(NT):
                head_squares(kc[tt], 4, stat[:, 8 + 4 * tt:12 + 4 * tt], "kc", Z[:, tt, NW:2 * NW], tt + 1)
            dve.wait_ge(sem("kc_sum"), 2)
            v.tensor_scalar(stat[:, 8:16], stat[:, 8:16], 1.0 / HD, EPS, ALU.mult, ALU.add).then_inc(sem("kc_mean"), 1)
            dve.wait_ge(sem("kc_root"), 1)
            v.reciprocal(stat[:, 8:16], stat[:, 8:16]).then_inc(sem("kc_inverse"), 1)
            dve.wait_ge(sem("kc_inverse"), 1)
            for tt in range(NT):
                v.tensor_tensor(kc[tt], kc[tt], bc(stat[:, 8 + 4 * tt:12 + 4 * tt], [P, 4, HD]), ALU.mult).then_inc(sem("kc_normal"), 1)
            dve.wait_ge(sem("kc_turned"), 1)
            dve.wait_ge(sem("head_gain"), 5)
            v.tensor_tensor(QK[:, 24:28], acc[2][:, :, :].rearrange("p a (b s) -> p (a b) s", b=2),
                            bc(gq[:, 24:28], [P, 4, S]), ALU.mult).then_inc(sem("kc_ready"), 1)
            norm_part(1, X)
            turned(1, READY["mem"], col("g_mix"))
            if stop < 5:
                return
            phase("qkv", to_tokens(lambda i, j, tt: Z[:, tt, bass.ds(i * (2 * NW) + j * NW, NW)]))
            dve.wait_ge(acc_used[0], 2 * (PH["qkv"].C0 // 2 + 4))
            dve.wait_ge(acc_used[1], 2 * (PH["qkv"].C0 // 2 + 4))
            SEGS = [(0, 12, 0), (2304, 8, 12), (3584, 4, 20)]
            cnt = 0
            tmp = X[:, 1, 0:1536]
            for tt in range(NT):
                for c0, n, h0 in SEGS:
                    cnt += 1
                    if cnt > 1:
                        dve.wait_ge(sem("hd_sum"), cnt - 1)
                    head_squares(Z[:, tt, c0:c0 + n * HD].rearrange("p (h d) -> p h d", h=n), n,
                                 smx1[:, 24 * tt + h0:24 * tt + h0 + n], "hd", tmp[:, 0:n * HD], cnt)
            dve.wait_ge(sem("hd_sum"), cnt)
            v.tensor_scalar(smx1[:, 0:48], smx1[:, 0:48], 1.0 / HD, EPS, ALU.mult, ALU.add).then_inc(sem("heads_mean"), 1)
            dve.wait_ge(sem("heads_root"), 1)
            v.reciprocal(smx1[:, 0:48], smx1[:, 0:48]).then_inc(sem("heads_inverse"), 1)
            dve.wait_ge(sem("heads_inverse"), 1)
            for tt in range(NT):
                for c0, n, h0 in SEGS:
                    z = Z[:, tt, c0:c0 + n * HD].rearrange("p (h d) -> p h d", h=n)
                    v.tensor_tensor(z, z, bc(smx1[:, 24 * tt + h0:24 * tt + h0 + n], [P, n, HD]), ALU.mult).then_inc(sem("heads_scaled"), 1)
            dve.wait_ge(sem("heads_scaled"), 6)
            dve.wait_ge(sem("rope_in"), 48)
            rope = X[:, 0, 0:256].rearrange("p (t c f) -> p t c f", t=2, c=2)
            for tt in range(NT):
                for c0, n, gain in ((2304, 6, X[:, 0, 256:384]), (3072, 2, X[:, 0, 384:512])):
                    z = Z[:, tt, c0:c0 + n * HD].rearrange("p (h d) -> p h d", h=n)
                    v.tensor_tensor(z, z, gain.unsqueeze(1).broadcast_to([P, n, HD]), ALU.mult).then_inc(sem("rope_gain"), 1)
            dve.wait_ge(sem("rope_gain"), 4)
            for tt in range(NT):
                z = Z[:, tt, 2304:3328].rearrange("p (h f c) -> p c h f", h=8, c=2)
                x0, x1 = z[:, 0], z[:, 1]
                cs = rope[:, tt, 0].unsqueeze(1).broadcast_to([P, 8, 64])
                sn = rope[:, tt, 1].unsqueeze(1).broadcast_to([P, 8, 64])
                w = [X[:, 1, 512 * k:512 * k + 512].rearrange("p (h f) -> p h f", h=8) for k in range(4)]
                if tt:
                    dve.wait_ge(sem("roped"), 2)
                for k, (a, b) in enumerate(((x0, cs), (x1, sn), (x0, sn), (x1, cs))):
                    v.tensor_tensor(w[k], a, b, ALU.mult).then_inc(sem("rope_part"), 1)
                dve.wait_ge(sem("rope_part"), 4 * tt + 4)
                v.tensor_tensor(x0, w[0], w[1], ALU.subtract).then_inc(sem("roped"), 1)
                v.tensor_tensor(x1, w[2], w[3], ALU.add).then_inc(sem("roped"), 1)
            for g in range(6):
                dve.wait_ge(sem("heads_turned"), g + 1)
                v.tensor_tensor(QK[:, 4 * g:4 * g + 4], acc[2 + g % 2][:, :, :].rearrange("p a (b s) -> p (a b) s", b=2),
                                bc(gq[:, 4 * g:4 * g + 4], [P, 4, S]), ALU.mult).then_inc(sem("heads_ready"), 1)
            if stop < 6:
                return
            dve.wait_ge(ada_stored, 16 * (PH["qkv"].A0 + PH["qkv"].iters))

            def finish1(job):
                segs = 3 if job < 2 else 1
                b = job % 2
                for tt in range(NT):
                    u = 2 * job + tt
                    dve.wait_ge(sem("attn1_exp"), u + 1)
                    r = asum1[:, 2 * b + tt:2 * b + tt + 1]
                    v.reciprocal(r, r).then_inc(sem("attn1_inverse"), 1)
                    dve.wait_ge(sem("attn1_inverse"), u + 1)
                    pr = P1[:, b, tt, 0:256 * segs]
                    v.tensor_scalar(pr, pr, r, None, ALU.mult).then_inc(sem("attn1_probs"), 1)

            def out1(job):
                dve.wait_ge(sem("attn1_mm"), job + 1)
                v.tensor_copy(XF[:, job], acc[3][:, 1, 0:S]).then_inc(sem("attn1_out"), 1)

            for job in range(12):
                b = job % 2
                for tt in range(NT):
                    u = 2 * job + tt
                    dve.wait_ge(sem("attn1_scores"), u + 1)
                    mx = amax1[:, 2 * b + tt:2 * b + tt + 1]
                    if job < 2:
                        sc = P1[:, b, tt, 0:768]
                        v.tensor_tensor(sc, acc[tt][:, :, :].rearrange("p a s -> p (a s)")[:, 0:768],
                                        BI[:, job, tt].rearrange("p g s -> p (g s)"), ALU.add).then_inc(sem("attn1_biased"), 1)
                        dve.wait_ge(sem("attn1_biased"), u + 1)
                    else:
                        sc = acc[tt][:, 0, 0:256]
                    v.tensor_reduce(mx, sc, AX.X, ALU.max).then_inc(sem("attn1_top"), 1)
                    dve.wait_ge(sem("attn1_top"), u + 1)
                    v.tensor_scalar(mx, mx, -1.0, None, ALU.mult).then_inc(sem("attn1_max"), 1)
                if job:
                    out1(job - 1)
                finish1(job)
            out1(11)
            if stop < 7:
                return
            phase("gates", None)
            if stop < 8:
                return
            for g in range(3):
                rest(READY["gates"], g)

            def branch_epilogue(i, j, p, used):
                dve.wait_ge(mm_half, chunk_done(cur[0], j, i))
                gate = SG[:, :, D * j + NW * i:D * j + NW * i + NW]
                dst = M[:, :, NW * i:NW * i + NW]
                if j == 0:
                    v.tensor_tensor(dst, acc[p][:, :, :], gate, ALU.mult).then_inc(acc_used[p], 2)
                    return
                v.tensor_tensor(gate, acc[p][:, :, :], gate, ALU.mult).then_inc(acc_used[p], 2)
                dve.wait_ge(acc_used[p], used.val(2, 2))
                v.tensor_tensor(dst, dst, gate, ALU.add).then_inc(sem("merging1"), 1)
                dve.wait_ge(sem("merging1"), 2 * i + j)
            phase("branch", branch_epilogue, straight=True)
            turned("m1", READY["branch"])

            def residual(name, wait=None, gain=None):
                def epilogue(i, j, p, used):
                    dve.wait_ge(mm_half, chunk_done(cur[0], j, i))
                    x = X[:, :, bass.ds(i * (2 * NW) + j * NW, NW)]
                    if gain is not None:
                        tmp = at(8, 2 * NW).rearrange("p (t n) -> p t n", t=NT)
                        gb = gain(i, j)
                        if not (isinstance(i, int) and i == 0 and j == 0):
                            dve.wait_ge(sem(name), i * 2 + j)
                        v.tensor_tensor(tmp, acc[p][:, :, :], gb, ALU.mult).then_inc(acc_used[p], 2)
                        dve.wait_ge(acc_used[p], used.val(2, 2))
                        v.tensor_tensor(x, x, tmp, ALU.add).then_inc(sem(name), 1)
                        return
                    v.tensor_tensor(x, x, acc[p][:, :, :], ALU.add).then_inc(acc_used[p], 2)
                return epilogue
            dve.wait_ge(sem("x_again"), 16)
            phase("w_o", residual("x1_ready"))
            if stop < 9:
                return
            norm_part(2, X)
            turned(2, READY["w_o"], col("g_ffn"))

            def hidden(name, p, i, j, used):
                dve.wait_ge(mm_half, chunk_done(cur[0], j, i))
                src = acc[p][:, :, :].rearrange("p a (b s) -> p (a b) s", b=2)
                v.tensor_tensor(AT[:, bass.ds(i * 4, 4), :], GT[:, 0], src, ALU.mult).then_inc(acc_used[p], 2)

            def swiglu(i, j, p, used):
                if j == 0:
                    return
                dve.wait_ge(acc_used[1 - p], gate_uses(i).val(2, 2))
                hidden("hidden1", p, i, j, used)
            gate_uses = lambda i: pair_of(PH["ffn_in"], 0, i)[1]
            phase("ffn_in", swiglu)
            if stop < 10:
                return

            def k_outer(name, base):
                ph = PH[name]

                def body(i, first):
                    for j in range(4):
                        dve.wait_ge(sem("hidden_rounded"), At(base + j, 4, i).val(1, 1))
                        a = AT[:, bass.ds(i * 4 + j, 1), :] if not isinstance(i, int) else AT[:, 4 * i + j:4 * i + j + 1, :]
                        v.tensor_tensor(XL[:, j:j + 1], a, XH[:, j:j + 1].bitcast(F32), ALU.subtract).then_inc(sem("hidden_rest"), 1)
                        for h in range(2):
                            H = At(ph.H0 + 2 * j + h, 8, i)
                            ring = (ph.H0 + 2 * j + h) % 4
                            dve.wait_ge(w_hi, H.val(1, 1))
                            v.tensor_tensor(WL[:, ring], raw[:, j, 2 * h:2 * h + 2], WH[:, ring].bitcast(F32), ALU.subtract).then_inc(w_lo, 1)
                run(dve, ph, body)

            k_outer("ffn_out", 0)
            for n in range(4):
                dve.wait_ge(mm_half, PH["ffn_out"].H0 + PH["ffn_out"].hpi * PH["ffn_out"].iters)
                v.tensor_tensor(X[:, :, NW * n:NW * n + NW], X[:, :, NW * n:NW * n + NW], acc[n][:, :, :], ALU.add).then_inc(sem("x2_ready"), 1)
            if stop < 11:
                return
            dve.wait_ge(sem("mod_turned"), 1)
            v.tensor_copy(mod, acc[0][:, 0, 0:64]).then_inc(sem("mod_copied"), 1)
            dve.wait_ge(sem("mod_copied"), 1)
            for n, g in ((0, "norm1_g_2"), (2, "norm2_g_2")):
                m = mod[:, 16 * n:16 * n + 16]
                v.scalar_tensor_tensor(m, m, 1.0, col(g), ALU.add, ALU.mult).then_inc(sem("mod_ready"), 1)
            dve.wait_ge(sem("mod_ready"), 2)
            norm_part(3, X)
            turned(3, READY["ffn_in"], mod[:, 0:16], mod[:, 16:32])

            def to_features(dst, scale=1.0):
                def epilogue(i, j, p, used):
                    dve.wait_ge(mm_half, chunk_done(cur[0], j, i))
                    src = acc[p][:, 1, :].rearrange("p (b s) -> p b s", b=2)
                    if scale != 1.0:
                        v.tensor_scalar(dst(i, j, 1), src, scale, None, ALU.mult).then_inc(acc_used[p], 1)
                    else:
                        v.tensor_copy(dst(i, j, 1), src).then_inc(acc_used[p], 1)
                return epilogue
            phase("q2", to_features(lambda i, j, b: Q2[:, bass.ds(i * 8 + (4 * j + 2 * b), 2), :], SCALE))
            kv_dst = [(KC2, 0), (VC2, 0), (KS2, 0), (VS2, 1), (KW2, 0), (VW2, 1)]

            def kv_epilogue(i, j, p, used):
                dst, token = kv_dst[2 * i + j]
                if token:
                    to_tokens(lambda i, j, tt: dst[:, tt, :])(i, j, p, used)
                else:
                    to_features(lambda i, j, b: dst[:, 2 * b:2 * b + 2, :])(i, j, p, used)
            phase("kv2", kv_epilogue, straight=True)
            phase("g48", None, width=48)
            LXY = XT(32, 32)
            phase("lru_in", to_features(lambda i, j, b: LXY[:, bass.ds(i * 8 + (4 * j + 2 * b), 2), :]))
            if stop < 12:
                return
            v.tensor_scalar(lamc[:, 16:32], col("lru_lambda_2"), 0.0, None, ALU.min).then_inc(sem("lam_min"), 1)
            dve.wait_ge(sem("lam_min"), 1)
            dve.wait_ge(sem("lam_log"), 1)
            v.tensor_tensor(lamc[:, 0:16], lamc[:, 0:16], lamc[:, 16:32], ALU.subtract).then_inc(sem("lam_sub"), 1)
            dve.wait_ge(sem("lam_sub"), 1)
            v.tensor_scalar(lamc[:, 0:16], lamc[:, 0:16], 8.0, None, ALU.mult).then_inc(sem("lam_ready"), 1)
            dve.wait_ge(sem("lam_ready"), 1)
            dve.wait_ge(acc_used[0], 2 * c_end("lru_in", 0))
            dve.wait_ge(acc_used[1], 2 * c_end("lru_in", 1))
            cw = col("lru_conv_w_2")
            for b in range(4):
                if b:
                    dve.wait_ge(sem("lru_out"), b)
                for n in range(4):
                    k = 4 * b + n
                    v.tensor_scalar(UT[:, n], LX[:, k], cw[:, 48 + k:49 + k], col("lru_conv_b_2")[:, k:k + 1],
                                    ALU.mult, ALU.add).then_inc(sem("conv_tap"), 1)
                for tap in (1, 2, 3):
                    for n in range(4):
                        k = 4 * b + n
                        dve.wait_ge(sem("conv_tap"), 16 * b + 4 * (tap - 1) + n + 1)
                        v.scalar_tensor_tensor(UT[:, n, tap:S], LX[:, k, 0:S - tap], cw[:, 16 * (3 - tap) + k:16 * (3 - tap) + k + 1],
                                               UT[:, n, tap:S], ALU.mult, ALU.add).then_inc(sem("conv_tap"), 1)
                dve.wait_ge(sem("lru_r"), 8 * b + 8)
                v.tensor_tensor(RT, RT, bc(lamc[:, 4 * b:4 * b + 4], [P, 4, S]), ALU.mult).then_inc(sem("lru_scaled"), 1)
                v.tensor_tensor(IT, IT, UT, ALU.mult).then_inc(sem("lru_iu"), 1)
                dve.wait_ge(sem("lru_tanh"), b + 1)
                dve.wait_ge(sem("lru_iu"), b + 1)
                v.tensor_scalar(UT, TT, 1.0, None, ALU.add).then_inc(sem("lru_den"), 1)
                dve.wait_ge(sem("lru_den"), b + 1)
                v.reciprocal(UT, UT).then_inc(sem("lru_rec"), 1)
                dve.wait_ge(sem("lru_rec"), b + 1)
                v.scalar_tensor_tensor(TT, TT, 2.0, UT, ALU.mult, ALU.mult).then_inc(sem("lru_one_minus"), 1)
                dve.wait_ge(sem("lru_sqrt"), b + 1)
                v.tensor_tensor(IT, IT, TT, ALU.mult).then_inc(sem("lru_b"), 1)
                dve.wait_ge(sem("lru_b"), b + 1)
                dve.wait_ge(sem("lru_a"), b + 1)
                for n in range(4):
                    v.tensor_tensor_scan(UT[:, n], AA[:, n], IT[:, n], 0.0, ALU.mult, ALU.add).then_inc(sem("lru_h"), 1)
                dve.wait_ge(sem("lru_h"), 4 * b + 4)
                dve.wait_ge(sem("lru_gelu"), b + 1)
                v.tensor_tensor(LX[:, 4 * b:4 * b + 4], UT, LY[:, 4 * b:4 * b + 4], ALU.mult).then_inc(sem("lru_out"), 1)
            if stop < 13:
                return
            for n, (src, pos) in enumerate(((KC2, "cmp_pos_k_2"), (VC2, "cmp_pos_v_2"))):
                if n:
                    dve.wait_ge(sem("cmp_hid"), 1)
                else:
                    dve.wait_ge(sem("lru_gates"), 16)
                for half in range(2):
                    dst = X[:, 0, 1024 * half:1024 * half + 1024].rearrange("p (n l) -> p n l", l=16)
                    v.tensor_tensor(dst, src[:, :, :].rearrange("p g (n l) -> p (g n) l", l=16),
                                    col(pos)[:, 16 * half:16 * half + 16].unsqueeze(1).broadcast_to([P, 64, 16]),
                                    ALU.add).then_inc(sem("cmp_blocks"), 1)
            if stop < 14:
                return
            dve.wait_ge(sem("mask2_in"), 16)
            dve.wait_ge(sem("cmp_kept"), 2)
            mk = X[:, 0, 0:2 * 527].rearrange("p (t n) -> p t n", t=2)

            def finish2(job):
                bb = job % 2
                for tt in range(NT):
                    u = 2 * job + tt
                    st = 12 * bb + 6 * tt
                    dve.wait_ge(sem("attn2_exp"), 3 * u + 3)
                    r = smx[:, st + 3:st + 6]
                    v.tensor_scalar(r, r, 1e-30, None, ALU.max).then_inc(sem("attn2_guard"), 1)
                    dve.wait_ge(sem("attn2_guard"), u + 1)
                    v.reciprocal(r, r).then_inc(sem("attn2_inverse"), 1)
                    dve.wait_ge(sem("attn2_inverse"), u + 1)
                    v.tensor_tensor(smx[:, st + 3:st + 5], smx[:, st + 3:st + 5], G48[:, tt, 3 * job + 1:3 * job + 3], ALU.mult).then_inc(sem("attn2_gated"), 1)
                    v.tensor_tensor(smx[:, st + 5:st + 6], smx[:, st + 5:st + 6], G48[:, tt, 3 * job:3 * job + 1], ALU.mult).then_inc(sem("attn2_gated"), 1)
                    dve.wait_ge(sem("attn2_gated"), 2 * u + 2)
                    for seg in range(3):
                        lo, hi = SEG[seg]
                        v.tensor_scalar(P2[:, bb, tt, lo:hi], P2[:, bb, tt, lo:hi], smx[:, st + 3 + seg:st + 4 + seg], None,
                                        ALU.mult).then_inc(sem("attn2_probs"), 1)

            def out2(job):
                dve.wait_ge(sem("attn2_mm"), job + 1)
                v.tensor_copy(Q2[:, job], acc[3][:, 1, 0:S]).then_inc(sem("attn2_out"), 1)

            for job in range(16):
                bb = job % 2
                for tt in range(NT):
                    u = 2 * job + tt
                    st = 12 * bb + 6 * tt
                    dve.wait_ge(sem("attn2_scores"), u + 1)
                    if job >= 2:
                        dve.wait_ge(sem("attn2_turned"), job - 1)
                    v.tensor_tensor(P2[:, bb, tt], acc[tt][:, :, :].rearrange("p a s -> p (a s)")[:, 0:527], mk[:, tt], ALU.add).then_inc(sem("attn2_masked"), 1)
                    dve.wait_ge(sem("attn2_masked"), u + 1)
                    v.tensor_reduce(smx[:, st:st + 2], P2[:, bb, tt, 0:512].rearrange("p (g s) -> p g s", g=2), AX.X, ALU.max).then_inc(sem("attn2_top"), 1)
                    v.tensor_reduce(smx[:, st + 2:st + 3], P2[:, bb, tt, 512:527], AX.X, ALU.max).then_inc(sem("attn2_top"), 1)
                    dve.wait_ge(sem("attn2_top"), 2 * u + 2)
                    v.tensor_scalar(smx[:, st:st + 3], smx[:, st:st + 3], -1e25, -1.0, ALU.max, ALU.mult).then_inc(sem("attn2_max"), 1)
                if job:
                    out2(job - 1)
                finish2(job)
            out2(15)
            if stop < 15:
                return
            phase("gates2", None)

            def split_from(src, ready):
                for g in range(4):
                    v.tensor_copy(XF[:, 4 * g:4 * g + 4], src[:, 4 * g:4 * g + 4]).then_inc(sem("acts_copied"), 1)
                    if g:
                        rest(ready, g - 1)
                rest(ready, 3)
            split_from(Q2, READY["mix2"])

            def proj_epilogue(second):
                def epilogue(i, j, p, used):
                    dve.wait_ge(mm_half, chunk_done(cur[0], j, i))
                    a = SG2[:, :, bass.ds(i * (2 * NW) + j * NW, NW)]
                    if not second:
                        v.tensor_tensor(a, acc[p][:, :, :], a, ALU.mult).then_inc(acc_used[p], 2)
                        return
                    b = SG2[:, :, bass.ds(i * (2 * NW) + (j * NW + D), NW)]
                    v.tensor_tensor(b, acc[p][:, :, :], b, ALU.mult).then_inc(acc_used[p], 2)
                    dve.wait_ge(acc_used[p], used.val(2, 2))
                    v.tensor_tensor(a, a, b, ALU.add).then_inc(sem("merging2"), 1)
                return epilogue
            phase("proj_a", proj_epilogue(False))
            split_from(LX, READY["proj_a"])
            phase("proj_b", proj_epilogue(True))
            dve.wait_ge(sem("x_back"), 16)
            turned("m2", READY["proj_b"])
            dve.wait_ge(sem("g1_in"), 16)
            phase("w_out", residual("x3_ready", gain=lambda i, j: at(0, D)[:, bass.ds(i * (2 * NW) + j * NW, NW)].unsqueeze(1).broadcast_to([P, NT, NW])))
            if stop < 16:
                return
            norm_part(4, X)
            turned(4, READY["w_out"], mod[:, 32:48], mod[:, 48:64])
            fcw, fcb = col("ffn_conv_w_2"), col("ffn_conv_b_2")

            def up_epilogue(i, j, p, used):
                dve.wait_ge(mm_half, chunk_done(cur[0], j, i))
                if j == 1:
                    dve.wait_ge(sem("gate_ready"), i + 1)
                    hidden("hidden2", p, i, j, used)
                    return
                src = acc[p][:, :, :].rearrange("p a (b s) -> p (a b) s", b=2)
                for m in range(4):
                    k = bass.ds(i * 4 + m, 1) if not isinstance(i, int) else slice(4 * i + m, 4 * i + m + 1)
                    k2 = bass.ds(i * 4 + (m + 96), 1)
                    v.tensor_scalar(CV[:, 0, m], src[:, m], fcw[:, k2], fcb[:, k], ALU.mult, ALU.add).then_inc(sem("up_tap"), 1)
                for tap in (1, 2):
                    for m in range(4):
                        if (tap, m) == (2, 3):
                            dve.wait_ge(sem("up_tap"), i * 11 + 11)
                        else:
                            dve.wait_ge(sem("up_tap"), i * 11 + (4 * (tap - 1) + m + 1))
                        k = bass.ds(i * 4 + (m + 48 * (2 - tap)), 1)
                        last = v.scalar_tensor_tensor(CV[:, 0, m, tap:S], src[:, m, 0:S - tap], fcw[:, k], CV[:, 0, m, tap:S],
                                                      ALU.mult, ALU.add)
                        if (tap, m) != (2, 3):
                            last.then_inc(sem("up_tap"), 1)
                last.then_inc(acc_used[p], 2)
            phase("ffn_up", up_epilogue)
            if stop < 17:
                return
            k_outer("ffn_down", KF1)
            dve.wait_ge(sem("g2_in"), 16)
            dve.wait_ge(sem("final_g_in"), 16)
            dve.wait_ge(mm_half, PH["ffn_down"].H0 + PH["ffn_down"].hpi * PH["ffn_down"].iters)
            for tt in range(NT):
                for n in range(4):
                    tmp = at(64 + 2 * n, NW)
                    v.tensor_tensor(tmp, acc[n][:, tt, :], at(0, D)[:, NW * n:NW * n + NW], ALU.mult).then_inc(sem("down2_gated"), 1)
                dve.wait_ge(sem("down2_gated"), 4 * tt + 4)
                v.tensor_tensor(X[:, tt], X[:, tt], at(64, D), ALU.add).then_inc(sem("x4_ready"), 2)
                dve.wait_ge(sem("x4_ready"), 2 * tt + 2)
            dve.wait_ge(sem("final_squares"), NT)
            v.tensor_scalar(stat[:, 2:4], stat[:, 0:2], 1.0 / D, EPS, ALU.mult, ALU.add).then_inc(sem("final_mean"), 1)
            dve.wait_ge(sem("final_root"), 1)
            v.reciprocal(stat[:, 6:8], stat[:, 4:6]).then_inc(sem("final_inverse"), 1)
            dve.wait_ge(sem("final_inverse"), 1)
            for tt in range(NT):
                v.scalar_tensor_tensor(XN[:, tt], X[:, tt], stat[:, 6 + tt:7 + tt], at(8, D), ALU.mult, ALU.mult).then_inc(sem("final"), 1)

        @block.tensor
        def _(pe):
            def product_phase(name, modes, straight=False, width=NW):
                ph = PH[name]

                def body(i, first):
                    g = 0
                    for n, b in enumerate(ph.body):
                        if b[0] == "a":
                            continue
                        _, j, tt, k0, nk = b
                        p, used = pair_of(ph, j, i)
                        mode = modes(i, j) if callable(modes) else modes
                        if tt == 0 and not (isinstance(i, int) and used.val() == 0):
                            pe.wait_ge(acc_used[p], used.val(2, 0))
                        lasttile = tt == len(ph.chunks[j]) - 1
                        for h, (a, e) in enumerate(halves(nk)):
                            H = half_at(ph, g, h, i)
                            ring = (ph.H0 + 2 * g + h) % 4
                            pe.wait_ge(w_lo, H.val(1, 1))
                            mm = None
                            for k in range(a, e):
                                kx = k0 + k
                                start, stop_ = tt == 0 and k == 0, lasttile and k == nk - 1
                                if mode == "tokens":
                                    for s in range(NT):
                                        o = acc[p][:, s, 0:width]
                                        xh, xl = XH[:, kx, s * P:(s + 1) * P], XL[:, kx, s * P:(s + 1) * P]
                                        wh, wl = WH[:, ring, k - a, 0:width], WL[:, ring, k - a, 0:width]
                                        pe.matmul(o, xh, wh, start=start, stop=False)
                                        pe.matmul(o, xh, wl, start=False, stop=False)
                                        mm = pe.matmul(o, xl, wh, start=False, stop=stop_)
                                else:
                                    for m in range(4):
                                        o = acc[p][:, m // 2, (m % 2) * S:(m % 2 + 1) * S]
                                        wh = WH[:, ring, k - a, m * P:(m + 1) * P]
                                        wl = WL[:, ring, k - a, m * P:(m + 1) * P]
                                        pe.matmul(o, wh, XH[:, kx], start=start and m % 2 == 0, stop=False, skip_group_check=True)
                                        pe.matmul(o, wh, XL[:, kx], start=False, stop=False, skip_group_check=True)
                                        mm = pe.matmul(o, wl, XH[:, kx], start=False, stop=stop_, skip_group_check=True)
                            mm.then_inc(mm_half, 1)
                        g += 1
                    if ph.ada:
                        ada_acc = ada_place(name)[0]
                        a = At(ph.A0, 1, i)
                        pe.wait_ge(ada_mac, a.val(16, 16))
                        if not (isinstance(i, int) and a.val() == 0):
                            pe.wait_ge(ada_rowed, a.val())
                        for q in range(2):
                            mm = pe.matmul(acc[2][0:1, 0, :], one1, ada_acc[:, q], start=q == 0, stop=q == 1)
                        mm.then_inc(ada_red, 1)
                if straight:
                    for i in range(ph.iters):
                        body(i, i == 0)
                else:
                    run(pe, ph, body)

            def turn(n, src, wait):
                wait()
                for g in range(4):
                    if g >= 2:
                        pe.wait_ge(sem("acts"), 4 * TURN[n] + g - 1)
                    for k in range(4):
                        for tt in range(NT):
                            o = acc[2 + g % 2][:, k // 2, (k % 2) * S + tt * P:(k % 2) * S + (tt + 1) * P]
                            mm = pe.transpose(o, src[:, tt, (4 * g + k) * P:(4 * g + k + 1) * P], ident[:, :])
                    mm.then_inc(sem("turned"), 1)

            pe.wait_ge(sem("ident_in"), 16)
            pe.wait_ge(sem("bias_wide"), 1)
            for h in range(6):
                if h >= 2:
                    pe.wait_ge(sem("bias_row"), h - 1)
                pe.matmul(acc[2 + h % 2][:, 0, :], at(76, 768)[0:32, P * h:P * h + P], at(33, 512)[0:32],
                          start=True, stop=True).then_inc(sem("bias_mm"), 1)
            pe.wait_ge(sem("bias_row"), 6)
            turn(0, XN, lambda: pe.wait_ge(sem("norm_rows"), 1 * NT))
            pe.wait_ge(sem("acts"), 4)
            if stop < 3:
                return
            pe.wait_ge(xl_ready, READY["mem"])
            product_phase("mem", "tokens")
            if stop < 4:
                return
            pe.wait_ge(ada_rowed, 1)
            pe.wait_ge(sem("kc_normal"), 2)
            for h in range(4):
                for tt in range(NT):
                    mm = pe.transpose(acc[2][:, h // 2, (h % 2) * S + tt * P:(h % 2) * S + (tt + 1) * P],
                                      Z[:, tt, P * h:P * h + P], ident[:, :])
            mm.then_inc(sem("kc_turned"), 1)
            pe.wait_ge(sem("kc_ready"), 1)
            turn(1, XN, lambda: pe.wait_ge(sem("norm_rows"), 2 * NT))
            if stop < 5:
                return
            pe.wait_ge(xl_ready, READY["qkv"])
            product_phase("qkv", "tokens")
            pe.wait_ge(ada_rowed, 5)
            pe.wait_ge(sem("heads_scaled"), 6)
            pe.wait_ge(sem("roped"), 4)
            HC = [P * h for h in range(12)] + [2304 + P * h for h in range(8)] + [3584 + P * h for h in range(4)]
            for g in range(6):
                if g >= 2:
                    pe.wait_ge(sem("heads_ready"), g - 1)
                for k in range(4):
                    for tt in range(NT):
                        c = HC[4 * g + k]
                        mm = pe.transpose(acc[2 + g % 2][:, k // 2, (k % 2) * S + tt * P:(k % 2) * S + (tt + 1) * P],
                                          Z[:, tt, c:c + P], ident[:, :])
                mm.then_inc(sem("heads_turned"), 1)
            if stop < 6:
                return
            pe.wait_ge(sem("heads_ready"), 6)
            pe.wait_ge(sem("bias_ready"), 4)

            def keys1(job):
                if job < 2:
                    return [(2 * g + job, 6 + 2 * g + job, lambda kt, h=2 * g + job: Z[:, kt, 1536 + P * h:1536 + P * h + P])
                            for g in range(3)]
                if job < 8:
                    h = job - 2
                    return [(12 + h, 18 + h // 3, lambda kt: Z[:, kt, 3328 + P * (h // 3):3328 + P * (h // 3) + P])]
                h = job - 8
                return [(20 + h, 24 + h, lambda kt: VC[:, kt, P * h:P * h + P])]

            def scores1(job):
                for tt in range(NT):
                    if job >= 1:
                        pe.wait_ge(sem("attn1_exp"), 2 * (job - 1) + tt + 1)
                    for g, (q, k, _) in enumerate(keys1(job)):
                        mm = pe.matmul(acc[tt][:, g // 2, (g % 2) * S:(g % 2 + 1) * S], QK[:, q, tt * P:(tt + 1) * P], QK[:, k],
                                       start=True, stop=True)
                    mm.then_inc(sem("attn1_scores"), 1)

            def values1(job):
                segs = keys1(job)
                pe.wait_ge(sem("attn1_probs"), 2 * job + 2)
                if job:
                    pe.wait_ge(sem("attn1_pt"), pt_count(job - 1))
                for g in range(len(segs)):
                    for kt in range(NT):
                        n = 2 * g + kt
                        for tt in range(NT):
                            o = acc[2 + n // 4][:, (n % 4) // 2, (n % 2) * S + tt * P:(n % 2) * S + (tt + 1) * P]
                            mm = pe.transpose(o, P1[:, job % 2, tt, S * g + P * kt:S * g + P * kt + P], ident[:, :])
                mm.then_inc(sem("attn1_turned"), 1)
                pe.wait_ge(sem("attn1_pt"), pt_count(job))
                if job:
                    pe.wait_ge(sem("attn1_out"), job)
                for g, (_, _, value) in enumerate(segs):
                    for kt in range(NT):
                        n = 2 * g + kt
                        mm = pe.matmul(acc[3][:, 1, 0:S], value(kt), PT1[:, job % 2, n], start=n == 0, stop=n == 2 * len(segs) - 1)
                mm.then_inc(sem("attn1_mm"), 1)

            def pt_count(job):
                return 2 * min(job + 1, 2) + max(job - 1, 0)

            scores1(0)
            for job in range(12):
                if job + 1 < 12:
                    scores1(job + 1)
                values1(job)
            pe.wait_ge(sem("attn1_out"), 12)
            if stop < 7:
                return
            product_phase("gates", "tokens")
            if stop < 8:
                return
            pe.wait_ge(xl_ready, READY["branch"])
            product_phase("branch", "tokens", straight=True)
            turn("m1", M, lambda: pe.wait_ge(sem("merging1"), 8))
            pe.wait_ge(xl_ready, READY["w_o"])
            product_phase("w_o", "tokens")
            if stop < 9:
                return
            pe.wait_ge(ada_rowed, 13)
            turn(2, XN, lambda: pe.wait_ge(sem("norm_rows"), 3 * NT))
            pe.wait_ge(xl_ready, READY["ffn_in"])
            product_phase("ffn_in", "features")
            if stop < 10:
                return

            def k_outer(name, base):
                ph = PH[name]
                for p in range(2):
                    pe.wait_ge(acc_used[p], 2 * c_end(before[name], p))

                def body(i, first):
                    for j in range(4):
                        pe.wait_ge(sem("hidden_rest"), At(base + j, 4, i).val(1, 1))
                        for h in range(2):
                            H = At(ph.H0 + 2 * j + h, 8, i)
                            ring = (ph.H0 + 2 * j + h) % 4
                            pe.wait_ge(w_lo, H.val(1, 1))
                            for nn in range(2):
                                for s in range(NT):
                                    o = acc[2 * h + nn][:, s, :]
                                    xh, xl = XH[:, j, s * P:(s + 1) * P], XL[:, j, s * P:(s + 1) * P]
                                    st = first and j == 0
                                    pe.matmul(o, xh, WH[:, ring, nn], start=st, stop=False, skip_group_check=True)
                                    pe.matmul(o, xh, WL[:, ring, nn], start=False, stop=False, skip_group_check=True)
                                    mm = pe.matmul(o, xl, WH[:, ring, nn], start=False, stop=True, skip_group_check=True)
                            mm.then_inc(mm_half, 1)
                run(pe, ph, body)
            before = {"ffn_out": "ffn_in", "ffn_down": "ffn_up"}
            pe.wait_ge(ada_rowed, ADA_CHUNKS)
            k_outer("ffn_out", 0)
            if stop < 11:
                return
            pe.wait_ge(sem("x2_ready"), 4)
            pe.wait_ge(sem("mod_in"), 64)
            pe.transpose(acc[0][:, 0, 0:64], at(88, P)[0:64], ident[0:64, 0:64]).then_inc(sem("mod_turned"), 1)
            turn(3, XN, lambda: pe.wait_ge(sem("norm_rows"), 4 * NT))
            pe.wait_ge(xl_ready, READY["mix2"])
            product_phase("q2", "features")
            product_phase("kv2", lambda i, j: ("features", "features", "features", "tokens", "features", "tokens")[2 * i + j], straight=True)
            product_phase("g48", "tokens", width=48)
            product_phase("lru_in", "features")
            if stop < 12:
                return
            pe.wait_ge(sem("lru_w_in"), 32)
            for k in range(16):
                b, n = k // 4, k % 4
                pe.wait_ge(sem("conv_tap"), 16 * b + 12 + n + 1)
                if k >= 2:
                    pe.wait_ge(sem("lru_r"), 2 * (k - 1))
                pe.matmul(acc[2 + k % 2][:, 0, 0:S], X[:, 0, P * k:P * k + P], UT[:, n], start=True, stop=True)
                pe.matmul(acc[2 + k % 2][:, 0, S:2 * S], X[:, 1, P * k:P * k + P], UT[:, n], start=True, stop=True).then_inc(sem("lru_gates"), 1)
            pe.wait_ge(sem("lru_r"), 32)
            if stop < 13:
                return
            for n in range(2):
                pe.wait_ge(sem("cmp_in"), 16 * n + 16)
                pe.wait_ge(sem("cmp_blocks"), 2 * n + 2)
                for l in range(32):
                    half, off = l // 16, l % 16
                    blocks = X[:, 0, 1024 * half:1024 * half + 1024].rearrange("p (g n l) -> p g n l", g=4, l=16)
                    mm = pe.matmul(acc[2 + n][:, 0, 0:60].rearrange("p (g n) -> p g n", g=4), at(0, 4096)[:, P * l:P * l + P],
                                   blocks[:, :, half:half + 15, off], start=l == 0, stop=l == 31)
                mm.then_inc(sem("cmp_hid"), 1)
            pe.wait_ge(sem("cmp_gelu"), 2)
            pe.wait_ge(sem("cmp2_in"), 32)
            pe.matmul(acc[2][:, 1, 0:60], X[:, 1, 0:P], X[:, 1, 256:316], start=True, stop=True).then_inc(sem("cmp_done"), 1)
            for g in range(4):
                mm = pe.matmul(acc[3][0:15, 1, P * g:P * g + P], X[:, 1, 320 + 15 * g:335 + 15 * g], X[:, 1, P:2 * P], start=True, stop=True)
            mm.then_inc(sem("cmp_done"), 1)
            pe.wait_ge(sem("cmp_kept"), 2)
            if stop < 14:
                return

            def scores2(job):
                kv = job // 4
                for tt in range(NT):
                    if job >= 1:
                        pe.wait_ge(sem("attn2_masked"), 2 * (job - 1) + tt + 1)
                    q = Q2[:, job, tt * P:(tt + 1) * P]
                    pe.matmul(acc[tt][:, 0, 0:S], q, KS2[:, kv], start=True, stop=True)
                    pe.matmul(acc[tt][:, 0, S:2 * S], q, KW2[:, kv], start=True, stop=True)
                    pe.matmul(acc[tt][:, 1, 0:15], q, KCMP[:, 15 * kv:15 * kv + 15], start=True, stop=True).then_inc(sem("attn2_scores"), 1)

            def values2(job):
                kv, bb = job // 4, job % 2
                pe.wait_ge(sem("attn2_probs"), 6 * job + 6)
                if job:
                    pe.wait_ge(sem("attn2_pt"), 2 * job)
                for g in range(2):
                    for kt in range(NT):
                        n = 2 * g + kt
                        for tt in range(NT):
                            pe.transpose(acc[2][:, n // 2, (n % 2) * S + tt * P:(n % 2) * S + (tt + 1) * P],
                                         P2[:, bb, tt, S * g + P * kt:S * g + P * kt + P], ident[:, :])
                for tt in range(NT):
                    mm = pe.transpose(acc[3][0:15, 0, tt * P:(tt + 1) * P], P2[:, bb, tt, 512:527], ident[:, :])
                mm.then_inc(sem("attn2_turned"), 1)
                pe.wait_ge(sem("attn2_pt"), 2 * job + 2)
                if job:
                    pe.wait_ge(sem("attn2_out"), job)
                o = acc[3][:, 1, 0:S]
                for kt in range(NT):
                    pe.matmul(o, VS2[:, kt, P * kv:P * kv + P], PT2[:, bb, kt], start=kt == 0, stop=False)
                for kt in range(NT):
                    pe.matmul(o, VW2[:, kt, P * kv:P * kv + P], PT2[:, bb, 2 + kt], start=False, stop=False)
                pe.matmul(o, VCMP[0:15, P * kv:P * kv + P], PC2[0:15, bb], start=False, stop=True).then_inc(sem("attn2_mm"), 1)

            scores2(0)
            for job in range(16):
                if job + 1 < 16:
                    scores2(job + 1)
                values2(job)
            pe.wait_ge(sem("attn2_out"), 16)
            if stop < 15:
                return
            product_phase("gates2", "tokens")
            pe.wait_ge(xl_ready, READY["proj_a"])
            product_phase("proj_a", "tokens")
            pe.wait_ge(xl_ready, READY["proj_b"])
            product_phase("proj_b", "tokens")
            turn("m2", SG2, lambda: pe.wait_ge(sem("merging2"), 4))
            pe.wait_ge(xl_ready, READY["w_out"])
            product_phase("w_out", "tokens")
            if stop < 16:
                return
            turn(4, XN, lambda: pe.wait_ge(sem("norm_rows"), 5 * NT))
            pe.wait_ge(xl_ready, READY["ffn_up"])
            product_phase("ffn_up", "features")
            if stop < 17:
                return
            k_outer("ffn_down", KF1)


def _bucket(rel):
    nb, max_dist = 16, 1024
    n = np.abs(rel)
    large = nb // 2 + (np.log(np.maximum(n, 1).astype(np.float32) / np.float32(nb // 2))
                       / np.float32(np.log(max_dist / (nb // 2))) * np.float32(nb - nb // 2)).astype(np.int32)
    return np.where(rel > 0, nb, 0) + np.where(n < nb // 2, n, np.minimum(large, nb - 1))


def _constants():
    pos = np.arange(S)
    diff = np.arange(-255, 256)
    one_hot = np.zeros((32, 512), np.float32)
    one_hot[_bucket(diff), diff + 255] = 1.0
    rel = pos[None, :] - pos[:, None]
    ok = [np.abs(rel) <= 64] + [(rel % dil == 0) & (np.abs(rel) // dil <= 64) for dil in (4, 16)]
    masks_a = np.stack([np.where(m, 0.0, NEG) for m in ok]).astype(np.float32)
    masks_a = masks_a.reshape(3, NT, P, S).transpose(2, 1, 0, 3).reshape(P, -1)
    causal = np.where(rel <= 0, 0.0, NEG)
    ends = np.arange(15) * 16 + 31
    cmp = np.where(ends[None, :] <= pos[:, None], 0.0, NEG)
    masks_2 = np.concatenate([causal, causal, cmp], 1).astype(np.float32)
    masks_2 = masks_2.reshape(NT, P, 527).transpose(1, 0, 2).reshape(P, -1)
    inv = np.float32(10000.0) ** (-np.arange(32, dtype=np.float32) / np.float32(32))
    r, c = (pos // 64).astype(np.float32), (pos % 64).astype(np.float32)
    ang = np.concatenate([r[:, None] * inv, c[:, None] * inv], 1).astype(np.float32)
    rope = np.stack([np.cos(ang), np.sin(ang)], 1).astype(np.float32)
    rope = rope.reshape(NT, P, 2, 64).transpose(1, 0, 2, 3).reshape(P, -1)
    return {"identity": np.eye(P, dtype=np.float32), "one_hot": one_hot, "masks_a": masks_a, "masks_2": masks_2,
            "rope": rope}


_AS_IS = ["rel_bias"]
_FIRST = ["w_in", "g_qb", "g_kb", "w_mem_kv", "w_br_a", "w_br_b", "w_br_c", "w_o", "w_ffn_in", "w_ffn_out",
          "ada_w_2", "w_in_2", "cmp_w1_k_2", "cmp_w2_k_2", "cmp_w1_v_2", "cmp_w2_v_2", "lru_wa_2", "lru_wi_2",
          "proj_a_2", "proj_b_2", "w_out_2", "ffn_up_2", "ffn_down_2", "x", "mem"]


def _inputs(inputs):
    a = {n: np.ascontiguousarray(inputs[n]) for n in _AS_IS}
    a |= {n: np.ascontiguousarray(inputs[n][0]) for n in _FIRST}
    a["g_qb"], a["g_kb"] = a["g_qb"].reshape(HD), a["g_kb"].reshape(HD)
    a["ada_b_2"] = np.ascontiguousarray(inputs["ada_b_2"]).reshape(1, -1)
    a["final_g_2"] = np.ascontiguousarray(inputs["final_g_2"]).reshape(-1)
    a["vectors"] = np.ascontiguousarray(np.concatenate(
        [np.asarray(inputs[n]).reshape(-1, P) for n, _ in VECTORS]).T)
    a |= _constants()
    return a


def build(nc, a, stop=99):
    t = {n: nc.dram_tensor(f"in_{n}", v.shape, mybir.dt.from_np(v.dtype), kind="ExternalInput").ap()
         for n, v in a.items()}
    out = nc.dram_tensor("out_0", (S, D), F32, kind="ExternalOutput").ap()
    two_block_program(nc, t, out, stop)


def kernel(**inputs):
    import concourse.bacc as bacc
    from concourse.bass_utils import run_bass_kernel_spmd

    a = _inputs(inputs)
    nc = bacc.Bacc("TRN2", target_bir_lowering=False, num_devices=1)
    build(nc, a)
    r = run_bass_kernel_spmd(nc, [{f"in_{n}": v for n, v in a.items()}], core_ids=[0])
    return r.results[0]["out_0"].reshape(1, S, D)
```

```python
from contextlib import ExitStack

import numpy as np

import concourse.bass as bass
from concourse import mybir

F32 = mybir.dt.float32
F32R = mybir.dt.float32r
ALU = mybir.AluOpType
ACT = mybir.ActivationFunctionType
AX = mybir.AxisListType

P = 128
S = 256
NT = S // P
D = 2048
KD = D // P
NW = 512
EPS = 1e-6
HD = 128
SCALE = float(HD) ** -0.5
NEG = -1e30

FF1 = 5632
KF1 = FF1 // P
FF2 = 6144
KF2 = FF2 // P
A_GROUPS, A_PER = 3, 2
ADA_CHUNKS = 6 * D // NW

VECTORS = [("c_2", 16), ("g_mem", 16), ("g_mix", 16), ("g_ffn", 16), ("norm1_g_2", 16), ("norm2_g_2", 16),
           ("g_qa", 1), ("g_ka", 1), ("g_qc", 1), ("g_kc", 1),
           ("lru_lambda_2", 16), ("lru_ba_2", 16), ("lru_bi_2", 16), ("lru_conv_b_2", 16), ("lru_conv_w_2", 64),
           ("ffn_conv_w_2", 144), ("ffn_conv_b_2", 48), ("cmp_pos_k_2", 32), ("cmp_pos_v_2", 32)]
COL = {}
_at = 0
for _n, _k in VECTORS:
    COL[_n] = _at
    _at += _k
NCOL = _at


READY = {"mem": 4, "qkv": 8, "gates": 8, "branch": 11, "w_o": 15, "ffn_in": 19, "mix2": 23,
         "proj_a": 27, "proj_b": 31, "w_out": 35, "ffn_up": 39}


TURN = {0: 0, 1: 1, "m1": 2, 2: 3, 3: 4, "m2": 5, 4: 6}
TURN_PAIRS = {0: (2, 3), 1: (3, 3), "m1": (2, 3), 2: (3, 3), 3: (0, 1), "m2": (2, 3), 4: (2, 3)}


class At:

    def __init__(self, base, per=0, i=0):
        self.base, self.per, self.i = base, per, i

    def val(self, scale=1, offset=0):
        const = scale * self.base + offset
        step = scale * self.per
        if isinstance(self.i, int):
            return const + step * self.i
        if step == 0:
            return const
        return self.i * step + const


K16 = [(0, 4), (4, 4), (8, 4), (12, 4)]
BRANCH = [[(0, 2)], [(2, 3), (5, 3)], [(8, 4)]]


def body_of(chunks, ada):
    out, q = [], 0
    for j, tiles in enumerate(chunks):
        for t, (k0, nk) in enumerate(tiles):
            out.append(("g", j, t, k0, nk))
            if ada and t % 2 == 0:
                out.append(("a", q, 0, 0, 0))
                q += 1
    return out


class Phase:
    def __init__(self, name, iters, chunks, ada=False):
        self.name, self.iters, self.chunks, self.ada = name, iters, chunks, ada
        self.body = body_of(chunks, ada)


def plan():
    two = [K16, K16]
    phases = [Phase("mem", 1, two, True), Phase("qkv", 4, two, True), Phase("gates", 6, two, True),
              Phase("branch", 4, BRANCH), Phase("w_o", 2, two, True), Phase("ffn_in", 11, two, True),
              Phase("ffn_out", KF1 // 4, [[(0, 1)] * 4]),
              Phase("q2", 2, two), Phase("kv2", 3, two), Phase("g48", 1, [K16]),
              Phase("lru_in", 4, two), Phase("gates2", 4, two), Phase("proj_a", 2, two), Phase("proj_b", 2, two),
              Phase("w_out", 2, two), Phase("ffn_up", 12, two), Phase("ffn_down", KF2 // 4, [[(0, 1)] * 4])]
    t = h = c = a = 0
    for p in phases:
        p.T0, p.H0, p.C0, p.A0 = t, h, c, a
        p.tpi = len(p.body)
        p.hpi = 2 * sum(b[0] == "g" for b in p.body)
        p.cpi = 0 if p.name in ("ffn_out", "ffn_down") else len(p.chunks)
        t += p.tpi * p.iters
        h += p.hpi * p.iters
        c += p.cpi * p.iters
        a += p.iters if p.ada else 0
        assert p.T0 % 4 == 0 and p.tpi % 4 == 0, p.name
    assert a == ADA_CHUNKS
    return {p.name: p for p in phases}


def two_block_program(nc, t, out, stop=99):
    PH = plan()
    ctx = ExitStack()
    with ctx:
        def sb(name, shape, dt):
            return ctx.enter_context(nc.sbuf_tensor(name, shape, dt))

        sems = {}

        def sem(name):
            if name not in sems:
                sems[name] = ctx.enter_context(nc.semaphore(name))
            return sems[name]

        raw = sb("raw", [P, 4, 4, NW], F32)
        WH = sb("WH", [P, 4, 2, NW], F32R)
        WL = sb("WL", [P, 4, 2, NW], F32R)
        XH = sb("XH", [P, KD, S], F32R)
        XL = sb("XL", [P, KD, S], F32R)
        X = sb("X", [P, NT, D], F32)
        KB = 256
        arena = sb("arena", [P, 92 * KB], F32)
        cols = sb("cols", [P, NCOL], F32)
        ident = sb("ident", [P, P], F32)
        small = sb("small", [P, 326], F32)
        acc = [ctx.enter_context(nc.psum_tensor(f"acc{i}", [P, 2, NW], F32)) for i in range(4)]

        def at(kb, n):
            return arena[:, int(kb * KB):int(kb * KB) + n]

        XF = at(0, KD * S).rearrange("p (k s) -> p k s", k=KD)
        XN = at(16, NT * D).rearrange("p (t n) -> p t n", t=NT)
        junk = at(64, NT * NW).rearrange("p (t n) -> p t n", t=NT)
        root_wide = at(68, NT * P).rearrange("p (t n) -> p t n", t=NT)
        KC = at(56, NT * NW).rearrange("p (t n) -> p t n", t=NT)
        Z = at(16, NT * 4096).rearrange("p (t n) -> p t n", t=NT)
        QK = at(48, 28 * S).rearrange("p (h s) -> p h s", h=28)
        VC = at(76, NT * NW).rearrange("p (t n) -> p t n", t=NT)
        BI = at(80, 12 * S).rearrange("p (j t g s) -> p j t g s", j=2, t=2, g=3)
        SG = at(16, NT * 6144).rearrange("p (t n) -> p t n", t=NT)
        M = at(64, NT * D).rearrange("p (t n) -> p t n", t=NT)
        AT = at(16, 48 * S).rearrange("p (k s) -> p k s", k=48)
        GT = at(64, 2 * 4 * S).rearrange("p (b m s) -> p b m s", b=2, m=4)
        CV = at(72, 2 * 4 * S).rearrange("p (b m s) -> p b m s", b=2, m=4)

        def ada_place(name):
            kb = {"mem": 48, "qkv": 0}.get(name, 80)
            return at(kb, 2 * NW).rearrange("p (b n) -> p b n", b=2), at(kb + 4, NW), at(kb + 6, NW)

        def col(name, n=None, first=0):
            n = dict(VECTORS)[name] if n is None else n
            return cols[:, COL[name] + first:COL[name] + first + n]

        def bc(ap, shape):
            return ap.unsqueeze(2).broadcast_to(shape)

        zero1 = small[:, 0:1]
        one1 = small[:, 1:2]
        cact = small[:, 2:18]
        stat = small[:, 18:34]
        gq = small[:, 34:62]
        smx = small[:, 290:326]
        mod = small[:, 94:158]
        lamc = small[:, 158:190]
        G48 = small[:, 190:286].rearrange("p (t n) -> p t n", t=NT)

        XT = lambda kb, n: at(kb, n * S).rearrange("p (k s) -> p k s", k=n)
        Q2, LX, LY = XT(16, 16), XT(32, 16), XT(48, 16)
        KC2, VC2, KS2, KW2 = XT(64, 4), XT(68, 4), XT(72, 4), XT(76, 4)
        VS2 = at(80, NT * NW).rearrange("p (t n) -> p t n", t=NT)
        VW2 = at(84, NT * NW).rearrange("p (t n) -> p t n", t=NT)
        KCMP = at(88, 64)
        VCMP = at(89, 512)
        SG2 = at(48, NT * 4096).rearrange("p (t n) -> p t n", t=NT)

        smx1 = mod
        HEADS = [(-1, KC[:, :, :], 24), (0, Z[:, :, 0:512], 0), (1, Z[:, :, 512:1024], 4), (2, Z[:, :, 1024:1536], 8),
                 (5, Z[:, :, 2304:3072], 12), (6, Z[:, :, 3072:3328], 18), (7, Z[:, :, 3584:4096], 20)]
        HEAD_STATS = smx1[:, 0:56].rearrange("p (t h) -> p t h", t=NT)
        HEAD_PAIR = (3, 3, 3, 3, 2, 3, 2)
        HEAD_GROUPS = (6, 0, 1, 2, 5, 3, 4)

        amax1, asum1 = smx[:, 0:6], smx[:, 6:12]
        x_flat = X[:, :, :].rearrange("p t n -> p (t n)")

        def probs1(job):
            n, start = (1536, 1536 * job) if job < 2 else (512, (3072, 3584, 0)[(job - 2) % 3])
            return x_flat[:, start:start + n].rearrange("p (t n) -> p t n", t=NT)
        PT1 = Z[:, :, 0:1536].rearrange("p b (k s) -> p b k s", k=6)
        IT2, UT2 = (XT(0, 4), XT(4, 4)), (XT(8, 4), XT(12, 4))
        RT, TT = (acc[p][:, :, :].rearrange("p a (b s) -> p (a b) s", b=2) for p in (1, 0))
        W1 = raw[:, :, :, :].rearrange("p (n s) k e -> p n (s k e)", n=2)
        CMP_HID = at(88.25, 2 * 64).rearrange("p (n e) -> p n e", n=2)
        CMP_W2 = at(91, 2 * P).rearrange("p (n e) -> p n e", n=2)
        SEG = [(2 * S, 2 * S + 15), (0, S), (S, 2 * S)]
        P2 = at(0, 6 * 527).rearrange("p (b t n) -> p b t n", b=3, t=2)
        PC2 = at(13, 2 * S).rearrange("p (b s) -> p b s", b=2)
        PT2 = X[:, 1, :].rearrange("p (b k s) -> p b k s", b=2, k=4)

        mod_dram = nc.dram_tensor("mod_scratch", (6 * D,), F32, kind="Internal").ap()
        bias_dram = nc.dram_tensor("bias_scratch", (6, P, 2 * S), F32, kind="Internal").ap()
        x_dram = nc.dram_tensor("x_scratch", (P, NT * D), F32, kind="Internal").ap()

        landed = [sem(f"tile_landed{i}") for i in range(4)]
        w_hi, w_lo = sem("weights_rounded"), sem("weights_rest")
        mm_half = sem("half_multiplied")
        acc_used = [sem("acc_used0"), sem("acc_used1")]
        ada_mac, ada_red, ada_rowed = sem("ada_multiplied"), sem("ada_reduced"), sem("ada_row_ready")
        ada_b_in, ada_stored = sem("ada_bias_landed"), sem("ada_row_stored")
        xh_ready, xl_ready = sem("acts_rounded"), sem("acts_rest")

        def run(eng, ph, body):
            body(0, True)
            if ph.iters > 1:
                with eng.Fori(1, ph.iters) as i:
                    body(i, False)

        def c_end(name, p):
            ph = PH[name]
            return (ph.C0 + ph.cpi * ph.iters + 1 - p) // 2

        def last_half(ph, n, i):
            g = sum(b[0] == "g" for b in ph.body[:n])
            return At(ph.H0 + 2 * g + 1, ph.hpi, i)

        def chunk_done(ph, j, i):
            n = max(n for n, b in enumerate(ph.body) if b[0] == "g" and b[1] == j)
            return last_half(ph, n, i).val(1, 1)

        def pair_of(ph, j, i):
            c = ph.C0 + j
            if ph.cpi == 3:
                c += 3 * i
                return c % 2, At(c // 2)
            return c % 2, At(c // 2, 1, i)

        block = ctx.enter_context(nc.Block())

        @block.sync
        def _(sp):
            tail = [None]

            def reuse(ph, n, i, first):
                if n >= 4:
                    m, before, at_i = n - 4, ph, i
                elif not first:
                    m, before, at_i = n - 4 + ph.tpi, ph, i - 1
                elif tail[0]:
                    before = tail[0]
                    m, at_i = n - 4 + before.tpi, before.iters - 1
                else:
                    if n == 2:
                        sp.wait_ge(sem("mem_in"), 16)
                    return
                if before.body[m][0] == "a":
                    sp.wait_ge(ada_mac, At(before.A0, 1, at_i).val(16, 4 * before.body[m][1] + 4))
                else:
                    sp.wait_ge(w_lo, last_half(before, m, at_i).val(1, 1))

            def load(T, slot, dst, src):
                sp.dma_start(dst, src).then_inc(landed[slot], 16)

            def stream(ph, source):
                def body(i, first):
                    for n, b in enumerate(ph.body):
                        T = At(ph.T0 + n, ph.tpi, i)
                        slot = n % 4
                        reuse(ph, n, i, first)
                        if b[0] == "a":
                            column = At(ph.A0, 1, i).val(NW)
                            src = t["ada_w_2"].rearrange("(k p) n -> p k n", p=P)[
                                :, 4 * b[1]:4 * b[1] + 4, bass.ds(column, NW)]
                            load(T, slot, raw[:, slot], src)
                        else:
                            source(i, T, slot, *b[1:])
                if ph.cpi == 3:
                    for i in range(ph.iters):
                        body(i, i == 0)
                else:
                    run(sp, ph, body)
                tail[0] = ph

            def chunked(w, column):
                wv = w.rearrange("(k p) n -> p k n", p=P)

                def source(i, T, slot, j, tt, k0, nk):
                    load(T, slot, raw[:, slot, 0:nk], wv[:, k0:k0 + nk, bass.ds(column(i, j), NW)])
                return source

            def rows(w, kf):
                def source(i, T, slot, j, tt, k0, nk):
                    start = At(tt, 4, i).val(P)
                    load(T, slot, raw[:, slot].rearrange("p a n -> p (a n)"), w[bass.ds(start, P), :])
                return source

            def lin(base, per_i, per_j):
                return lambda i, j: i * per_i + (base + j * per_j)

            stream(PH["mem"], chunked(t["w_mem_kv"], lin(0, 2 * NW, NW)))
            stream(PH["qkv"], chunked(t["w_in"], lin(0, 2 * NW, NW)))
            stream(PH["gates"], chunked(t["w_in"], lin(4096, 2 * NW, NW)))
            wa = t["w_br_a"].rearrange("(k p) n -> p k n", p=P)
            wb = t["w_br_b"].rearrange("(k p) n -> p k n", p=P)
            wc = t["w_br_c"].rearrange("(k p) n -> p k n", p=P)

            def branch(i, T, slot, j, tt, k0, nk):
                w, base = ((wa, 0), (wb, 2), (wc, 8))[j]
                load(T, slot, raw[:, slot, 0:nk], w[:, k0 - base:k0 - base + nk, i * NW:(i + 1) * NW])
            stream(PH["branch"], branch)
            stream(PH["w_o"], chunked(t["w_o"], lin(0, 2 * NW, NW)))
            stream(PH["ffn_in"], chunked(t["w_ffn_in"], lin(0, NW, FF1)))
            stream(PH["ffn_out"], rows(t["w_ffn_out"], KF1))
            w2 = t["w_in_2"]
            stream(PH["q2"], chunked(w2, lin(0, 2 * NW, NW)))
            stream(PH["kv2"], chunked(w2, lin(2048, 2 * NW, NW)))
            w2v = w2.rearrange("(k p) n -> p k n", p=P)

            def g48(i, T, slot, j, tt, k0, nk):
                load(T, slot, raw[:, slot, :, 0:48], w2v[:, k0:k0 + nk, 5120:5168])
            stream(PH["g48"], g48)
            stream(PH["lru_in"], chunked(w2, lin(5168, 2 * NW, NW)))
            sp.wait_ge(sem("cmp_hid"), 2)
            stream(PH["gates2"], chunked(w2, lin(9264, 2 * NW, NW)))
            stream(PH["proj_a"], chunked(t["proj_a_2"], lin(0, 2 * NW, NW)))
            stream(PH["proj_b"], chunked(t["proj_b_2"], lin(0, 2 * NW, NW)))
            stream(PH["w_out"], chunked(t["w_out_2"], lin(0, 2 * NW, NW)))
            stream(PH["ffn_up"], chunked(t["ffn_up_2"], lin(0, NW, FF2)))
            stream(PH["ffn_down"], rows(t["ffn_down_2"], KF2))

        @block.gpsimd
        def _(gp):
            gp.dma_start(X[:, :, :], t["mem"].rearrange("(t p) n -> p t n", p=P)).then_inc(sem("mem_in"), 16)
            gp.dma_start(ident[:, :], t["identity"]).then_inc(sem("ident_in"), 16)
            gp.dma_start(cols[:, :], t["vectors"]).then_inc(sem("cols_in"), 16)
            gp.dma_start(at(32, 6)[0:32], t["rel_bias"]).then_inc(sem("bias_in"), 16)
            gp.dma_start(at(33, 512)[0:32], t["one_hot"]).then_inc(sem("bias_in"), 16)
            gp.memset(zero1, 0.0).then_inc(sem("small_set"), 1)
            gp.memset(one1, 1.0).then_inc(sem("small_set"), 1)
            gp.memset(gq, 1.0).then_inc(sem("small_set"), 1)
            gp.dma_start(at(36, 6 * S), t["masks_a"]).then_inc(sem("mask_in"), 16)
            gp.wait_ge(sem("turned"), 4)
            gp.wait_ge(sem("norm_squares"), 8)
            gp.dma_start(X[:, :, :], t["x"].rearrange("(t p) n -> p t n", p=P)).then_inc(sem("x_in"), 16)
            for h in range(6):
                gp.wait_ge(sem("bias_row"), h + 1)
                gp.dma_start(bias_dram[h], at(16 + 2 * h, 512)).then_inc(sem("bias_out"), 16)
            gp.wait_ge(sem("bias_out"), 16 * 6)
            for h in range(6):
                g, j = h // 2, h % 2
                for tt in range(NT):
                    src = bass.AP(tensor=bias_dram.tensor, offset=h * P * 512 + 255 - tt * P, ap=[[511, P], [1, S]])
                    gp.dma_start(BI[:, j, tt, g, :], src).then_inc(sem("bias_back"), 16)
            if stop < 3:
                return
            def ada_rows(name):
                ph = PH[name]
                _, ada_row, ada_brow = ada_place(name)

                if name == "qkv":
                    gp.wait_ge(xl_ready, READY["qkv"])
                for a in range(ph.A0, ph.A0 + ph.iters):
                    gp.dma_start(ada_brow[0:1], t["ada_b_2"][:, NW * a:NW * a + NW]).then_inc(ada_b_in, 16)
                    gp.wait_ge(ada_rowed, a + 1)
                    gp.dma_start(mod_dram[NW * a:NW * a + NW].unsqueeze(0), ada_row[0:1]).then_inc(ada_stored, 16)
                    gp.wait_ge(ada_stored, 16 * a + 16)
                    if a == 5 * D // NW - 1:
                        for n, part in enumerate((1, 0, 4, 3)):
                            gp.dma_start(at(88, P)[16 * n:16 * n + 16], mod_dram[part * D:(part + 1) * D].rearrange(
                                "(k p) -> k p", p=P)).then_inc(sem("mod_in"), 16)
            ada_rows("mem")
            gp.wait_ge(sem("turned"), 8)
            gp.wait_ge(sem("norm_squares"), 16)
            gp.dma_start(X[:, 0, 0:256], t["rope"]).then_inc(sem("rope_in"), 16)
            gp.dma_start(X[:, 0, 256:384], t["g_qb"].partition_broadcast(P)).then_inc(sem("rope_in"), 16)
            gp.dma_start(X[:, 0, 384:512], t["g_kb"].partition_broadcast(P)).then_inc(sem("rope_in"), 16)
            ada_rows("qkv")
            if stop < 6:
                return
            gp.wait_ge(sem("attn1_out"), 12)
            ada_rows("gates")
            gp.dma_start(X[:, :, :], t["x"].rearrange("(t p) n -> p t n", p=P)).then_inc(sem("x_again"), 16)
            ada_rows("w_o")
            ada_rows("ffn_in")
            if stop < 10:
                return
            gp.wait_ge(sem("x2_ready"), 4)
            gp.dma_start(x_dram, X[:, :, :].rearrange("p t n -> p (t n)")).then_inc(sem("x_away"), 16)
            gp.wait_ge(sem("x_away"), 16)
            gp.wait_ge(sem("turned"), 4 * TURN[3] + 4)
            gp.wait_ge(sem("norm_squares"), 8 * 4)
            gp.dma_start(X[:, 0, :].rearrange("p (n e) -> p n e", n=16),
                         t["lru_wa_2"].rearrange("n d e -> d n e")).then_inc(sem("lru_w_in"), 16)
            gp.dma_start(X[:, 1, :].rearrange("p (n e) -> p n e", n=16),
                         t["lru_wi_2"].rearrange("n d e -> d n e")).then_inc(sem("lru_w_in"), 16)
            gp.wait_ge(w_lo, PH["gates2"].H0)
            for n, (w1, w2) in enumerate((("cmp_w1_k_2", "cmp_w2_k_2"), ("cmp_w1_v_2", "cmp_w2_v_2"))):
                gp.dma_start(W1[:, n].rearrange("p (l e) -> p l e", l=32), t[w1].rearrange("l d e -> d l e")).then_inc(sem(f"cmp_in{n}"), 16)
                gp.dma_start(CMP_W2[:, n], t[w2]).then_inc(sem("cmp2_in"), 16)
            gp.wait_ge(sem("lru_gates"), 16)
            gp.dma_start(X[:, 0, 0:2 * 527], t["masks_2"]).then_inc(sem("mask2_in"), 16)
            if stop < 14:
                return
            gp.wait_ge(sem("attn2_out"), 16)
            gp.dma_start(X[:, :, :].rearrange("p t n -> p (t n)"), x_dram).then_inc(sem("x_back"), 16)
            gp.dma_start(at(80, D), mod_dram[2 * D:3 * D].partition_broadcast(P)).then_inc(sem("g1_in"), 16)
            gp.wait_ge(xl_ready, READY["ffn_up"])
            gp.dma_start(at(0, D), mod_dram[5 * D:6 * D].partition_broadcast(P)).then_inc(sem("g2_in"), 16)
            gp.dma_start(at(8, D), t["final_g_2"].partition_broadcast(P)).then_inc(sem("final_g_in"), 16)
            for tt in range(NT):
                gp.wait_ge(sem("final"), tt + 1)
                gp.dma_start(out[tt * P:(tt + 1) * P, :], XN[:, tt, :]).then_inc(sem("out_stored"), 16)
            gp.wait_ge(sem("out_stored"), 16 * NT)

        def halves(nk):
            a = (nk + 1) // 2
            return ((0, a), (a, nk))

        def half_at(ph, g, h, i):
            return At(ph.H0 + 2 * g + h, ph.hpi, i)

        def epilogue_of(ph, j, i, first):
            if j > 0:
                return (i, j - 1)
            return None if first else (i - 1, len(ph.chunks) - 1)

        def products(eng, ph, tile, epilogue, ada=None, straight=False, side=None, prepared=0, tail=None):
            def body(i, first):
                g = 0
                for n, b in enumerate(ph.body):
                    T = At(ph.T0 + n, ph.tpi, i)
                    if b[0] == "a":
                        if ada:
                            ada("tile", i, (T, n % 4, b[1]))
                        continue
                    if not (first and g < prepared):
                        tile(i, T, n % 4, g, *b[1:])
                    g += 1
                    if ada and not first and g == 1:
                        ada("row", i - 1, None)
                    last = epilogue_of(ph, b[1], i, first) if b[2] == 0 else None
                    if last and epilogue:
                        epilogue(*last, *pair_of(ph, last[1], last[0]))
                    if side:
                        side(i, b[1], b[2])
            if straight:
                for i in range(ph.iters):
                    body(i, i == 0)
            else:
                run(eng, ph, body)
            end = (ph.iters - 1, len(ph.chunks) - 1)
            if tail:
                tail()
            if epilogue:
                epilogue(*end, *pair_of(ph, end[1], end[0]))
            if ada:
                ada("row", ph.iters - 1, None)

        def prepare(ph, tile, count, start):
            for g, (n, b) in list(enumerate([(n, b) for n, b in enumerate(ph.body) if b[0] == "g"]))[start:count]:
                tile(0, At(ph.T0 + n, ph.tpi, 0), n % 4, g, *b[1:])

        @block.scalar
        def _(act):
            def act_copy(out, in_, func=ACT.Copy, **kw):
                return nc.scalar.activation(out, in_, func, **kw)

            def tile(width=NW):
                def one(i, T, slot, g, j, tt, k0, nk):
                    ph = cur[0]
                    act.wait_ge(landed[slot], T.val(4, 16 - 4 * slot))
                    for h, (a, b) in enumerate(halves(nk)):
                        H = half_at(ph, g, h, i)
                        if not (isinstance(i, int) and H.val() < 4):
                            act.wait_ge(mm_half, H.val(1, -3))
                        act_copy(WH[:, (2 * slot_g(ph, g) + h) % 4, 0:b - a, 0:width],
                                 raw[:, slot, a:b, 0:width]).then_inc(w_hi, 1)
                return one
            cur = [None]

            def slot_g(ph, g):
                return (ph.H0 // 2 + g) % 2

            def phase(name, epilogue, straight=False, width=NW, side=None, prepared=0, tail=None):
                cur[0] = PH[name]
                products(act, PH[name], tile(width), epilogue, straight=straight, side=side, prepared=prepared, tail=tail)

            def ahead(name, count, start=0):
                now, cur[0] = cur[0], PH[name]
                prepare(PH[name], tile(), count, start)
                cur[0] = now

            done = [0]

            def squares(c):
                for tt in range(NT):
                    if done[0] >= 2:
                        act.wait_ge(sem("norm_squares"), done[0] - 1)
                    done[0] += 1
                    act_copy(junk[:, tt], X[:, tt, NW * c:NW * c + NW], ACT.Square,
                             accum_out=stat[:, 4 * tt + c:4 * tt + c + 1]).then_inc(sem("norm_squares"), 1)

            def root(n):
                act.wait_ge(sem("norm_mean"), n + 1)
                act_copy(stat[:, 10:12], stat[:, 8:10], ACT.Sqrt).then_inc(sem("norm_root"), 1)

            def round_acts(name, done=None, base=0, src=XF, groups=range(4)):
                act.wait_ge(mm_half, PH[name].H0)
                for g in groups:
                    if done:
                        act.wait_ge(done, base + g + 1)
                    act_copy(XH[:, 4 * g:4 * g + 4], src[:, 4 * g:4 * g + 4]).then_inc(xh_ready, 1)

            act.wait_ge(sem("cols_in"), 16)
            act_copy(cact, col("c_2"), ACT.Silu).then_inc(sem("c_ready"), 1)
            act.wait_ge(sem("mem_in"), 16)
            for c in range(4):
                squares(c)
            ahead("mem", 1)
            root(0)
            for h in range(6):
                act.wait_ge(sem("bias_mm"), h + 1)
                act_copy(at(16 + 2 * h, 512), acc[h % 2][:, h // 2 % 2, :]).then_inc(sem("bias_row"), 1)
            for g in range(4):
                act.wait_ge(sem("acts"), g + 1)
                act_copy(XH[:, 4 * g:4 * g + 4], XF[:, 4 * g:4 * g + 4]).then_inc(xh_ready, 1)
            if stop < 2:
                return

            def to_tokens(dst):
                def epilogue(i, j, p, used):
                    act.wait_ge(mm_half, chunk_done(cur[0], j, i))
                    act_copy(dst(i, j, 0), acc[p][:, 0, :]).then_inc(acc_used[p], 1)
                return epilogue
            if stop < 3:
                return

            def x_squares(i, j, t):
                if j == 1:
                    if t == 0:
                        act.wait_ge(sem("x_in"), 16)
                    squares(t)
            phase("mem", to_tokens(lambda i, j, tt: (KC, VC)[j][:, tt, :]), straight=True, side=x_squares, prepared=1, tail=lambda: ahead("qkv", 1))
            root(1)
            round_acts("qkv", sem("acts"), 4)
            if stop < 5:
                return
            def heads_root(s):
                act.wait_ge(sem("heads_mean"), s + 1)
                n, h0 = HEADS[s][1].shape[2] // HD, HEADS[s][2]
                act_copy(HEAD_STATS[:, :, h0:h0 + n], HEAD_STATS[:, :, h0:h0 + n], ACT.Sqrt).then_inc(sem("heads_root"), 1)

            def heads_side(i, j, t):
                for s, (done_at, _, _) in enumerate(HEADS):
                    if (done_at + 1, 1) == (2 * i + j, t):
                        heads_root(s)
            phase("qkv", to_tokens(lambda i, j, tt: Z[:, tt, NW * (2 * i + j):NW * (2 * i + j) + NW]), straight=True,
                  side=heads_side, prepared=1)
            heads_root(6)
            ahead("gates", 1)

            def exps1(job):
                n, probs = (768 if job < 2 else 256), probs1(job)
                if job >= 4:
                    act.wait_ge(sem("attn1_turned"), job - 2 if job > 4 else 1)
                act.wait_ge(sem("attn1_max"), job + 1)
                for tt in range(NT):
                    st = 2 * (job % 3) + tt
                    src = probs[:, tt] if job < 2 else acc[tt][:, 0, 0:256]
                    act_copy(probs[:, tt], src, ACT.Exp, bias=amax1[:, st:st + 1],
                             accum_out=asum1[:, st:st + 1]).then_inc(sem("attn1_exp"), 1)

            exps1(0)
            exps1(1)
            for job in range(12):
                act.wait_ge(sem("attn1_turned"), job + 1)
                if job >= 2:
                    act.wait_ge(sem("attn1_mm"), job - 1)
                blocks = 6 if job < 2 else 2
                act_copy(PT1[:, job % 2, 0:min(blocks, 4), :], acc[2][:, :, :].rearrange("p a (b s) -> p (a b) s", b=2)[:, 0:min(blocks, 4)]).then_inc(sem("attn1_pt"), 1)
                if blocks > 4:
                    act_copy(PT1[:, job % 2, 4:6, :], acc[3][:, 0, :].rearrange("p (b s) -> p b s", b=2)).then_inc(sem("attn1_pt"), 1)
                if job + 2 < 12:
                    exps1(job + 2)
            act.wait_ge(sem("attn1_out"), 12)
            if stop < 7:
                return

            def gates(dst, width):
                def epilogue(i, j, p, used):
                    act.wait_ge(mm_half, chunk_done(cur[0], j, i))
                    for tt in range(NT):
                        act_copy(dst[:, tt, bass.ds(i * (2 * NW) + j * NW, NW)], acc[p][:, tt, :],
                                 ACT.Sigmoid).then_inc(acc_used[p], 1)
                return epilogue
            phase("gates", gates(SG, 6144), prepared=1, tail=lambda: [ahead("branch", 1), round_acts("branch", groups=range(3))])
            phase("branch", None, straight=True, prepared=1,
                  tail=lambda: [ahead("w_o", 1), round_acts("w_o", sem("xf_filled"), 4 * TURN["m1"], groups=range(3))])
            round_acts("w_o", sem("xf_filled"), 4 * TURN["m1"], groups=(3,))

            def residual_squares(i, j, t):
                c = 2 * i + j - 1
                if t == 1 and c >= 0:
                    p = (cur[0].C0 + c) % 2
                    act.wait_ge(acc_used[p], 2 * ((cur[0].C0 + c) // 2 + 1))
                    if cur[0].name == "w_out":
                        act.wait_ge(sem("x3_ready"), c + 1)
                    squares(c)

            def last_squares():
                residual_squares(2, 0, 1)
            phase("w_o", None, straight=True, side=residual_squares, prepared=1, tail=lambda: ahead("ffn_in", 1))
            last_squares()
            if stop < 9:
                return
            root(2)
            round_acts("ffn_in", sem("acts"), 8)

            def used_before(ph, i):
                return pair_of(ph, 1, i)[1]

            def silu_gate(func, src_of, guard):
                def epilogue(i, j, p, used):
                    if j == 1:
                        return
                    act.wait_ge(mm_half, chunk_done(cur[0], j, i))
                    act.wait_ge(acc_used[1 - p], used_before(cur[0], i).val(2, 0))
                    act_copy(GT[:, 0], acc[p][:, :, :].rearrange("p a (b s) -> p (a b) s", b=2), func).then_inc(acc_used[p], 2)
                return epilogue
            def k_weights(ph, j, i):
                H = At(ph.H0 + 2 * j, 8, i)
                act.wait_ge(landed[j], At(ph.T0 + j, 4, i).val(4, 16 - 4 * j))
                for h in range(2):
                    act.wait_ge(mm_half, H.val(1, h - 3))
                    act_copy(WH[:, (ph.H0 + 2 * j + h) % 4], raw[:, j, 2 * h:2 * h + 2]).then_inc(w_hi, 1)
            phase("ffn_in", silu_gate(ACT.Silu, None, None), prepared=1, tail=lambda: k_weights(PH["ffn_out"], 0, 0))

            def k_outer(name):
                ph = PH[name]

                def body(i, first):
                    for j in range(4):
                        H = At(ph.H0 + 2 * j, 8, i)
                        act.wait_ge(mm_half, ph.H0 if first else H.val(1, -6))
                        act_copy(XH[:, j:j + 1], AT[:, bass.ds(i * 4 + j, 1), :]).then_inc(sem("hidden_rounded"), 1)
                        if not (first and j == 0):
                            k_weights(ph, j, i)
                    if first:
                        for p in range(2):
                            act.wait_ge(acc_used[p], 2 * c_end(before[name], p))
                for p in range(2):
                    act.wait_ge(acc_used[p], 2 * c_end(before[name], p) - 2)
                run(act, ph, body)
            before = {"ffn_out": "ffn_in", "ffn_down": "ffn_up"}
            k_outer("ffn_out")
            if stop < 11:
                return
            ahead("q2", 1)
            for c in range(4):
                act.wait_ge(sem("x2_ready"), c + 1)
                squares(c)
            root(3)
            round_acts("q2", sem("acts"), 12)

            def to_features(dst, scale=1.0):
                def epilogue(i, j, p, used):
                    act.wait_ge(mm_half, chunk_done(cur[0], j, i))
                    act_copy(dst(i, j, 0), acc[p][:, 0, :].rearrange("p (b s) -> p b s", b=2), scale=scale).then_inc(acc_used[p], 1)
                return epilogue
            phase("q2", to_features(lambda i, j, b: Q2[:, bass.ds(i * 8 + (4 * j + 2 * b), 2), :], SCALE), prepared=1)
            act.wait_ge(ada_stored, 16 * ADA_CHUNKS)
            kv_dst = [(KC2, 0), (VC2, 0), (KS2, 0), (VS2, 1), (KW2, 0), (VW2, 1)]

            def kv_epilogue(i, j, p, used):
                dst, token = kv_dst[2 * i + j]
                if token:
                    to_tokens(lambda i, j, tt: dst[:, tt, :])(i, j, p, used)
                else:
                    to_features(lambda i, j, b: dst[:, 2 * b:2 * b + 2, :])(i, j, p, used)
            phase("kv2", kv_epilogue, straight=True)

            def g48_epilogue(i, j, p, used):
                act.wait_ge(mm_half, chunk_done(cur[0], j, i))
                act_copy(G48[:, :, :], acc[p][:, :, 0:48], ACT.Sigmoid).then_inc(acc_used[p], 2)
            phase("g48", g48_epilogue, width=48)
            LXY = XT(32, 32)
            phase("lru_in", to_features(lambda i, j, b: LXY[:, bass.ds(i * 8 + (4 * j + 2 * b), 2), :]))
            if stop < 12:
                return
            act_copy(lamc[:, 0:16], col("lru_lambda_2"), ACT.Abs).then_inc(sem("lam_abs"), 1)
            act.wait_ge(sem("lam_abs"), 1)
            act_copy(lamc[:, 0:16], lamc[:, 0:16], ACT.Exp, scale=-1.0).then_inc(sem("lam_exp"), 1)
            act.wait_ge(sem("lam_exp"), 1)
            act_copy(lamc[:, 0:16], lamc[:, 0:16], ACT.Ln, bias=1.0).then_inc(sem("lam_log"), 1)
            act.wait_ge(sem("lam_ready"), 1)
            for p in range(2):
                act.wait_ge(acc_used[p], 2 * c_end("lru_in", p))
            for b in range(4):
                act_copy(LY[:, 4 * b:4 * b + 4], LY[:, 4 * b:4 * b + 4], ACT.Gelu_apprx_tanh).then_inc(sem("lru_gelu"), 1)

            def gate_sigmoids(b):
                if b:
                    act.wait_ge(sem("lru_a"), 2 * b)
                if b >= 2:
                    act.wait_ge(sem("lru_h"), 4 * (b - 1))
                for n in range(4):
                    k = 4 * b + n
                    act.wait_ge(sem("lru_gates"), k + 1)
                    act_copy(RT[:, n], acc[2 + k % 2][:, 0, 0:S], ACT.Sigmoid, bias=col("lru_ba_2")[:, k:k + 1]).then_inc(sem("lru_r"), 1)
                    act_copy(IT2[b % 2][:, n], acc[2 + k % 2][:, 0, S:2 * S], ACT.Sigmoid, bias=col("lru_bi_2")[:, k:k + 1]).then_inc(sem("lru_r"), 1)

            gate_sigmoids(0)
            for b in range(4):
                act.wait_ge(sem("lru_scaled"), b + 1)
                if b:
                    act.wait_ge(sem("lru_b"), b)
                act_copy(TT, RT, ACT.Tanh).then_inc(sem("lru_tanh"), 1)
                act_copy(LX[:, 4 * b:4 * b + 4], RT, ACT.Exp, scale=-1.0).then_inc(sem("lru_a"), 1)
                act.wait_ge(sem("lru_iu"), b + 1)
                act_copy(UT2[b % 2], RT, ACT.Exp, scale=-2.0).then_inc(sem("lru_a"), 1)
                act.wait_ge(sem("lru_one_minus"), b + 1)
                act_copy(TT, TT, ACT.Sqrt).then_inc(sem("lru_sqrt"), 1)
                if b < 3:
                    gate_sigmoids(b + 1)
            for n in range(2):
                act.wait_ge(sem("cmp_hid"), n + 1)
                act_copy(CMP_HID[:, n, 0:60], acc[2 + n][:, 1, 0:60], ACT.Gelu_apprx_tanh).then_inc(sem("cmp_gelu"), 1)
            act.wait_ge(sem("cmp_done"), 1)
            act_copy(KCMP[:, 0:60], acc[2][:, 1, 64:124]).then_inc(sem("cmp_kept"), 1)
            act.wait_ge(sem("cmp_done"), 2)
            act_copy(VCMP[0:15, :], acc[3][0:15, 1, :]).then_inc(sem("cmp_kept"), 1)
            if stop < 14:
                return
            def exps2(job):
                bb = job % 3
                act.wait_ge(sem("attn2_max"), job + 1)
                for tt in range(NT):
                    for seg, (lo, hi) in enumerate(SEG):
                        st = 12 * bb + 3 * tt + seg
                        act_copy(P2[:, bb, tt, lo:hi], P2[:, bb, tt, lo:hi], ACT.Exp, bias=smx[:, st:st + 1],
                                 accum_out=smx[:, st + 6:st + 7]).then_inc(sem("attn2_exp"), 1)

            exps2(0)
            exps2(1)
            for job in range(16):
                bb = job % 2
                act.wait_ge(sem("attn2_turned"), job + 1)
                if job >= 2:
                    act.wait_ge(sem("attn2_mm"), job - 1)
                act_copy(PT2[:, bb], acc[2][:, :, :].rearrange("p a (b s) -> p (a b) s", b=2)).then_inc(sem("attn2_pt"), 1)
                act_copy(PC2[0:15, bb], acc[3][0:15, 0, 0:S]).then_inc(sem("attn2_pt"), 1)
                if job + 2 < 16:
                    exps2(job + 2)
                if job == 11:
                    ahead("gates2", 2)
            act.wait_ge(sem("attn2_out"), 16)
            if stop < 15:
                return
            phase("gates2", gates(SG2, 4096), prepared=2, tail=lambda: [ahead("proj_a", 1), round_acts("proj_a", src=Q2)])
            phase("proj_a", None, prepared=1, tail=lambda: [ahead("proj_b", 1), round_acts("proj_b", src=LX)])
            phase("proj_b", None, prepared=1,
                  tail=lambda: [ahead("w_out", 1), round_acts("w_out", sem("xf_filled"), 4 * TURN["m2"], groups=range(3))])
            round_acts("w_out", sem("xf_filled"), 4 * TURN["m2"], groups=(3,))
            phase("w_out", None, straight=True, side=residual_squares, prepared=1, tail=lambda: ahead("ffn_up", 1))
            last_squares()
            if stop < 16:
                return
            root(4)
            round_acts("ffn_up", sem("acts"), 16)

            def gelu_gate(i, j, t):
                if (j, t) == (1, 2):
                    p, used = pair_of(cur[0], 0, i)
                    act.wait_ge(acc_used[p], used.val(2, 2))
                    act_copy(GT[:, 0], CV[:, 0], ACT.Gelu_apprx_tanh).then_inc(sem("gate_ready"), 1)
            phase("ffn_up", None, side=gelu_gate, prepared=1, tail=lambda: k_weights(PH["ffn_down"], 0, 0))
            if stop < 17:
                return
            k_outer("ffn_down")
            for tt in range(NT):
                act.wait_ge(sem("x4_ready"), 2 * tt + 2)
                act_copy(at(32 + 8 * tt, D), X[:, tt, :], ACT.Square, accum_out=stat[:, tt:tt + 1]).then_inc(sem("final_squares"), 1)
            act.wait_ge(sem("final_mean"), 1)
            act_copy(stat[:, 4:6], stat[:, 2:4], ACT.Sqrt).then_inc(sem("final_root"), 1)

        @block.vector
        def _(dve):
            v = nc.vector
            cur = [None]

            def tile(width=NW):
                def one(i, T, slot, g, j, tt, k0, nk):
                    ph = cur[0]
                    last = None
                    for h, (a, b) in enumerate(halves(nk)):
                        H = half_at(ph, g, h, i)
                        dve.wait_ge(w_hi, H.val(1, 1))
                        ring = (2 * ((ph.H0 // 2 + g) % 2) + h) % 4
                        last = v.tensor_tensor(WL[:, ring, 0:b - a, 0:width], raw[:, slot, a:b, 0:width],
                                               WH[:, ring, 0:b - a, 0:width].bitcast(F32), ALU.subtract)
                        last.then_inc(w_lo, 1)
                return one

            def ada(what, i, arg):
                ph = cur[0]
                ada_acc, ada_row, ada_brow = ada_place(ph.name)
                a = At(ph.A0, 1, i)
                if what == "row":
                    dve.wait_ge(ada_red, a.val(1, 1))
                    dve.wait_ge(ada_b_in, a.val(16, 16))
                    v.tensor_tensor(ada_row[0:1], acc[2][0:1, 0, :], ada_brow[0:1], ALU.add).then_inc(ada_rowed, 1)
                    return
                T, slot, q = arg
                dve.wait_ge(landed[slot], T.val(4, 16 - 4 * slot))
                for kk in range(4):
                    n = 4 * q + kk
                    count = a.val(16, n)
                    if n < 2:
                        if not (isinstance(i, int) and a.val() == 0):
                            dve.wait_ge(ada_red, a.val(1, 0))
                        v.tensor_scalar(ada_acc[:, n % 2], raw[:, slot, kk], cact[:, n:n + 1], None, ALU.mult).then_inc(ada_mac, 1)
                    else:
                        dve.wait_ge(ada_mac, a.val(16, n - 1))
                        v.scalar_tensor_tensor(ada_acc[:, n % 2], raw[:, slot, kk], cact[:, n:n + 1], ada_acc[:, n % 2],
                                               ALU.mult, ALU.add).then_inc(ada_mac, 1)

            def phase(name, epilogue, straight=False, width=NW, side=None, prepared=0, tail=None):
                cur[0] = PH[name]
                products(dve, PH[name], tile(width), epilogue, ada=ada if PH[name].ada else None, straight=straight,
                         side=side, prepared=prepared, tail=tail)

            def ahead(name, count, start=0):
                now, cur[0] = cur[0], PH[name]
                prepare(PH[name], tile(), count, start)
                cur[0] = now

            def rest(ready, g, src=XF):
                dve.wait_ge(xh_ready, ready + g + 1)
                v.tensor_tensor(XL[:, 4 * g:4 * g + 4], src[:, 4 * g:4 * g + 4], XH[:, 4 * g:4 * g + 4].bitcast(F32),
                                ALU.subtract).then_inc(xl_ready, 1)

            def fill(n, g, gain=None):
                dve.wait_ge(sem("turned"), 4 * TURN[n] + g + 1)
                src = acc[TURN_PAIRS[n][g % 2]][:, :, :].rearrange("p a (b s) -> p (a b) s", b=2)
                if gain is None:
                    v.tensor_copy(XF[:, 4 * g:4 * g + 4], src).then_inc(sem("xf_filled"), 1)
                else:
                    v.tensor_tensor(XF[:, 4 * g:4 * g + 4], src, bc(gain[:, 4 * g:4 * g + 4], [P, 4, S]), ALU.mult).then_inc(sem("xf_filled"), 1)

            def norm_mean(n):
                dve.wait_ge(sem("norm_squares"), 8 * (n + 1))
                v.tensor_reduce(stat[:, 12:14], stat[:, 0:8].rearrange("p (t c) -> p t c", t=NT), AX.X, ALU.add).then_inc(sem("norm_sum"), 1)
                dve.wait_ge(sem("norm_sum"), n + 1)
                v.tensor_scalar(stat[:, 8:10], stat[:, 12:14], 1.0 / D, EPS, ALU.mult, ALU.add).then_inc(sem("norm_mean"), 1)

            def norm_tail(n, ready, shift=None):
                dve.wait_ge(sem("norm_root"), n + 1)
                v.reciprocal(stat[:, 12:14], stat[:, 10:12]).then_inc(sem("norm_inverse"), 1)
                dve.wait_ge(sem("norm_inverse"), n + 1)
                v.tensor_copy(root_wide, bc(stat[:, 12:14], [P, NT, P])).then_inc(sem("norm_rows"), 1)
                dve.wait_ge(sem("norm_spread"), n + 1)
                by_token = acc[2][:, 1, 0:S].unsqueeze(1).broadcast_to([P, 4, S])
                for g in range(4):
                    x = XF[:, 4 * g:4 * g + 4]
                    dve.wait_ge(sem("xf_filled"), 4 * TURN[n] + g + 1)
                    if shift is None:
                        v.tensor_tensor(x, x, by_token, ALU.mult).then_inc(sem("acts"), 1)
                    else:
                        v.tensor_tensor(x, x, by_token, ALU.mult).then_inc(sem("acts_scaled"), 1)
                        dve.wait_ge(sem("acts_scaled"), (4 if n == 4 else 0) + g + 1)
                        v.tensor_tensor(x, x, bc(shift[:, 4 * g:4 * g + 4], [P, 4, S]), ALU.add).then_inc(sem("acts"), 1)
                    if g:
                        rest(ready, g - 1)
                rest(ready, 3)

            dve.wait_ge(sem("bias_in"), 32)
            v.tensor_copy(at(76, 768)[0:32].rearrange("p (h q) -> p h q", h=6), bc(at(32, 6)[0:32], [32, 6, P])).then_inc(sem("bias_wide"), 1)
            dve.wait_ge(sem("cols_in"), 16)
            for g in range(4):
                fill(0, g, col("g_mem"))
            norm_mean(0)
            ahead("mem", 1)
            norm_tail(0, 0)
            if stop < 2:
                return
            dve.wait_ge(sem("small_set"), 3)
            dve.wait_ge(sem("cols_in"), 16)
            for dst, name, n, s in ((0, "g_qa", 6, SCALE), (6, "g_ka", 6, 1.0), (20, "g_qc", 4, SCALE), (24, "g_kc", 4, 1.0)):
                v.tensor_scalar(gq[:, dst:dst + n], col(name).broadcast_to([P, n]), s, None, ALU.mult).then_inc(sem("head_gain"), 1)
            v.tensor_scalar(gq[:, 12:18], one1.broadcast_to([P, 6]), SCALE, None, ALU.mult).then_inc(sem("head_gain"), 1)

            def bias_masks():
                dve.wait_ge(sem("bias_back"), 16 * 12)
                dve.wait_ge(sem("mask_in"), 16)
                mk = at(36, 6 * S).rearrange("p (t g s) -> p t g s", t=2, g=3)
                for j in range(2):
                    for tt in range(NT):
                        v.tensor_tensor(BI[:, j, tt], BI[:, j, tt], mk[:, tt], ALU.add).then_inc(sem("bias_ready"), 1)

            def to_tokens(dst):
                def epilogue(i, j, p, used):
                    dve.wait_ge(mm_half, chunk_done(cur[0], j, i))
                    v.tensor_copy(dst(i, j, 1), acc[p][:, 1, :]).then_inc(acc_used[p], 1)
                return epilogue
            if stop < 3:
                return
            dve.wait_ge(sem("c_ready"), 1)
            dve.wait_ge(xl_ready, 4)
            def mem_side(i, j, t):
                n = 4 * j + t
                if n in (3, 5, 7):
                    fill(1, (n - 3) // 2, col("g_mix"))
                if n == 6:
                    bias_masks()
            phase("mem", to_tokens(lambda i, j, tt: (KC, VC)[j][:, tt, :]), straight=True, prepared=1, side=mem_side,
                  tail=lambda: ahead("qkv", 1))
            fill(1, 3, col("g_mix"))
            if stop < 4:
                return

            norm_mean(1)
            norm_tail(1, READY["mem"])
            if stop < 5:
                return
            def by_head(rows):
                return rows.rearrange("p t (h d) -> p t h d", d=HD)

            def heads_mean(s):
                done_at, rows, h0 = HEADS[s]
                z = by_head(rows)
                n = rows.shape[2] // HD
                if s:
                    c = PH["qkv"].C0 + done_at
                    dve.wait_ge(acc_used[c % 2], 2 * (c // 2 + 1))
                    dve.wait_ge(sem("hd_sum"), s)
                sq = X[:, 1, 0:2 * n * HD].rearrange("p (t h d) -> p t h d", t=NT, h=n)
                v.tensor_tensor(sq, z, z, ALU.mult).then_inc(sem("hd_sq"), 1)
                dve.wait_ge(sem("hd_sq"), s + 1)
                stats = HEAD_STATS[:, :, h0:h0 + n]
                v.tensor_reduce(stats, sq, AX.X, ALU.add).then_inc(sem("hd_sum"), 1)
                dve.wait_ge(sem("hd_sum"), s + 1)
                v.tensor_scalar(stats, stats, 1.0 / HD, EPS, ALU.mult, ALU.add).then_inc(sem("heads_mean"), 1)

            def heads_scale(s):
                _, rows, h0 = HEADS[s]
                n = rows.shape[2] // HD
                stats = HEAD_STATS[:, :, h0:h0 + n]
                dve.wait_ge(sem("heads_root"), s + 1)
                v.reciprocal(stats, stats).then_inc(sem("heads_inverse"), 1)
                dve.wait_ge(sem("heads_inverse"), s + 1)
                z = by_head(rows)
                v.tensor_tensor(z, z, stats.unsqueeze(3).broadcast_to([P, NT, n, HD]), ALU.mult).then_inc(sem("heads_scaled"), 1)

            def rope_gain(s, gain):
                z = by_head(HEADS[s][1])
                n = HEADS[s][1].shape[2] // HD
                dve.wait_ge(sem("heads_scaled"), s + 1)
                dve.wait_ge(sem("rope_in"), 48)
                v.tensor_tensor(z, z, gain.unsqueeze(1).unsqueeze(1).broadcast_to([P, NT, n, HD]), ALU.mult).then_inc(sem("rope_gain"), 1)

            def rope_heads(tt):
                rope = X[:, 0, 0:256].rearrange("p (t c f) -> p t c f", t=2, c=2)
                z = Z[:, tt, 2304:3328].rearrange("p (h f c) -> p c h f", h=8, c=2)
                x0, x1 = z[:, 0], z[:, 1]
                cs = rope[:, tt, 0].unsqueeze(1).broadcast_to([P, 8, 64])
                sn = rope[:, tt, 1].unsqueeze(1).broadcast_to([P, 8, 64])
                w = [X[:, 1, 512 * k:512 * k + 512].rearrange("p (h f) -> p h f", h=8) for k in range(4)]
                if tt:
                    dve.wait_ge(sem("roped"), 2)
                else:
                    dve.wait_ge(sem("rope_gain"), 2)
                for k, (a, b) in enumerate(((x0, cs), (x1, sn), (x0, sn), (x1, cs))):
                    v.tensor_tensor(w[k], a, b, ALU.mult).then_inc(sem("rope_part"), 1)
                dve.wait_ge(sem("rope_part"), 4 * tt + 4)
                v.tensor_tensor(x0, w[0], w[1], ALU.subtract).then_inc(sem("roped"), 1)
                v.tensor_tensor(x1, w[2], w[3], ALU.add).then_inc(sem("roped"), 1)

            def heads_fetch(n):
                g = HEAD_GROUPS[n]
                dve.wait_ge(sem("heads_turned"), n + 1)
                v.tensor_tensor(QK[:, 4 * g:4 * g + 4], acc[HEAD_PAIR[n]][:, :, :].rearrange("p a (b s) -> p (a b) s", b=2),
                                bc(gq[:, 4 * g:4 * g + 4], [P, 4, S]), ALU.mult).then_inc(sem("heads_ready"), 1)

            def heads_side(i, j, t):
                c = 2 * i + j
                for s, (done_at, _, _) in enumerate(HEADS):
                    if (done_at + 1, 0) == (c, t):
                        heads_mean(s)
                    if (done_at + 1, 2) == (c, t):
                        heads_scale(s)
                if t == 3 and 1 <= c <= 4:
                    if c == 1:
                        dve.wait_ge(ada_stored, 16)
                        dve.wait_ge(sem("head_gain"), 5)
                    heads_fetch(c - 1)
                if t == 3 and c in (6, 7):
                    rope_gain(c - 2, X[:, 0, 256:384] if c == 6 else X[:, 0, 384:512])
            phase("qkv", to_tokens(lambda i, j, tt: Z[:, tt, NW * (2 * i + j):NW * (2 * i + j) + NW]), straight=True,
                  side=heads_side, prepared=1)
            heads_mean(6)
            heads_scale(6)
            rope_heads(0)
            heads_fetch(4)
            rope_heads(1)
            heads_fetch(5)
            heads_fetch(6)
            dve.wait_ge(ada_stored, 16 * (PH["qkv"].A0 + PH["qkv"].iters))
            if stop < 6:
                return
            def finish1(job):
                b, probs = job % 3, probs1(job)
                dve.wait_ge(sem("attn1_exp"), 2 * job + 2)
                r = asum1[:, 2 * b:2 * b + 2]
                v.reciprocal(r, r).then_inc(sem("attn1_inverse"), 1)
                dve.wait_ge(sem("attn1_inverse"), job + 1)
                v.tensor_tensor(probs, probs, bc(r, [P, NT, 768 if job < 2 else 256]), ALU.mult).then_inc(sem("attn1_probs"), 1)

            def out1(job):
                dve.wait_ge(sem("attn1_mm"), job + 1)
                v.tensor_copy(XF[:, job], acc[3][:, 1, 0:S]).then_inc(sem("attn1_out"), 1)

            def top1(job):
                b = job % 3
                mx = amax1[:, 2 * b:2 * b + 2]
                for tt in range(NT):
                    u = 2 * job + tt
                    dve.wait_ge(sem("attn1_scores"), u + 1)
                    if job < 2:
                        sc = probs1(job)[:, tt]
                        v.tensor_tensor(sc, acc[tt][:, :, :].rearrange("p a s -> p (a s)")[:, 0:768],
                                        BI[:, job, tt].rearrange("p g s -> p (g s)"), ALU.add).then_inc(sem("attn1_biased"), 1)
                        dve.wait_ge(sem("attn1_biased"), u + 1)
                    else:
                        sc = acc[tt][:, 0, 0:256]
                    v.tensor_reduce(mx[:, tt:tt + 1], sc, AX.X, ALU.max).then_inc(sem("attn1_top"), 1)
                dve.wait_ge(sem("attn1_top"), 2 * job + 2)
                v.tensor_scalar(mx, mx, -1.0, None, ALU.mult).then_inc(sem("attn1_max"), 1)

            top1(0)
            top1(1)
            for job in range(12):
                if job == 6:
                    ahead("gates", 1)
                finish1(job)
                if job >= 2:
                    out1(job - 2)
                if job + 2 < 12:
                    top1(job + 2)
            out1(10)
            out1(11)
            if stop < 7:
                return
            phase("gates", None, prepared=1, tail=lambda: [ahead("branch", 1)] + [rest(READY["gates"], g) for g in range(3)])

            def branch_epilogue(i, j, p, used):
                dve.wait_ge(mm_half, chunk_done(cur[0], j, i))
                gate = SG[:, :, D * j + NW * i:D * j + NW * i + NW]
                dst = M[:, :, NW * i:NW * i + NW]
                if j == 0:
                    v.tensor_tensor(dst, acc[p][:, :, :], gate, ALU.mult).then_inc(acc_used[p], 2)
                    return
                v.tensor_tensor(gate, acc[p][:, :, :], gate, ALU.mult).then_inc(acc_used[p], 2)
                dve.wait_ge(acc_used[p], used.val(2, 2))
                v.tensor_tensor(dst, dst, gate, ALU.add).then_inc(sem("merging1"), 1)
                dve.wait_ge(sem("merging1"), 2 * i + j)
            def merged_fill(n):
                def side(i, j, t):
                    if i and (j, t) == (2, 0):
                        fill(n, i - 1)
                return side
            phase("branch", branch_epilogue, straight=True, prepared=1, side=merged_fill("m1"),
                  tail=lambda: [ahead("w_o", 1), rest(READY["branch"], 0)])
            fill("m1", 3)
            for g in range(1, 4):
                rest(READY["branch"], g)

            def residual(name, wait=None, gain=None):
                def epilogue(i, j, p, used):
                    dve.wait_ge(mm_half, chunk_done(cur[0], j, i))
                    x = X[:, :, bass.ds(i * (2 * NW) + j * NW, NW)]
                    if gain is not None:
                        tmp = at(88, 2 * NW).rearrange("p (t n) -> p t n", t=NT)
                        gb = gain(i, j)
                        if not (isinstance(i, int) and i == 0 and j == 0):
                            dve.wait_ge(sem(name), i * 2 + j)
                        v.tensor_tensor(tmp, acc[p][:, :, :], gb, ALU.mult).then_inc(acc_used[p], 2)
                        dve.wait_ge(acc_used[p], used.val(2, 2))
                        v.tensor_tensor(x, x, tmp, ALU.add).then_inc(sem(name), 1)
                        return
                    v.tensor_tensor(x, x, acc[p][:, :, :], ALU.add).then_inc(acc_used[p], 2)
                return epilogue
            dve.wait_ge(sem("x_again"), 16)
            def residual_fill(n, gain):
                def side(i, j, t):
                    c = 2 * i + j - 1
                    if t == 3 and c >= 0:
                        fill(n, c, gain)
                return side
            phase("w_o", residual("x1_ready"), straight=True, side=residual_fill(2, col("g_ffn")), prepared=1,
                  tail=lambda: ahead("ffn_in", 1))
            fill(2, 3, col("g_ffn"))
            if stop < 9:
                return
            norm_mean(2)
            norm_tail(2, READY["w_o"])

            def hidden(name, p, i, j, used):
                dve.wait_ge(mm_half, chunk_done(cur[0], j, i))
                src = acc[p][:, :, :].rearrange("p a (b s) -> p (a b) s", b=2)
                v.tensor_tensor(AT[:, bass.ds(i * 4, 4), :], GT[:, 0], src, ALU.mult).then_inc(acc_used[p], 2)

            def swiglu(i, j, p, used):
                if j == 0:
                    return
                dve.wait_ge(acc_used[1 - p], gate_uses(i).val(2, 2))
                hidden("hidden1", p, i, j, used)
            gate_uses = lambda i: pair_of(PH["ffn_in"], 0, i)[1]
            def k_weights(ph, j, i):
                for h in range(2):
                    ring = (ph.H0 + 2 * j + h) % 4
                    dve.wait_ge(w_hi, At(ph.H0 + 2 * j + h, 8, i).val(1, 1))
                    v.tensor_tensor(WL[:, ring], raw[:, j, 2 * h:2 * h + 2], WH[:, ring].bitcast(F32), ALU.subtract).then_inc(w_lo, 1)
            phase("ffn_in", swiglu, prepared=1, tail=lambda: k_weights(PH["ffn_out"], 0, 0))
            if stop < 10:
                return

            def k_outer(name, base):
                ph = PH[name]

                def body(i, first):
                    for j in range(4):
                        dve.wait_ge(sem("hidden_rounded"), At(base + j, 4, i).val(1, 1))
                        v.tensor_tensor(XL[:, j:j + 1], AT[:, bass.ds(i * 4 + j, 1), :], XH[:, j:j + 1].bitcast(F32), ALU.subtract).then_inc(sem("hidden_rest"), 1)
                        if not (first and j == 0):
                            k_weights(ph, j, i)
                run(dve, ph, body)

            dve.wait_ge(sem("mod_turned"), 1)
            v.tensor_copy(mod, acc[2][:, 1, 0:64]).then_inc(sem("mod_copied"), 1)
            dve.wait_ge(sem("mod_copied"), 1)
            for n, g in ((0, "norm1_g_2"), (2, "norm2_g_2")):
                m = mod[:, 16 * n:16 * n + 16]
                v.scalar_tensor_tensor(m, m, 1.0, col(g), ALU.add, ALU.mult).then_inc(sem("mod_ready"), 1)
            dve.wait_ge(sem("mod_ready"), 2)
            k_outer("ffn_out", 0)
            ahead("q2", 1)
            for n in range(4):
                dve.wait_ge(mm_half, PH["ffn_out"].H0 + PH["ffn_out"].hpi * PH["ffn_out"].iters)
                v.tensor_tensor(X[:, :, NW * n:NW * n + NW], X[:, :, NW * n:NW * n + NW], acc[n][:, :, :], ALU.add).then_inc(sem("x2_ready"), 1)
            if stop < 11:
                return
            for g in range(4):
                fill(3, g, mod[:, 0:16])
            norm_mean(3)
            norm_tail(3, READY["ffn_in"], mod[:, 16:32])

            def to_features(dst, scale=1.0):
                def epilogue(i, j, p, used):
                    dve.wait_ge(mm_half, chunk_done(cur[0], j, i))
                    src = acc[p][:, 1, :].rearrange("p (b s) -> p b s", b=2)
                    if scale != 1.0:
                        v.tensor_scalar(dst(i, j, 1), src, scale, None, ALU.mult).then_inc(acc_used[p], 1)
                    else:
                        v.tensor_copy(dst(i, j, 1), src).then_inc(acc_used[p], 1)
                return epilogue
            phase("q2", to_features(lambda i, j, b: Q2[:, bass.ds(i * 8 + (4 * j + 2 * b), 2), :], SCALE), prepared=1)
            dve.wait_ge(ada_stored, 16 * ADA_CHUNKS)
            kv_dst = [(KC2, 0), (VC2, 0), (KS2, 0), (VS2, 1), (KW2, 0), (VW2, 1)]

            def kv_epilogue(i, j, p, used):
                dst, token = kv_dst[2 * i + j]
                if token:
                    to_tokens(lambda i, j, tt: dst[:, tt, :])(i, j, p, used)
                else:
                    to_features(lambda i, j, b: dst[:, 2 * b:2 * b + 2, :])(i, j, p, used)
            phase("kv2", kv_epilogue, straight=True)
            phase("g48", None, width=48)
            LXY = XT(32, 32)
            phase("lru_in", to_features(lambda i, j, b: LXY[:, bass.ds(i * 8 + (4 * j + 2 * b), 2), :]))
            if stop < 12:
                return
            dve.wait_ge(acc_used[0], 2 * c_end("lru_in", 0))
            dve.wait_ge(acc_used[1], 2 * c_end("lru_in", 1))
            cw = col("lru_conv_w_2")

            def lru_conv(b):
                UT = UT2[b % 2]
                if b >= 2:
                    dve.wait_ge(sem("lru_out"), b - 1)
                for n in range(4):
                    k = 4 * b + n
                    v.tensor_scalar(UT[:, n], LX[:, k], cw[:, 48 + k:49 + k], col("lru_conv_b_2")[:, k:k + 1],
                                    ALU.mult, ALU.add).then_inc(sem("conv_tap"), 1)
                for tap in (1, 2, 3):
                    for n in range(4):
                        k = 4 * b + n
                        dve.wait_ge(sem("conv_tap"), 16 * b + 4 * (tap - 1) + n + 1)
                        v.scalar_tensor_tensor(UT[:, n, tap:S], LX[:, k, 0:S - tap], cw[:, 16 * (3 - tap) + k:16 * (3 - tap) + k + 1],
                                               UT[:, n, tap:S], ALU.mult, ALU.add).then_inc(sem("conv_tap"), 1)

            lru_conv(0)
            v.tensor_scalar(lamc[:, 16:32], col("lru_lambda_2"), 0.0, None, ALU.min).then_inc(sem("lam_min"), 1)
            dve.wait_ge(sem("lam_min"), 1)
            dve.wait_ge(sem("lam_log"), 1)
            v.tensor_tensor(lamc[:, 0:16], lamc[:, 0:16], lamc[:, 16:32], ALU.subtract).then_inc(sem("lam_sub"), 1)
            dve.wait_ge(sem("lam_sub"), 1)
            v.tensor_scalar(lamc[:, 0:16], lamc[:, 0:16], 8.0, None, ALU.mult).then_inc(sem("lam_ready"), 1)
            dve.wait_ge(sem("lam_ready"), 1)
            for b in range(4):
                IT, UT, AA = IT2[b % 2], UT2[b % 2], LX[:, 4 * b:4 * b + 4]
                dve.wait_ge(sem("lru_r"), 8 * b + 8)
                v.tensor_tensor(RT, RT, bc(lamc[:, 4 * b:4 * b + 4], [P, 4, S]), ALU.mult).then_inc(sem("lru_scaled"), 1)
                v.tensor_tensor(IT, IT, UT, ALU.mult).then_inc(sem("lru_iu"), 1)
                if b < 3:
                    lru_conv(b + 1)
                dve.wait_ge(sem("lru_tanh"), b + 1)
                dve.wait_ge(sem("lru_a"), 2 * b + 2)
                v.scalar_tensor_tensor(TT, UT, 1.0, TT, ALU.add, ALU.mult).then_inc(sem("lru_one_minus"), 1)
                dve.wait_ge(sem("lru_iu"), b + 1)
                dve.wait_ge(sem("lru_sqrt"), b + 1)
                v.tensor_tensor(IT, IT, TT, ALU.mult).then_inc(sem("lru_b"), 1)
                dve.wait_ge(sem("lru_b"), b + 1)
                for n in range(4):
                    v.tensor_tensor_scan(UT[:, n], AA[:, n], IT[:, n], 0.0, ALU.mult, ALU.add).then_inc(sem("lru_h"), 1)
                dve.wait_ge(sem("lru_h"), 4 * b + 4)
                dve.wait_ge(sem("lru_gelu"), b + 1)
                v.tensor_tensor(AA, UT, LY[:, 4 * b:4 * b + 4], ALU.mult).then_inc(sem("lru_out"), 1)
            if stop < 14:
                return
            dve.wait_ge(sem("mask2_in"), 16)
            dve.wait_ge(sem("lru_out"), 4)
            mk = X[:, 0, 0:2 * 527].rearrange("p (t n) -> p t n", t=2)
            stats2 = smx.rearrange("p (b w t g) -> p b w t g", b=3, w=2, t=2)
            wide2 = P2[:, :, :, 0:512].rearrange("p b t (g s) -> p b t g s", g=2)

            def mask2(job):
                bb = job % 3
                if job >= 3:
                    dve.wait_ge(sem("attn2_turned"), job - 2)
                for tt in range(NT):
                    dve.wait_ge(sem("attn2_scores"), 2 * job + tt + 1)
                    v.tensor_tensor(P2[:, bb, tt], acc[tt][:, :, :].rearrange("p a s -> p (a s)")[:, 0:527], mk[:, tt], ALU.add).then_inc(sem("attn2_masked"), 1)
                dve.wait_ge(sem("attn2_masked"), 2 * job + 2)
                v.tensor_reduce(stats2[:, bb, 0, :, 1:3], wide2[:, bb], AX.X, ALU.max).then_inc(sem("attn2_top"), 1)
                v.tensor_reduce(stats2[:, bb, 0, :, 0:1], P2[:, bb, :, 512:527].unsqueeze(2), AX.X, ALU.max).then_inc(sem("attn2_top"), 1)
                dve.wait_ge(sem("attn2_top"), 2 * job + 2)
                top = smx[:, 12 * bb:12 * bb + 6]
                v.tensor_scalar(top, top, -1e25, -1.0, ALU.max, ALU.mult).then_inc(sem("attn2_max"), 1)

            def finish2(job):
                bb = job % 3
                dve.wait_ge(sem("attn2_exp"), 6 * job + 6)
                r = smx[:, 12 * bb + 6:12 * bb + 12]
                v.tensor_scalar(r, r, 1e-30, None, ALU.max).then_inc(sem("attn2_guard"), 1)
                dve.wait_ge(sem("attn2_guard"), job + 1)
                v.reciprocal(r, r).then_inc(sem("attn2_inverse"), 1)
                dve.wait_ge(sem("attn2_inverse"), job + 1)
                rs = stats2[:, bb, 1]
                v.tensor_tensor(rs, rs, G48[:, :, 3 * job:3 * job + 3], ALU.mult).then_inc(sem("attn2_gated"), 1)
                dve.wait_ge(sem("attn2_gated"), job + 1)
                for tt in range(NT):
                    w = wide2[:, bb, tt]
                    v.tensor_tensor(w, w, bc(rs[:, tt, 1:3], [P, 2, S]), ALU.mult).then_inc(sem("attn2_probs"), 1)
                c = P2[:, bb, :, 512:527]
                v.tensor_tensor(c, c, rs[:, :, 0:1].broadcast_to([P, NT, 15]), ALU.mult).then_inc(sem("attn2_probs"), 1)

            def out2(job):
                dve.wait_ge(sem("attn2_mm"), job + 1)
                v.tensor_copy(Q2[:, job], acc[3][:, 1, 0:S]).then_inc(sem("attn2_out"), 1)

            mask2(0)
            mask2(1)
            for job in range(16):
                if job == 13:
                    ahead("gates2", 2)
                finish2(job)
                if job >= 2:
                    out2(job - 2)
                if job + 2 < 16:
                    mask2(job + 2)
            out2(14)
            out2(15)
            if stop < 15:
                return
            phase("gates2", None, prepared=2,
                  tail=lambda: [ahead("proj_a", 1)] + [rest(READY["mix2"], g, Q2) for g in range(4)])

            def proj_epilogue(second):
                def epilogue(i, j, p, used):
                    dve.wait_ge(mm_half, chunk_done(cur[0], j, i))
                    a = SG2[:, :, bass.ds(i * (2 * NW) + j * NW, NW)]
                    if not second:
                        v.tensor_tensor(a, acc[p][:, :, :], a, ALU.mult).then_inc(acc_used[p], 2)
                        return
                    b = SG2[:, :, bass.ds(i * (2 * NW) + (j * NW + D), NW)]
                    v.tensor_tensor(b, acc[p][:, :, :], b, ALU.mult).then_inc(acc_used[p], 2)
                    dve.wait_ge(acc_used[p], used.val(2, 2))
                    v.tensor_tensor(a, a, b, ALU.add).then_inc(sem("merging2"), 1)
                return epilogue
            phase("proj_a", proj_epilogue(False), prepared=1,
                  tail=lambda: [ahead("proj_b", 1)] + [rest(READY["proj_a"], g, LX) for g in range(4)])
            phase("proj_b", proj_epilogue(True), straight=True, prepared=1,
                  side=lambda i, j, t: fill("m2", 2 * i + j - 1) if t == 3 and 2 * i + j else None,
                  tail=lambda: [ahead("w_out", 1), rest(READY["proj_b"], 0)])
            fill("m2", 3)
            for g in range(1, 4):
                rest(READY["proj_b"], g)
            dve.wait_ge(sem("x_back"), 16)
            dve.wait_ge(sem("g1_in"), 16)
            phase("w_out", residual("x3_ready", gain=lambda i, j: at(80, D)[:, bass.ds(i * (2 * NW) + j * NW, NW)].unsqueeze(1).broadcast_to([P, NT, NW])),
                  straight=True, side=residual_fill(4, mod[:, 32:48]), prepared=1, tail=lambda: ahead("ffn_up", 1))
            fill(4, 3, mod[:, 32:48])
            if stop < 16:
                return
            norm_mean(4)
            norm_tail(4, READY["w_out"], mod[:, 48:64])
            fcw, fcb = col("ffn_conv_w_2"), col("ffn_conv_b_2")

            def convolve(i, p, used, part):
                src = acc[p][:, :, :].rearrange("p a (b s) -> p (a b) s", b=2)
                ms = (2 * part, 2 * part + 1)
                for m in ms:
                    v.tensor_scalar(CV[:, 0, m], src[:, m], fcw[:, bass.ds(i * 4 + (m + 96), 1)], fcb[:, bass.ds(i * 4 + m, 1)],
                                    ALU.mult, ALU.add).then_inc(sem("up_tap"), 1)
                for tap in (1, 2):
                    for m in ms:
                        before = 6 * part + 2 * (tap - 1) + m % 2 + 1
                        last = (part, tap, m % 2) == (1, 2, 1)
                        dve.wait_ge(sem("up_tap"), i * 11 + (11 if last else before))
                        op = v.scalar_tensor_tensor(CV[:, 0, m, tap:S], src[:, m, 0:S - tap], fcw[:, bass.ds(i * 4 + (m + 48 * (2 - tap)), 1)],
                                                    CV[:, 0, m, tap:S], ALU.mult, ALU.add)
                        if last:
                            op.then_inc(acc_used[p], 2)
                        else:
                            op.then_inc(sem("up_tap"), 1)

            def up_epilogue(i, j, p, used):
                dve.wait_ge(mm_half, chunk_done(cur[0], j, i))
                if j == 1:
                    dve.wait_ge(sem("gate_ready"), i + 1)
                    hidden("hidden2", p, i, j, used)
                else:
                    convolve(i, p, used, 0)

            def up_side(i, j, t):
                if (j, t) == (1, 1):
                    convolve(i, *pair_of(cur[0], 0, i), 1)
            phase("ffn_up", up_epilogue, side=up_side, prepared=1, tail=lambda: k_weights(PH["ffn_down"], 0, 0))
            if stop < 17:
                return
            k_outer("ffn_down", KF1)
            dve.wait_ge(sem("g2_in"), 16)
            dve.wait_ge(sem("final_g_in"), 16)
            dve.wait_ge(mm_half, PH["ffn_down"].H0 + PH["ffn_down"].hpi * PH["ffn_down"].iters)
            for tt in range(NT):
                for n in range(4):
                    tmp = at(64 + 2 * n, NW)
                    v.tensor_tensor(tmp, acc[n][:, tt, :], at(0, D)[:, NW * n:NW * n + NW], ALU.mult).then_inc(sem("down2_gated"), 1)
                dve.wait_ge(sem("down2_gated"), 4 * tt + 4)
                v.tensor_tensor(X[:, tt], X[:, tt], at(64, D), ALU.add).then_inc(sem("x4_ready"), 2)
                dve.wait_ge(sem("x4_ready"), 2 * tt + 2)
            dve.wait_ge(sem("final_squares"), NT)
            v.tensor_scalar(stat[:, 2:4], stat[:, 0:2], 1.0 / D, EPS, ALU.mult, ALU.add).then_inc(sem("final_mean"), 1)
            dve.wait_ge(sem("final_root"), 1)
            v.reciprocal(stat[:, 6:8], stat[:, 4:6]).then_inc(sem("final_inverse"), 1)
            dve.wait_ge(sem("final_inverse"), 1)
            for tt in range(NT):
                v.scalar_tensor_tensor(XN[:, tt], X[:, tt], stat[:, 6 + tt:7 + tt], at(8, D), ALU.mult, ALU.mult).then_inc(sem("final"), 1)

        @block.tensor
        def _(pe):
            def product_phase(name, modes, straight=False, width=NW, side=None, fresh=None):
                ph = PH[name]

                def body(i, first):
                    g = 0
                    for n, b in enumerate(ph.body):
                        if b[0] == "a":
                            continue
                        _, j, tt, k0, nk = b
                        p, used = pair_of(ph, j, i)
                        mode = modes(i, j) if callable(modes) else modes
                        if tt == 0 and not (isinstance(i, int) and used.val() == 0):
                            pe.wait_ge(acc_used[p], used.val(2, 0))
                        lasttile = tt == len(ph.chunks[j]) - 1
                        if first and fresh is not None:
                            pe.wait_ge(xl_ready, fresh + (k0 + nk - 1) // 4 + 1)
                        for h, (a, e) in enumerate(halves(nk)):
                            H = half_at(ph, g, h, i)
                            ring = (ph.H0 + 2 * g + h) % 4
                            pe.wait_ge(w_lo, H.val(1, 1))
                            mm = None
                            for k in range(a, e):
                                kx = k0 + k
                                start, stop_ = tt == 0 and k == 0, lasttile and k == nk - 1
                                if mode == "tokens":
                                    for s in range(NT):
                                        o = acc[p][:, s, 0:width]
                                        xh, xl = XH[:, kx, s * P:(s + 1) * P], XL[:, kx, s * P:(s + 1) * P]
                                        wh, wl = WH[:, ring, k - a, 0:width], WL[:, ring, k - a, 0:width]
                                        pe.matmul(o, xh, wh, start=start, stop=False)
                                        pe.matmul(o, xh, wl, start=False, stop=False)
                                        mm = pe.matmul(o, xl, wh, start=False, stop=stop_)
                                else:
                                    for m in range(4):
                                        o = acc[p][:, m // 2, (m % 2) * S:(m % 2 + 1) * S]
                                        wh = WH[:, ring, k - a, m * P:(m + 1) * P]
                                        wl = WL[:, ring, k - a, m * P:(m + 1) * P]
                                        pe.matmul(o, wh, XH[:, kx], start=start and m % 2 == 0, stop=False, skip_group_check=True)
                                        pe.matmul(o, wh, XL[:, kx], start=False, stop=False, skip_group_check=True)
                                        mm = pe.matmul(o, wl, XH[:, kx], start=False, stop=stop_, skip_group_check=True)
                            mm.then_inc(mm_half, 1)
                        g += 1
                        if side:
                            side(i, j, tt)
                    if ph.ada:
                        ada_acc = ada_place(name)[0]
                        a = At(ph.A0, 1, i)
                        pe.wait_ge(ada_mac, a.val(16, 16))
                        if not (isinstance(i, int) and a.val() == 0):
                            pe.wait_ge(ada_rowed, a.val())
                        for q in range(2):
                            mm = pe.matmul(acc[2][0:1, 0, :], one1, ada_acc[:, q], start=q == 0, stop=q == 1)
                        mm.then_inc(ada_red, 1)
                if straight:
                    for i in range(ph.iters):
                        body(i, i == 0)
                else:
                    run(pe, ph, body)

            def turn(n, g, src):
                pairs = TURN_PAIRS[n]
                if g >= (1 if pairs[0] == pairs[1] else 2):
                    pe.wait_ge(sem("xf_filled"), 4 * TURN[n] + g - (0 if pairs[0] == pairs[1] else 1))
                for k in range(4):
                    for tt in range(NT):
                        o = acc[pairs[g % 2]][:, k // 2, (k % 2) * S + tt * P:(k % 2) * S + (tt + 1) * P]
                        mm = pe.transpose(o, src[:, tt, (4 * g + k) * P:(4 * g + k + 1) * P], ident[:, :])
                mm.then_inc(sem("turned"), 1)

            def spread(n):
                pe.wait_ge(sem("norm_rows"), n + 1)
                pe.wait_ge(sem("xf_filled"), 4 * TURN[n] + 4)
                for tt in range(NT):
                    mm = pe.matmul(acc[2][:, 1, tt * P:(tt + 1) * P], root_wide[:, tt], ident[:, :], start=True, stop=True)
                mm.then_inc(sem("norm_spread"), 1)

            pe.wait_ge(sem("ident_in"), 16)
            pe.wait_ge(sem("mem_in"), 16)
            for g in range(4):
                turn(0, g, X)
            pe.wait_ge(sem("bias_wide"), 1)
            for h in range(6):
                if h >= 4:
                    pe.wait_ge(sem("bias_row"), h - 3)
                pe.matmul(acc[h % 2][:, h // 2 % 2, :], at(76, 768)[0:32, P * h:P * h + P], at(33, 512)[0:32],
                          start=True, stop=True).then_inc(sem("bias_mm"), 1)
            spread(0)
            if stop < 3:
                return
            def turn_x(i, j, t):
                n = 4 * j + t
                if n % 2:
                    if n == 1:
                        pe.wait_ge(sem("x_in"), 16)
                    turn(1, n // 2, X)
            pe.wait_ge(sem("bias_row"), 6)
            product_phase("mem", "tokens", straight=True, fresh=0, side=turn_x)
            if stop < 4:
                return
            pe.wait_ge(ada_rowed, 1)
            spread(1)
            HC = [P * h for h in range(12)] + [2304 + P * h for h in range(8)] + [3584 + P * h for h in range(4)]

            def turn_heads(n):
                g, pair = HEAD_GROUPS[n], HEAD_PAIR[n]
                if n == 4:
                    pe.wait_ge(ada_rowed, 5)
                if n > 0 and n != 4:
                    pe.wait_ge(sem("heads_ready"), n if n < 4 else n - 1)
                pe.wait_ge(sem("heads_scaled"), (1, 2, 3, 4, 7, 7, 7)[n])
                if n >= 5:
                    pe.wait_ge(sem("roped"), 4)
                for k in range(4):
                    for tt in range(NT):
                        rows = KC[:, tt, P * k:P * k + P] if g == 6 else Z[:, tt, HC[4 * g + k]:HC[4 * g + k] + P]
                        mm = pe.transpose(acc[pair][:, k // 2, (k % 2) * S + tt * P:(k % 2) * S + (tt + 1) * P], rows, ident[:, :])
                mm.then_inc(sem("heads_turned"), 1)

            product_phase("qkv", "tokens", straight=True, fresh=READY["mem"],
                          side=lambda i, j, t: turn_heads(2 * i + j - 1) if t == 0 and 1 <= 2 * i + j <= 4 else None)
            for n in range(4, 7):
                turn_heads(n)
            if stop < 6:
                return
            pe.wait_ge(sem("heads_ready"), 7)
            pe.wait_ge(sem("bias_ready"), 4)

            def keys1(job):
                if job < 2:
                    return [(2 * g + job, 6 + 2 * g + job, lambda kt, h=2 * g + job: Z[:, kt, 1536 + P * h:1536 + P * h + P])
                            for g in range(3)]
                if job < 8:
                    h = job - 2
                    return [(12 + h, 18 + h // 3, lambda kt: Z[:, kt, 3328 + P * (h // 3):3328 + P * (h // 3) + P])]
                h = job - 8
                return [(20 + h, 24 + h, lambda kt: VC[:, kt, P * h:P * h + P])]

            def scores1(job):
                for tt in range(NT):
                    if job >= 1:
                        pe.wait_ge(sem("attn1_exp"), 2 * (job - 1) + tt + 1)
                    for g, (q, k, _) in enumerate(keys1(job)):
                        mm = pe.matmul(acc[tt][:, g // 2, (g % 2) * S:(g % 2 + 1) * S], QK[:, q, tt * P:(tt + 1) * P], QK[:, k],
                                       start=True, stop=True)
                    mm.then_inc(sem("attn1_scores"), 1)

            def turn1(job):
                pe.wait_ge(sem("attn1_probs"), job + 1)
                if job:
                    pe.wait_ge(sem("attn1_pt"), pt_count(job - 1))
                for g in range(len(keys1(job))):
                    for kt in range(NT):
                        n = 2 * g + kt
                        for tt in range(NT):
                            o = acc[2 + n // 4][:, (n % 4) // 2, (n % 2) * S + tt * P:(n % 2) * S + (tt + 1) * P]
                            mm = pe.transpose(o, probs1(job)[:, tt, S * g + P * kt:S * g + P * kt + P], ident[:, :])
                mm.then_inc(sem("attn1_turned"), 1)

            def values1(job):
                segs = keys1(job)
                pe.wait_ge(sem("attn1_pt"), pt_count(job))
                if job:
                    pe.wait_ge(sem("attn1_out"), job)
                for g, (_, _, value) in enumerate(segs):
                    for kt in range(NT):
                        n = 2 * g + kt
                        mm = pe.matmul(acc[3][:, 1, 0:S], value(kt), PT1[:, job % 2, n], start=n == 0, stop=n == 2 * len(segs) - 1)
                mm.then_inc(sem("attn1_mm"), 1)

            def pt_count(job):
                return 2 * min(job + 1, 2) + max(job - 1, 0)

            for job in range(3):
                scores1(job)
            for job in range(12):
                turn1(job)
                if job:
                    values1(job - 1)
                if job + 3 < 12:
                    scores1(job + 3)
            values1(11)
            pe.wait_ge(sem("attn1_out"), 12)
            if stop < 7:
                return
            product_phase("gates", "tokens")
            if stop < 8:
                return
            def merged_turn(i, j, t):
                if i and (j, t) == (1, 0):
                    pe.wait_ge(sem("merging1"), 2 * i)
                    if i == 1:
                        pe.wait_ge(ada_rowed, 11)
                    turn("m1", i - 1, M)
            product_phase("branch", "tokens", straight=True, fresh=READY["gates"], side=merged_turn)
            pe.wait_ge(sem("merging1"), 8)
            turn("m1", 3, M)

            def residual_turn(n):
                def side(i, j, t):
                    c = 2 * i + j - 1
                    if t == 1 and c >= 0:
                        C = PH["w_o" if n == 2 else "w_out"].C0 + c
                        pe.wait_ge(acc_used[C % 2], 2 * (C // 2 + 1))
                        if n == 4:
                            pe.wait_ge(sem("x3_ready"), c + 1)
                        turn(n, c, X)
                return side
            product_phase("w_o", "tokens", straight=True, fresh=READY["branch"], side=residual_turn(2))
            residual_turn(2)(2, 0, 1)
            if stop < 9:
                return
            pe.wait_ge(ada_rowed, 13)
            spread(2)
            product_phase("ffn_in", "features", fresh=READY["w_o"])
            if stop < 10:
                return

            def k_outer(name, base):
                ph = PH[name]
                for p in range(2):
                    pe.wait_ge(acc_used[p], 2 * c_end(before[name], p))

                def body(i, first):
                    for j in range(4):
                        pe.wait_ge(sem("hidden_rest"), At(base + j, 4, i).val(1, 1))
                        for h in range(2):
                            H = At(ph.H0 + 2 * j + h, 8, i)
                            ring = (ph.H0 + 2 * j + h) % 4
                            pe.wait_ge(w_lo, H.val(1, 1))
                            for nn in range(2):
                                for s in range(NT):
                                    o = acc[2 * h + nn][:, s, :]
                                    xh, xl = XH[:, j, s * P:(s + 1) * P], XL[:, j, s * P:(s + 1) * P]
                                    st = first and j == 0
                                    pe.matmul(o, xh, WH[:, ring, nn], start=st, stop=False, skip_group_check=True)
                                    pe.matmul(o, xh, WL[:, ring, nn], start=False, stop=False, skip_group_check=True)
                                    mm = pe.matmul(o, xl, WH[:, ring, nn], start=False, stop=True, skip_group_check=True)
                            mm.then_inc(mm_half, 1)
                run(pe, ph, body)
            before = {"ffn_out": "ffn_in", "ffn_down": "ffn_up"}
            pe.wait_ge(ada_rowed, ADA_CHUNKS)
            pe.wait_ge(sem("mod_in"), 64)
            pe.transpose(acc[2][:, 1, 0:64], at(88, P)[0:64], ident[0:64, 0:64]).then_inc(sem("mod_turned"), 1)
            pe.wait_ge(sem("mod_copied"), 1)
            k_outer("ffn_out", 0)
            if stop < 11:
                return
            for g in range(4):
                pe.wait_ge(sem("x2_ready"), g + 1)
                turn(3, g, X)
            spread(3)
            product_phase("q2", "features", fresh=READY["ffn_in"])
            product_phase("kv2", lambda i, j: ("features", "features", "features", "tokens", "features", "tokens")[2 * i + j], straight=True)
            product_phase("g48", "tokens", width=48)
            product_phase("lru_in", "features")
            if stop < 12:
                return
            pe.wait_ge(sem("lru_w_in"), 32)

            def lru_gate_products(b):
                for n in range(4):
                    k = 4 * b + n
                    pe.wait_ge(sem("conv_tap"), 16 * b + 12 + n + 1)
                    if k >= 2:
                        pe.wait_ge(sem("lru_r"), 2 * (k - 1))
                    pe.matmul(acc[2 + k % 2][:, 0, 0:S], X[:, 0, P * k:P * k + P], UT2[b % 2][:, n], start=True, stop=True)
                    pe.matmul(acc[2 + k % 2][:, 0, S:2 * S], X[:, 1, P * k:P * k + P], UT2[b % 2][:, n], start=True, stop=True).then_inc(sem("lru_gates"), 1)

            def compress(n, kv, pos):
                pe.wait_ge(sem(f"cmp_in{n}"), 16)
                by16 = kv[:, :, :].rearrange("p g (w l) -> p g w l", l=16)
                for l in range(32):
                    w = W1[:, n, P * l:P * l + P]
                    pe.matmul(acc[2 + n][:, 1, 0:60].rearrange("p (g w) -> p g w", g=4), w, by16[:, :, l // 16:l // 16 + 15, l % 16],
                              start=l == 0, stop=False)
                    mm = pe.matmul(acc[2 + n][:, 1, 0:60], w, col(pos)[:, l:l + 1].broadcast_to([P, 60]), start=False, stop=l == 31)
                mm.then_inc(sem("cmp_hid"), 1)

            lru_gate_products(0)
            compress(0, KC2, "cmp_pos_k_2")
            lru_gate_products(1)
            compress(1, VC2, "cmp_pos_v_2")
            lru_gate_products(2)
            lru_gate_products(3)
            pe.wait_ge(sem("cmp2_in"), 32)
            pe.wait_ge(sem("cmp_gelu"), 2)
            pe.matmul(acc[2][:, 1, 64:124], CMP_W2[:, 0], CMP_HID[:, 0, 0:60], start=True, stop=True).then_inc(sem("cmp_done"), 1)
            for g in range(4):
                mm = pe.matmul(acc[3][0:15, 1, P * g:P * g + P], CMP_HID[:, 1, 15 * g:15 * g + 15], CMP_W2[:, 1], start=True, stop=True)
            mm.then_inc(sem("cmp_done"), 1)
            pe.wait_ge(sem("cmp_kept"), 2)
            pe.wait_ge(sem("lru_out"), 4)
            if stop < 14:
                return

            def scores2(job):
                kv = job // 4
                for tt in range(NT):
                    if job >= 1:
                        pe.wait_ge(sem("attn2_masked"), 2 * (job - 1) + tt + 1)
                    q = Q2[:, job, tt * P:(tt + 1) * P]
                    pe.matmul(acc[tt][:, 0, 0:S], q, KS2[:, kv], start=True, stop=True)
                    pe.matmul(acc[tt][:, 0, S:2 * S], q, KW2[:, kv], start=True, stop=True)
                    pe.matmul(acc[tt][:, 1, 0:15], q, KCMP[:, 15 * kv:15 * kv + 15], start=True, stop=True).then_inc(sem("attn2_scores"), 1)

            def turn2(job):
                bb = job % 3
                pe.wait_ge(sem("attn2_probs"), 3 * job + 3)
                if job:
                    pe.wait_ge(sem("attn2_pt"), 2 * job)
                for g in range(2):
                    for kt in range(NT):
                        n = 2 * g + kt
                        for tt in range(kt, NT):
                            pe.transpose(acc[2][:, n // 2, (n % 2) * S + tt * P:(n % 2) * S + (tt + 1) * P],
                                         P2[:, bb, tt, S * g + P * kt:S * g + P * kt + P], ident[:, :])
                for tt in range(NT):
                    mm = pe.transpose(acc[3][0:15, 0, tt * P:(tt + 1) * P], P2[:, bb, tt, 512:527], ident[:, :])
                mm.then_inc(sem("attn2_turned"), 1)

            def values2(job):
                kv, bb = job // 4, job % 2
                pe.wait_ge(sem("attn2_pt"), 2 * job + 2)
                if job:
                    pe.wait_ge(sem("attn2_out"), job)
                o = acc[3][:, 1, 0:S]
                for n, values in ((0, VS2), (2, VW2)):
                    for kt in range(NT):
                        pe.matmul(o[:, P * kt:S], values[:, kt, P * kv:P * kv + P], PT2[:, bb, n + kt, P * kt:S], start=(n, kt) == (0, 0), stop=False)
                pe.matmul(o, VCMP[0:15, P * kv:P * kv + P], PC2[0:15, bb], start=False, stop=True).then_inc(sem("attn2_mm"), 1)

            for job in range(3):
                scores2(job)
            for job in range(16):
                turn2(job)
                if job:
                    values2(job - 1)
                if job + 3 < 16:
                    scores2(job + 3)
            values2(15)
            pe.wait_ge(sem("attn2_out"), 16)
            if stop < 15:
                return
            product_phase("gates2", "tokens")
            product_phase("proj_a", "tokens", fresh=READY["mix2"])

            def turn_merged(i, j, t):
                c = 2 * i + j - 1
                if t == 1 and c >= 0:
                    pe.wait_ge(sem("merging2"), c + 1)
                    turn("m2", c, SG2)
            product_phase("proj_b", "tokens", fresh=READY["proj_a"], straight=True, side=turn_merged)
            turn_merged(2, 0, 1)
            product_phase("w_out", "tokens", fresh=READY["proj_b"], straight=True, side=residual_turn(4))
            residual_turn(4)(2, 0, 1)
            if stop < 16:
                return
            spread(4)
            product_phase("ffn_up", "features", fresh=READY["w_out"])
            if stop < 17:
                return
            k_outer("ffn_down", KF1)


def _bucket(rel):
    nb, max_dist = 16, 1024
    n = np.abs(rel)
    large = nb // 2 + (np.log(np.maximum(n, 1).astype(np.float32) / np.float32(nb // 2))
                       / np.float32(np.log(max_dist / (nb // 2))) * np.float32(nb - nb // 2)).astype(np.int32)
    return np.where(rel > 0, nb, 0) + np.where(n < nb // 2, n, np.minimum(large, nb - 1))


def _constants():
    pos = np.arange(S)
    diff = np.arange(-255, 256)
    one_hot = np.zeros((32, 512), np.float32)
    one_hot[_bucket(diff), diff + 255] = 1.0
    rel = pos[None, :] - pos[:, None]
    ok = [np.abs(rel) <= 64] + [(rel % dil == 0) & (np.abs(rel) // dil <= 64) for dil in (4, 16)]
    masks_a = np.stack([np.where(m, 0.0, NEG) for m in ok]).astype(np.float32)
    masks_a = masks_a.reshape(3, NT, P, S).transpose(2, 1, 0, 3).reshape(P, -1)
    causal = np.where(rel <= 0, 0.0, NEG)
    ends = np.arange(15) * 16 + 31
    cmp = np.where(ends[None, :] <= pos[:, None], 0.0, NEG)
    masks_2 = np.concatenate([causal, causal, cmp], 1).astype(np.float32)
    masks_2 = masks_2.reshape(NT, P, 527).transpose(1, 0, 2).reshape(P, -1)
    inv = np.float32(10000.0) ** (-np.arange(32, dtype=np.float32) / np.float32(32))
    r, c = (pos // 64).astype(np.float32), (pos % 64).astype(np.float32)
    ang = np.concatenate([r[:, None] * inv, c[:, None] * inv], 1).astype(np.float32)
    rope = np.stack([np.cos(ang), np.sin(ang)], 1).astype(np.float32)
    rope = rope.reshape(NT, P, 2, 64).transpose(1, 0, 2, 3).reshape(P, -1)
    return {"identity": np.eye(P, dtype=np.float32), "one_hot": one_hot, "masks_a": masks_a, "masks_2": masks_2,
            "rope": rope}


_AS_IS = ["rel_bias"]
_FIRST = ["w_in", "g_qb", "g_kb", "w_mem_kv", "w_br_a", "w_br_b", "w_br_c", "w_o", "w_ffn_in", "w_ffn_out",
          "ada_w_2", "w_in_2", "cmp_w1_k_2", "cmp_w2_k_2", "cmp_w1_v_2", "cmp_w2_v_2", "lru_wa_2", "lru_wi_2",
          "proj_a_2", "proj_b_2", "w_out_2", "ffn_up_2", "ffn_down_2", "x", "mem"]


def _inputs(inputs):
    a = {n: np.ascontiguousarray(inputs[n]) for n in _AS_IS}
    a |= {n: np.ascontiguousarray(inputs[n][0]) for n in _FIRST}
    a["g_qb"], a["g_kb"] = a["g_qb"].reshape(HD), a["g_kb"].reshape(HD)
    a["ada_b_2"] = np.ascontiguousarray(inputs["ada_b_2"]).reshape(1, -1)
    a["final_g_2"] = np.ascontiguousarray(inputs["final_g_2"]).reshape(-1)
    a["vectors"] = np.ascontiguousarray(np.concatenate(
        [np.asarray(inputs[n]).reshape(-1, P) for n, _ in VECTORS]).T)
    a |= _constants()
    return a


def build(nc, a, stop=99):
    t = {n: nc.dram_tensor(f"in_{n}", v.shape, mybir.dt.from_np(v.dtype), kind="ExternalInput").ap()
         for n, v in a.items()}
    out = nc.dram_tensor("out_0", (S, D), F32, kind="ExternalOutput").ap()
    two_block_program(nc, t, out, stop)


def kernel(**inputs):
    import concourse.bacc as bacc
    from concourse.bass_utils import run_bass_kernel_spmd

    a = _inputs(inputs)
    nc = bacc.Bacc("TRN2", target_bir_lowering=False, num_devices=1)
    build(nc, a)
    r = run_bass_kernel_spmd(nc, [{f"in_{n}": v for n, v in a.items()}], core_ids=[0])
    return r.results[0]["out_0"].reshape(1, S, D)
```

```python
from contextlib import ExitStack

import numpy as np

import concourse.bass as bass
from concourse import mybir

F32 = mybir.dt.float32
F32R = mybir.dt.float32r
ALU = mybir.AluOpType
ACT = mybir.ActivationFunctionType
AX = mybir.AxisListType

P = 128
S = 256
NT = S // P
D = 2048
KD = D // P
NW = 512
EPS = 1e-6
HD = 128
SCALE = float(HD) ** -0.5
NEG = -1e30

FF1 = 5632
KF1 = FF1 // P
FF2 = 6144
KF2 = FF2 // P
A_GROUPS, A_PER = 3, 2
ADA_CHUNKS = 6 * D // NW

VECTORS = [("c_2", 16), ("g_mem", 16), ("g_mix", 16), ("g_ffn", 16), ("norm1_g_2", 16), ("norm2_g_2", 16),
           ("g_qa", 1), ("g_ka", 1), ("g_qc", 1), ("g_kc", 1),
           ("lru_lambda_2", 16), ("lru_ba_2", 16), ("lru_bi_2", 16), ("lru_conv_b_2", 16), ("lru_conv_w_2", 64),
           ("ffn_conv_w_2", 144), ("ffn_conv_b_2", 48), ("cmp_pos_k_2", 32), ("cmp_pos_v_2", 32)]
COL = {}
_at = 0
for _n, _k in VECTORS:
    COL[_n] = _at
    _at += _k
NCOL = _at


READY = {"mem": 4, "qkv": 8, "gates": 8, "branch": 11, "w_o": 15, "ffn_in": 19, "mix2": 23,
         "proj_a": 27, "proj_b": 31, "w_out": 35, "ffn_up": 39}


TURN = {0: 0, 1: 1, "m1": 2, 2: 3, 3: 4, "m2": 5, 4: 6}
TURN_PAIRS = {0: (2, 3), 1: (3, 3), "m1": (2, 3), 2: (3, 3), 3: (0, 1), "m2": (2, 3), 4: (2, 3)}


class At:

    def __init__(self, base, per=0, i=0):
        self.base, self.per, self.i = base, per, i

    def val(self, scale=1, offset=0):
        const = scale * self.base + offset
        step = scale * self.per
        if isinstance(self.i, int):
            return const + step * self.i
        if step == 0:
            return const
        return self.i * step + const


K16 = [(0, 4), (4, 4), (8, 4), (12, 4)]
BRANCH = [[(0, 2)], [(2, 3), (5, 3)], [(8, 4)]]


def body_of(chunks, ada):
    out, q = [], 0
    for j, tiles in enumerate(chunks):
        for t, (k0, nk) in enumerate(tiles):
            out.append(("g", j, t, k0, nk))
            if ada and t % 2 == 0:
                out.append(("a", q, 0, 0, 0))
                q += 1
    return out


class Phase:
    def __init__(self, name, iters, chunks, ada=False):
        self.name, self.iters, self.chunks, self.ada = name, iters, chunks, ada
        self.body = body_of(chunks, ada)


def plan():
    two = [K16, K16]
    phases = [Phase("mem", 1, two, True), Phase("qkv", 4, two, True), Phase("gates", 6, two, True),
              Phase("branch", 4, BRANCH), Phase("w_o", 2, two, True), Phase("ffn_in", 11, two, True),
              Phase("ffn_out", KF1 // 4, [[(0, 1)] * 4]),
              Phase("lru_x", 2, two), Phase("lru_y", 2, two), Phase("q2", 2, two), Phase("kv2", 3, two), Phase("g48", 1, [K16]),
              Phase("gates2", 4, two), Phase("proj_a", 2, two), Phase("proj_b", 2, two),
              Phase("w_out", 2, two), Phase("ffn_up", 12, two), Phase("ffn_down", KF2 // 4, [[(0, 1)] * 4])]
    t = h = c = a = 0
    for p in phases:
        p.T0, p.H0, p.C0, p.A0 = t, h, c, a
        p.tpi = len(p.body)
        p.hpi = 2 * sum(b[0] == "g" for b in p.body)
        p.cpi = 0 if p.name in ("ffn_out", "ffn_down") else len(p.chunks)
        t += p.tpi * p.iters
        h += p.hpi * p.iters
        c += p.cpi * p.iters
        a += p.iters if p.ada else 0
        assert p.T0 % 4 == 0 and p.tpi % 4 == 0, p.name
    assert a == ADA_CHUNKS
    return {p.name: p for p in phases}


def two_block_program(nc, t, out):
    PH = plan()
    ctx = ExitStack()
    with ctx:
        def sb(name, shape, dt):
            return ctx.enter_context(nc.sbuf_tensor(name, shape, dt))

        sems = {}

        def sem(name):
            if name not in sems:
                sems[name] = ctx.enter_context(nc.semaphore(name))
            return sems[name]

        raw = sb("raw", [P, 4, 4, NW], F32)
        WH = sb("WH", [P, 4, 2, NW], F32R)
        WL = sb("WL", [P, 4, 2, NW], F32R)
        XH = sb("XH", [P, KD, S], F32R)
        XL = sb("XL", [P, KD, S], F32R)
        X = sb("X", [P, NT, D], F32)
        KB = 256
        arena = sb("arena", [P, 92 * KB], F32)
        cols = sb("cols", [P, NCOL], F32)
        ident = sb("ident", [P, P], F32)
        small = sb("small", [P, 326], F32)
        acc = [ctx.enter_context(nc.psum_tensor(f"acc{i}", [P, 2, NW], F32)) for i in range(4)]

        def at(kb, n):
            return arena[:, int(kb * KB):int(kb * KB) + n]

        XF = at(0, KD * S).rearrange("p (k s) -> p k s", k=KD)
        XN = at(16, NT * D).rearrange("p (t n) -> p t n", t=NT)
        junk = at(64, NT * NW).rearrange("p (t n) -> p t n", t=NT)
        root_wide = at(68, NT * P).rearrange("p (t n) -> p t n", t=NT)
        KC = at(56, NT * NW).rearrange("p (t n) -> p t n", t=NT)
        Z = at(16, NT * 4096).rearrange("p (t n) -> p t n", t=NT)
        QK = at(48, 28 * S).rearrange("p (h s) -> p h s", h=28)
        VC = at(76, NT * NW).rearrange("p (t n) -> p t n", t=NT)
        BI = at(80, 12 * S).rearrange("p (j t g s) -> p j t g s", j=2, t=2, g=3)
        SG = at(16, NT * 6144).rearrange("p (t n) -> p t n", t=NT)
        M = at(64, NT * D).rearrange("p (t n) -> p t n", t=NT)
        AT = at(16, 48 * S).rearrange("p (k s) -> p k s", k=48)
        GT = at(64, 4 * S).rearrange("p (m s) -> p m s", m=4)
        CV = at(72, 4 * S).rearrange("p (m s) -> p m s", m=4)

        def ada_place(name):
            kb = {"mem": 48, "qkv": 0}.get(name, 80)
            return at(kb, 2 * NW).rearrange("p (b n) -> p b n", b=2), at(kb + 4, NW), at(kb + 6, NW)

        def col(name):
            return cols[:, COL[name]:COL[name] + dict(VECTORS)[name]]

        def bc(ap, shape):
            return ap.unsqueeze(2).broadcast_to(shape)

        one1 = small[:, 1:2]
        cact = small[:, 2:18]
        stat = small[:, 18:34]
        gq = small[:, 34:62]
        smx = small[:, 290:326]
        mod = small[:, 94:158]
        lamc = small[:, 158:190]
        G48 = small[:, 190:286].rearrange("p (t n) -> p t n", t=NT)

        XT = lambda kb, n: at(kb, n * S).rearrange("p (k s) -> p k s", k=n)
        Q2, LX, LY = XT(16, 16), XT(32, 16), XT(48, 16)
        KC2, VC2, KS2, KW2 = XT(64, 4), XT(68, 4), XT(72, 4), XT(76, 4)
        VS2 = at(80, NT * NW).rearrange("p (t n) -> p t n", t=NT)
        VW2 = at(84, NT * NW).rearrange("p (t n) -> p t n", t=NT)
        KCMP = at(88, 64)
        VCMP = at(89, 512)
        SG2 = at(48, NT * 4096).rearrange("p (t n) -> p t n", t=NT)

        HEADS = [(-1, KC[:, :, :], 24), (0, Z[:, :, 0:512], 0), (1, Z[:, :, 512:1024], 4), (2, Z[:, :, 1024:1536], 8),
                 (5, Z[:, :, 2304:3072], 12), (6, Z[:, :, 3072:3328], 18), (7, Z[:, :, 3584:4096], 20)]
        HEAD_TILE = [2] + [4 * (done_at + 1) for done_at, _, _ in HEADS[1:]]
        HEAD_STATS = mod[:, 0:56].rearrange("p (t h) -> p t h", t=NT)
        ROPE = at(12, NW)
        JOB_OUT = (0, 1, 8, 9, 10, 11, 2, 3, 4, 5, 6, 7)
        HEAD_PAIR = (3, 3, 3, 3, 2, 2, 3)
        HEAD_GROUPS = (6, 0, 1, 2, 5, 3, 4)

        amax1, asum1 = smx[:, 0:6], smx[:, 6:12]
        x_flat = X[:, :, :].rearrange("p t n -> p (t n)")

        def probs1(job):
            n, start = (1536, 1536 * job) if job < 2 else (512, (3072, 3584, 0)[(job - 2) % 3])
            return x_flat[:, start:start + n].rearrange("p (t n) -> p t n", t=NT)
        PT1 = Z[:, :, 0:1536].rearrange("p b (k s) -> p b k s", k=6)
        SIDE0 = {"lru_y": 0, "q2": 16, "kv2": 32}
        IT2, UT2 = (XT(0, 4), XT(4, 4)), (XT(8, 4), XT(12, 4))
        RT, TT = XT(64, 4), XT(68, 4)
        BLOCKS = at(48, 4 * 1024).rearrange("p (m h n) -> p m h n", m=2, h=2)
        W1 = (at(0, 4096), X[:, :, :].rearrange("p t n -> p (t n)"))
        CMP_HID = at(88.25, 2 * 64).rearrange("p (n e) -> p n e", n=2)
        CMP_W2 = at(91, 2 * P).rearrange("p (n e) -> p n e", n=2)
        GATE_ROWS = at(48, S)[0:48]
        SEG = [(2 * S, 2 * S + 15), (0, S), (S, 2 * S)]
        P2 = at(0, 6 * 527).rearrange("p (b t n) -> p b t n", b=3, t=2)
        PC2 = at(13, 2 * S).rearrange("p (b s) -> p b s", b=2)
        PT2 = X[:, 1, :].rearrange("p (b k s) -> p b k s", b=2, k=4)

        mod_dram = nc.dram_tensor("mod_scratch", (6 * D,), F32, kind="Internal").ap()
        bias_dram = nc.dram_tensor("bias_scratch", (6, P, 2 * S), F32, kind="Internal").ap()
        x_dram = nc.dram_tensor("x_scratch", (P, NT * D), F32, kind="Internal").ap()

        landed = [sem(f"tile_landed{i}") for i in range(4)]
        w_hi, w_lo = sem("weights_rounded"), sem("weights_rest")
        mm_half = sem("half_multiplied")
        acc_used = [sem("acc_used0"), sem("acc_used1")]
        ada_mac, ada_red, ada_rowed = sem("ada_multiplied"), sem("ada_reduced"), sem("ada_row_ready")
        ada_b_in, ada_stored = sem("ada_bias_landed"), sem("ada_row_stored")
        xh_ready, xl_ready = sem("acts_rounded"), sem("acts_rest")

        def run(eng, ph, body):
            body(0, True)
            if ph.iters > 1:
                with eng.Fori(1, ph.iters) as i:
                    body(i, False)

        def c_end(name, p):
            ph = PH[name]
            return (ph.C0 + ph.cpi * ph.iters + 1 - p) // 2

        def last_half(ph, n, i):
            g = sum(b[0] == "g" for b in ph.body[:n])
            return At(ph.H0 + 2 * g + 1, ph.hpi, i)

        def chunk_done(ph, j, i):
            n = max(n for n, b in enumerate(ph.body) if b[0] == "g" and b[1] == j)
            return last_half(ph, n, i).val(1, 1)

        def pair_of(ph, j, i):
            c = ph.C0 + j
            if ph.cpi == 3:
                c += 3 * i
                return c % 2, At(c // 2)
            return c % 2, At(c // 2, 1, i)

        block = ctx.enter_context(nc.Block())

        @block.sync
        def _(sp):
            tail = [None]

            def reuse(ph, n, i, first):
                if n >= 4:
                    m, before, at_i = n - 4, ph, i
                elif not first:
                    m, before, at_i = n - 4 + ph.tpi, ph, i - 1
                elif tail[0]:
                    before = tail[0]
                    m, at_i = n - 4 + before.tpi, before.iters - 1
                else:
                    if n == 2:
                        sp.wait_ge(sem("mem_in"), 16)
                    return
                if before.body[m][0] == "a":
                    sp.wait_ge(ada_mac, At(before.A0, 1, at_i).val(16, 4 * before.body[m][1] + 4))
                else:
                    sp.wait_ge(w_lo, last_half(before, m, at_i).val(1, 1))

            def load(T, slot, dst, src):
                sp.dma_start(dst, src).then_inc(landed[slot], 16)

            def stream(ph, source):
                def body(i, first):
                    for n, b in enumerate(ph.body):
                        T = At(ph.T0 + n, ph.tpi, i)
                        slot = n % 4
                        reuse(ph, n, i, first)
                        if b[0] == "a":
                            column = At(ph.A0, 1, i).val(NW)
                            src = t["ada_w_2"].rearrange("(k p) n -> p k n", p=P)[
                                :, 4 * b[1]:4 * b[1] + 4, bass.ds(column, NW)]
                            load(T, slot, raw[:, slot], src)
                        else:
                            source(i, T, slot, *b[1:])
                if ph.cpi == 3:
                    for i in range(ph.iters):
                        body(i, i == 0)
                else:
                    run(sp, ph, body)
                tail[0] = ph

            def chunked(w, column):
                wv = w.rearrange("(k p) n -> p k n", p=P)

                def source(i, T, slot, j, tt, k0, nk):
                    load(T, slot, raw[:, slot, 0:nk], wv[:, k0:k0 + nk, bass.ds(column(i, j), NW)])
                return source

            def rows(w):
                def source(i, T, slot, j, tt, k0, nk):
                    start = At(tt, 4, i).val(P)
                    load(T, slot, raw[:, slot].rearrange("p a n -> p (a n)"), w[bass.ds(start, P), :])
                return source

            def lin(base, per_i, per_j):
                return lambda i, j: i * per_i + (base + j * per_j)

            stream(PH["mem"], chunked(t["w_mem_kv"], lin(0, 2 * NW, NW)))
            stream(PH["qkv"], chunked(t["w_in"], lin(0, 2 * NW, NW)))
            stream(PH["gates"], chunked(t["w_in"], lin(4096, 2 * NW, NW)))
            wa = t["w_br_a"].rearrange("(k p) n -> p k n", p=P)
            wb = t["w_br_b"].rearrange("(k p) n -> p k n", p=P)
            wc = t["w_br_c"].rearrange("(k p) n -> p k n", p=P)

            def branch(i, T, slot, j, tt, k0, nk):
                w, base = ((wa, 0), (wb, 2), (wc, 8))[j]
                load(T, slot, raw[:, slot, 0:nk], w[:, k0 - base:k0 - base + nk, i * NW:(i + 1) * NW])
            stream(PH["branch"], branch)
            stream(PH["w_o"], chunked(t["w_o"], lin(0, 2 * NW, NW)))
            stream(PH["ffn_in"], chunked(t["w_ffn_in"], lin(0, NW, FF1)))
            stream(PH["ffn_out"], rows(t["w_ffn_out"]))
            w2 = t["w_in_2"]
            stream(PH["lru_x"], chunked(w2, lin(5168, 2 * NW, NW)))
            stream(PH["lru_y"], chunked(w2, lin(5168 + D, 2 * NW, NW)))
            stream(PH["q2"], chunked(w2, lin(0, 2 * NW, NW)))
            stream(PH["kv2"], chunked(w2, lin(2048, 2 * NW, NW)))
            w2v = w2.rearrange("(k p) n -> p k n", p=P)

            def g48(i, T, slot, j, tt, k0, nk):
                load(T, slot, raw[:, slot, :, 0:48], w2v[:, k0:k0 + nk, 5120:5168])
            stream(PH["g48"], g48)
            stream(PH["gates2"], chunked(w2, lin(9264, 2 * NW, NW)))
            stream(PH["proj_a"], chunked(t["proj_a_2"], lin(0, 2 * NW, NW)))
            stream(PH["proj_b"], chunked(t["proj_b_2"], lin(0, 2 * NW, NW)))
            stream(PH["w_out"], chunked(t["w_out_2"], lin(0, 2 * NW, NW)))
            stream(PH["ffn_up"], chunked(t["ffn_up_2"], lin(0, NW, FF2)))
            stream(PH["ffn_down"], rows(t["ffn_down_2"]))

        @block.gpsimd
        def _(gp):
            gp.dma_start(X[:, :, :], t["mem"].rearrange("(t p) n -> p t n", p=P)).then_inc(sem("mem_in"), 16)
            gp.dma_start(ident[:, :], t["identity"]).then_inc(sem("ident_in"), 16)
            gp.dma_start(cols[:, :], t["vectors"]).then_inc(sem("cols_in"), 16)
            gp.dma_start(at(32, 6)[0:32], t["rel_bias"]).then_inc(sem("bias_in"), 16)
            gp.dma_start(at(33, 512)[0:32], t["one_hot"]).then_inc(sem("bias_in"), 16)
            gp.memset(one1, 1.0).then_inc(sem("small_set"), 1)
            gp.memset(gq, 1.0).then_inc(sem("small_set"), 1)
            gp.dma_start(at(36, 6 * S), t["masks_a"]).then_inc(sem("mask_in"), 16)
            gp.wait_ge(sem("turned"), 4)
            gp.wait_ge(sem("norm_squares"), 8)
            gp.dma_start(X[:, :, :], t["x"].rearrange("(t p) n -> p t n", p=P)).then_inc(sem("x_in"), 16)
            for h in range(6):
                gp.wait_ge(sem("bias_row"), h + 1)
                gp.dma_start(bias_dram[h], at(16 + 2 * h, 512)).then_inc(sem("bias_out"), 16)
            gp.wait_ge(sem("bias_out"), 16 * 6)
            for h in range(6):
                g, j = h // 2, h % 2
                for tt in range(NT):
                    src = bass.AP(tensor=bias_dram.tensor, offset=h * P * 512 + 255 - tt * P, ap=[[511, P], [1, S]])
                    gp.dma_start(BI[:, j, tt, g, :], src).then_inc(sem("bias_back"), 16)
            def ada_rows(name):
                ph = PH[name]
                _, ada_row, ada_brow = ada_place(name)

                if name == "qkv":
                    gp.wait_ge(xl_ready, READY["qkv"])
                    gp.dma_start(ROPE[:, 0:256], t["rope"]).then_inc(sem("rope_in"), 16)
                    gp.dma_start(ROPE[:, 256:384], t["g_qb"].partition_broadcast(P)).then_inc(sem("rope_in"), 16)
                    gp.dma_start(ROPE[:, 384:512], t["g_kb"].partition_broadcast(P)).then_inc(sem("rope_in"), 16)
                for a in range(ph.A0, ph.A0 + ph.iters):
                    gp.dma_start(ada_brow[0:1], t["ada_b_2"][:, NW * a:NW * a + NW]).then_inc(ada_b_in, 16)
                    gp.wait_ge(ada_rowed, a + 1)
                    gp.dma_start(mod_dram[NW * a:NW * a + NW].unsqueeze(0), ada_row[0:1]).then_inc(ada_stored, 16)
                    gp.wait_ge(ada_stored, 16 * a + 16)
                    if a == 5 * D // NW - 1:
                        for n, part in enumerate((1, 0, 4, 3)):
                            gp.dma_start(at(88, P)[16 * n:16 * n + 16], mod_dram[part * D:(part + 1) * D].rearrange(
                                "(k p) -> k p", p=P)).then_inc(sem("mod_in"), 16)
            ada_rows("mem")
            ada_rows("qkv")
            gp.wait_ge(sem("attn1_out"), 12)
            ada_rows("gates")
            gp.dma_start(X[:, :, :], t["x"].rearrange("(t p) n -> p t n", p=P)).then_inc(sem("x_again"), 16)
            ada_rows("w_o")
            ada_rows("ffn_in")
            gp.wait_ge(sem("x2_ready"), 4)
            gp.dma_start(x_dram, X[:, :, :].rearrange("p t n -> p (t n)")).then_inc(sem("x_away"), 16)
            gp.wait_ge(sem("x_away"), 16)
            gp.wait_ge(sem("turned"), 4 * TURN[3] + 4)
            gp.wait_ge(sem("norm_squares"), 8 * 4)
            gp.dma_start(X[:, 0, :].rearrange("p (n e) -> p n e", n=16),
                         t["lru_wa_2"].rearrange("n d e -> d n e")).then_inc(sem("lru_w_in"), 16)
            gp.dma_start(X[:, 1, :].rearrange("p (n e) -> p n e", n=16),
                         t["lru_wi_2"].rearrange("n d e -> d n e")).then_inc(sem("lru_w_in"), 16)
            for n, (w1, w2) in ((1, ("cmp_w1_v_2", "cmp_w2_v_2")), (0, ("cmp_w1_k_2", "cmp_w2_k_2"))):
                if n:
                    gp.wait_ge(sem("lru_gates"), 16)
                else:
                    gp.wait_ge(sem("lru_out"), 4)
                gp.dma_start(W1[n].rearrange("p (l e) -> p l e", l=32), t[w1].rearrange("l d e -> d l e")).then_inc(sem(f"cmp_in{n}"), 16)
                gp.dma_start(CMP_W2[:, n], t[w2]).then_inc(sem("cmp2_in"), 16)
            gp.wait_ge(sem("cmp_hid"), 2)
            gp.dma_start(X[:, 0, 0:2 * 527], t["masks_2"]).then_inc(sem("mask2_in"), 16)
            gp.wait_ge(sem("attn2_out"), 16)
            gp.dma_start(X[:, :, :].rearrange("p t n -> p (t n)"), x_dram).then_inc(sem("x_back"), 16)
            gp.dma_start(at(80, D), mod_dram[2 * D:3 * D].partition_broadcast(P)).then_inc(sem("g1_in"), 16)
            gp.wait_ge(xl_ready, READY["ffn_up"])
            gp.dma_start(at(0, D), mod_dram[5 * D:6 * D].partition_broadcast(P)).then_inc(sem("g2_in"), 16)
            gp.dma_start(at(8, D), t["final_g_2"].partition_broadcast(P)).then_inc(sem("final_g_in"), 16)
            for n in range(2 * NT):
                tt, half = n // 2, slice(D // 2 * (n % 2), D // 2 * (n % 2 + 1))
                gp.wait_ge(sem("final"), n + 1)
                gp.dma_start(out[tt * P:(tt + 1) * P, half], XN[:, tt, half]).then_inc(sem("out_stored"), 16)
            gp.wait_ge(sem("out_stored"), 16 * 2 * NT)

        def halves(nk):
            a = (nk + 1) // 2
            return ((0, a), (a, nk))

        def half_at(ph, g, h, i):
            return At(ph.H0 + 2 * g + h, ph.hpi, i)

        def epilogue_of(ph, j, i, first):
            if j > 0:
                return (i, j - 1)
            return None if first else (i - 1, len(ph.chunks) - 1)

        def products(eng, ph, tile, epilogue, ada=None, straight=False, side=None, prepared=0, tail=None):
            def body(i, first):
                g = 0
                for n, b in enumerate(ph.body):
                    T = At(ph.T0 + n, ph.tpi, i)
                    if b[0] == "a":
                        if ada:
                            ada("tile", i, (T, n % 4, b[1]))
                        continue
                    if not (first and g < prepared):
                        tile(i, T, n % 4, g, *b[1:])
                    g += 1
                    if ada and not first and g == 1:
                        ada("row", i - 1, None)
                    last = epilogue_of(ph, b[1], i, first) if b[2] == 0 else None
                    if last and epilogue:
                        epilogue(*last, *pair_of(ph, last[1], last[0]))
                    if side:
                        side(i, b[1], b[2])
            if straight:
                for i in range(ph.iters):
                    body(i, i == 0)
            else:
                run(eng, ph, body)
            end = (ph.iters - 1, len(ph.chunks) - 1)
            if tail:
                tail()
            if epilogue:
                epilogue(*end, *pair_of(ph, end[1], end[0]))
            if ada:
                ada("row", ph.iters - 1, None)

        def prepare(ph, tile, count, start):
            for g, (n, b) in list(enumerate([(n, b) for n, b in enumerate(ph.body) if b[0] == "g"]))[start:count]:
                tile(0, At(ph.T0 + n, ph.tpi, 0), n % 4, g, *b[1:])

        @block.scalar
        def _(act):
            def act_copy(out, in_, func=ACT.Copy, **kw):
                return nc.scalar.activation(out, in_, func, **kw)

            def tile(width=NW):
                def one(i, T, slot, g, j, tt, k0, nk):
                    ph = cur[0]
                    act.wait_ge(landed[slot], T.val(4, 16 - 4 * slot))
                    for h, (a, b) in enumerate(halves(nk)):
                        H = half_at(ph, g, h, i)
                        if not (isinstance(i, int) and H.val() < 4):
                            act.wait_ge(mm_half, H.val(1, -3))
                        act_copy(WH[:, (ph.H0 + 2 * g + h) % 4, 0:b - a, 0:width],
                                 raw[:, slot, a:b, 0:width]).then_inc(w_hi, 1)
                return one
            cur = [None]

            def phase(name, epilogue, straight=False, width=NW, side=None, prepared=0, tail=None):
                cur[0] = PH[name]
                products(act, PH[name], tile(width), epilogue, straight=straight, side=side, prepared=prepared, tail=tail)

            def ahead(name, count, start=0):
                now, cur[0] = cur[0], PH[name]
                prepare(PH[name], tile(), count, start)
                cur[0] = now

            done = [0]

            def squares(c):
                for tt in range(NT):
                    if done[0] >= 2:
                        act.wait_ge(sem("norm_squares"), done[0] - 1)
                    done[0] += 1
                    act_copy(junk[:, tt], X[:, tt, NW * c:NW * c + NW], ACT.Square,
                             accum_out=stat[:, 4 * tt + c:4 * tt + c + 1]).then_inc(sem("norm_squares"), 1)

            def root(n):
                act.wait_ge(sem("norm_mean"), n + 1)
                act_copy(stat[:, 10:12], stat[:, 8:10], ACT.Sqrt).then_inc(sem("norm_root"), 1)

            def round_acts(name, done=None, base=0, src=XF, groups=range(4), shift=None):
                if PH[name].H0:
                    act.wait_ge(mm_half, PH[name].H0)
                for g in groups:
                    if done:
                        act.wait_ge(done, base + g + 1)
                    if shift is None:
                        act_copy(XH[:, 4 * g:4 * g + 4], src[:, 4 * g:4 * g + 4]).then_inc(xh_ready, 1)
                        continue
                    for k in range(4 * g, 4 * g + 4):
                        op = act_copy(XH[:, k], src[:, k], ACT.Identity, bias=shift[:, k:k + 1])
                    op.then_inc(xh_ready, 1)

            act.wait_ge(sem("cols_in"), 16)
            act_copy(cact, col("c_2"), ACT.Silu).then_inc(sem("c_ready"), 1)
            act.wait_ge(sem("mem_in"), 16)
            for c in range(4):
                squares(c)
            ahead("mem", 1)
            root(0)
            for h in range(6):
                act.wait_ge(sem("bias_mm"), h + 1)
                act_copy(at(16 + 2 * h, 512), acc[h % 2][:, h // 2 % 2, :]).then_inc(sem("bias_row"), 1)
            round_acts("mem", sem("acts"), 0)

            def to_tokens(dst, tiles=(0,)):
                def epilogue(i, j, p, used):
                    act.wait_ge(mm_half, chunk_done(cur[0], j, i))
                    for tt in tiles:
                        act_copy(dst(i, j, tt), acc[p][:, tt, :]).then_inc(acc_used[p], 1)
                return epilogue

            def x_squares(i, j, t):
                if j == 1:
                    if t == 0:
                        act.wait_ge(sem("x_in"), 16)
                    squares(t)
            phase("mem", to_tokens(lambda i, j, tt: (KC, VC)[j][:, tt, :]), straight=True, side=x_squares, prepared=1, tail=lambda: ahead("qkv", 1))
            root(1)
            round_acts("qkv", sem("acts"), 4)

            def heads_root(s):
                act.wait_ge(sem("heads_mean"), s + 1)
                n, h0 = HEADS[s][1].shape[2] // HD, HEADS[s][2]
                act_copy(HEAD_STATS[:, :, h0:h0 + n], HEAD_STATS[:, :, h0:h0 + n], ACT.Sqrt).then_inc(sem("heads_root"), 1)

            def heads_side(i, j, t):
                for s, start in enumerate(HEAD_TILE):
                    if 8 * i + 4 * j + t == start + 1:
                        heads_root(s)
            phase("qkv", to_tokens(lambda i, j, tt: Z[:, tt, NW * (2 * i + j):NW * (2 * i + j) + NW], range(NT)), straight=True,
                  side=heads_side, prepared=1)
            heads_root(6)
            ahead("gates", 1)

            def exps1(job):
                n, probs = (768 if job < 2 else 256), probs1(job)
                if job >= 4:
                    act.wait_ge(sem("attn1_turned"), job - 2 if job > 4 else 1)
                act.wait_ge(sem("attn1_max"), job + 1)
                for tt in range(NT):
                    st = 2 * (job % 3) + tt
                    src = probs[:, tt] if job < 2 else acc[tt][:, 0, 0:256]
                    act_copy(probs[:, tt], src, ACT.Exp, bias=amax1[:, st:st + 1],
                             accum_out=asum1[:, st:st + 1]).then_inc(sem("attn1_exp"), 1)

            exps1(0)
            exps1(1)
            for job in range(12):
                act.wait_ge(sem("attn1_turned"), job + 1)
                if job >= 2:
                    act.wait_ge(sem("attn1_mm"), job - 1)
                blocks = 6 if job < 2 else 2
                act_copy(PT1[:, job % 2, 0:min(blocks, 4), :], acc[2][:, :, :].rearrange("p a (b s) -> p (a b) s", b=2)[:, 0:min(blocks, 4)]).then_inc(sem("attn1_pt"), 1)
                if blocks > 4:
                    act_copy(PT1[:, job % 2, 4:6, :], acc[3][:, 0, :].rearrange("p (b s) -> p b s", b=2)).then_inc(sem("attn1_pt"), 1)
                if job + 2 < 12:
                    exps1(job + 2)
            act.wait_ge(sem("attn1_out"), 12)

            def gates(dst):
                def epilogue(i, j, p, used):
                    act.wait_ge(mm_half, chunk_done(cur[0], j, i))
                    for tt in range(NT):
                        act_copy(dst[:, tt, bass.ds(i * (2 * NW) + j * NW, NW)], acc[p][:, tt, :],
                                 ACT.Sigmoid).then_inc(acc_used[p], 1)
                return epilogue
            phase("gates", gates(SG), prepared=1, tail=lambda: [ahead("branch", 1), round_acts("branch", groups=range(3))])
            phase("branch", None, straight=True, prepared=1,
                  tail=lambda: [ahead("w_o", 1), round_acts("w_o", sem("xf_filled"), 4 * TURN["m1"], groups=range(3))])

            def residual_squares(i, j, t):
                c = 2 * i + j - 1
                if t == 1 and c >= 0:
                    p = (cur[0].C0 + c) % 2
                    act.wait_ge(acc_used[p], 2 * ((cur[0].C0 + c) // 2 + 1))
                    if cur[0].name == "w_out":
                        act.wait_ge(sem("x3_ready"), c + 1)
                    squares(c)

            def last_squares():
                residual_squares(2, 0, 1)
            def w_o_side(i, j, t):
                if (i, j, t) == (0, 0, 1):
                    round_acts("w_o", sem("xf_filled"), 4 * TURN["m1"], groups=(3,))
                residual_squares(i, j, t)
            phase("w_o", None, straight=True, side=w_o_side, prepared=1, tail=lambda: ahead("ffn_in", 1))
            last_squares()
            root(2)
            round_acts("ffn_in", sem("acts"), 8)

            def silu_gate(i, j, p, used):
                if j == 1:
                    return
                act.wait_ge(mm_half, chunk_done(cur[0], j, i))
                act.wait_ge(acc_used[1 - p], pair_of(cur[0], 1, i)[1].val(2, 0))
                act_copy(GT, acc[p][:, :, :].rearrange("p a (b s) -> p (a b) s", b=2), ACT.Silu).then_inc(acc_used[p], 2)

            def k_weights(ph, j, i):
                H = At(ph.H0 + 2 * j, 8, i)
                act.wait_ge(landed[j], At(ph.T0 + j, 4, i).val(4, 16 - 4 * j))
                for h in range(2):
                    act.wait_ge(mm_half, H.val(1, h - 3))
                    act_copy(WH[:, (ph.H0 + 2 * j + h) % 4], raw[:, j, 2 * h:2 * h + 2]).then_inc(w_hi, 1)
            phase("ffn_in", silu_gate, prepared=1, tail=lambda: k_weights(PH["ffn_out"], 0, 0))

            def k_outer(name):
                ph = PH[name]

                def body(i, first):
                    for j in range(4):
                        H = At(ph.H0 + 2 * j, 8, i)
                        act.wait_ge(mm_half, ph.H0 if first else H.val(1, -6))
                        act_copy(XH[:, j:j + 1], AT[:, bass.ds(i * 4 + j, 1), :]).then_inc(sem("hidden_rounded"), 1)
                        if not (first and j == 0):
                            k_weights(ph, j, i)
                    if first:
                        for p in range(2):
                            act.wait_ge(acc_used[p], 2 * c_end(before[name], p))
                for p in range(2):
                    act.wait_ge(acc_used[p], 2 * c_end(before[name], p) - 2)
                run(act, ph, body)
            before = {"ffn_out": "ffn_in", "ffn_down": "ffn_up"}
            k_outer("ffn_out")
            ahead("lru_x", 1)
            for c in range(4):
                act.wait_ge(sem("x2_ready"), c + 1)
                squares(c)
            root(3)
            round_acts("lru_x", sem("acts"), 12, shift=mod[:, 16:32])

            def to_features(dst, scale=1.0):
                def epilogue(i, j, p, used):
                    act.wait_ge(mm_half, chunk_done(cur[0], j, i))
                    act_copy(dst(i, j, 0), acc[p][:, 0, :].rearrange("p (b s) -> p b s", b=2), scale=scale).then_inc(acc_used[p], 1)
                return epilogue
            phase("lru_x", to_features(lambda i, j, b: LX[:, bass.ds(i * 8 + (4 * j + 2 * b), 2), :]), prepared=1,
                  tail=lambda: ahead("lru_y", 1))

            def gate_sigmoids(b, n):
                IT = IT2[b % 2]
                if b:
                    act.wait_ge(sem("lru_a"), 2 * b)
                if b >= 2:
                    act.wait_ge(sem("lru_h"), 4 * (b - 1))
                k = 4 * b + n
                act.wait_ge(sem("lru_gates"), k + 1)
                act_copy(RT[:, n], acc[2 + k % 2][:, 0, 0:S], ACT.Sigmoid, bias=col("lru_ba_2")[:, k:k + 1]).then_inc(sem("lru_r"), 1)
                act_copy(IT[:, n], acc[2 + k % 2][:, 0, S:2 * S], ACT.Sigmoid, bias=col("lru_bi_2")[:, k:k + 1]).then_inc(sem("lru_r"), 1)

            def lru_side(n):
                if n == 0:
                    act_copy(lamc[:, 0:16], col("lru_lambda_2"), ACT.Abs).then_inc(sem("lam_abs"), 1)
                    act.wait_ge(sem("lam_abs"), 1)
                    act_copy(lamc[:, 0:16], lamc[:, 0:16], ACT.Exp, scale=-1.0).then_inc(sem("lam_exp"), 1)
                    act.wait_ge(sem("lam_exp"), 1)
                    act_copy(lamc[:, 0:16], lamc[:, 0:16], ACT.Ln, bias=1.0).then_inc(sem("lam_log"), 1)
                for b in range(4):
                    step = n - 8 * b
                    if step in (4, 5):
                        gate_sigmoids(b, 2 * (step - 4))
                        gate_sigmoids(b, 2 * (step - 4) + 1)
                    if step == 7:
                        act.wait_ge(sem("lru_scaled"), b + 1)
                        if b:
                            act.wait_ge(sem("lru_b"), b)
                        act_copy(TT, RT, ACT.Tanh).then_inc(sem("lru_tanh"), 1)
                        act_copy(LX[:, 4 * b:4 * b + 4], RT, ACT.Exp, scale=-1.0).then_inc(sem("lru_a"), 1)
                        act.wait_ge(sem("lru_iu"), b + 1)
                        act_copy(UT2[b % 2], RT, ACT.Exp, scale=-2.0).then_inc(sem("lru_a"), 1)
                    if step == 9:
                        act.wait_ge(sem("lru_one_minus"), b + 1)
                        act_copy(TT, TT, ACT.Sqrt).then_inc(sem("lru_sqrt"), 1)
                    if step == 11:
                        c = PH["lru_y"].C0 + b
                        act.wait_ge(acc_used[c % 2], 2 * (c // 2 + 1))
                        act_copy(LY[:, 4 * b:4 * b + 4], LY[:, 4 * b:4 * b + 4], ACT.Gelu_apprx_tanh).then_inc(sem("lru_gelu"), 1)
                if n == 39:
                    act.wait_ge(sem("lru_out"), 4)
                if n == 51:
                    for m in range(2):
                        act.wait_ge(sem("cmp_hid"), m + 1)
                        act_copy(CMP_HID[:, m, 0:60], acc[2 + m][:, 1, 0:60], ACT.Gelu_apprx_tanh).then_inc(sem("cmp_gelu"), 1)
                if n == 54:
                    act.wait_ge(sem("cmp_done"), 1)
                    act_copy(KCMP[:, 0:60], acc[2][:, 1, 64:124]).then_inc(sem("cmp_kept"), 1)
                    act.wait_ge(sem("cmp_done"), 2)
                    act_copy(VCMP[0:15, :], acc[3][0:15, 1, :]).then_inc(sem("cmp_kept"), 1)

            def under(name):
                return lambda i, j, t: lru_side(SIDE0[name] + 8 * i + 4 * j + t)
            phase("lru_y", to_features(lambda i, j, b: LY[:, 8 * i + 4 * j + 2 * b:8 * i + 4 * j + 2 * b + 2]), straight=True,
                  side=under("lru_y"), prepared=1, tail=lambda: ahead("q2", 1))
            phase("q2", to_features(lambda i, j, b: Q2[:, 8 * i + 4 * j + 2 * b:8 * i + 4 * j + 2 * b + 2], SCALE), straight=True,
                  side=under("q2"), prepared=1, tail=lambda: ahead("kv2", 1))
            act.wait_ge(ada_stored, 16 * ADA_CHUNKS)
            kv_dst = [(KC2, 0), (VC2, 0), (KS2, 0), (VS2, 1), (KW2, 0), (VW2, 1)]

            def kv_epilogue(i, j, p, used):
                dst, token = kv_dst[2 * i + j]
                if token:
                    to_tokens(lambda i, j, tt: dst[:, tt, :])(i, j, p, used)
                else:
                    to_features(lambda i, j, b: dst[:, 2 * b:2 * b + 2, :])(i, j, p, used)
            phase("kv2", kv_epilogue, straight=True, side=under("kv2"), prepared=1)

            def g48_epilogue(i, j, p, used):
                act.wait_ge(mm_half, chunk_done(cur[0], j, i))
                act_copy(GATE_ROWS, acc[p][0:48, 0, 0:S], ACT.Sigmoid).then_inc(acc_used[p], 2)
            phase("g48", g48_epilogue, width=48)
            def exps2(job):
                bb = job % 3
                act.wait_ge(sem("attn2_max"), job + 1)
                for tt in range(NT):
                    for seg, (lo, hi) in enumerate(SEG):
                        st = 12 * bb + 3 * tt + seg
                        act_copy(P2[:, bb, tt, lo:hi], P2[:, bb, tt, lo:hi], ACT.Exp, bias=smx[:, st:st + 1],
                                 accum_out=smx[:, st + 6:st + 7]).then_inc(sem("attn2_exp"), 1)

            exps2(0)
            exps2(1)
            for job in range(16):
                bb = job % 2
                act.wait_ge(sem("attn2_turned"), job + 1)
                if job >= 2:
                    act.wait_ge(sem("attn2_mm"), job - 1)
                act_copy(PT2[:, bb], acc[2][:, :, :].rearrange("p a (b s) -> p (a b) s", b=2)).then_inc(sem("attn2_pt"), 1)
                act_copy(PC2[0:15, bb], acc[3][0:15, 0, 0:S]).then_inc(sem("attn2_pt"), 1)
                if job + 2 < 16:
                    exps2(job + 2)
                if job == 11:
                    ahead("gates2", 2)
            act.wait_ge(sem("attn2_out"), 16)
            phase("gates2", gates(SG2), prepared=2, tail=lambda: [ahead("proj_a", 1), round_acts("proj_a", src=Q2)])
            phase("proj_a", None, prepared=1, tail=lambda: [ahead("proj_b", 1), round_acts("proj_b", src=LX)])
            phase("proj_b", None, prepared=1,
                  tail=lambda: [ahead("w_out", 1), round_acts("w_out", sem("xf_filled"), 4 * TURN["m2"], groups=range(3))])

            def w_out_side(i, j, t):
                if (i, j, t) == (0, 0, 1):
                    round_acts("w_out", sem("xf_filled"), 4 * TURN["m2"], groups=(3,))
                residual_squares(i, j, t)
            phase("w_out", None, straight=True, side=w_out_side, prepared=1, tail=lambda: ahead("ffn_up", 1))
            last_squares()
            root(4)
            round_acts("ffn_up", sem("acts"), 16, shift=mod[:, 48:64])

            def gelu_gate(i, j, t):
                if (j, t) == (1, 2):
                    p, used = pair_of(cur[0], 0, i)
                    act.wait_ge(acc_used[p], used.val(2, 2))
                    act_copy(GT, CV, ACT.Gelu_apprx_tanh).then_inc(sem("gate_ready"), 1)
            phase("ffn_up", None, side=gelu_gate, prepared=1, tail=lambda: k_weights(PH["ffn_down"], 0, 0))
            k_outer("ffn_down")
            for c in range(4):
                act.wait_ge(sem("x4_ready"), c + 1)
                squares(c)
            root(5)

        @block.vector
        def _(dve):
            v = nc.vector
            cur = [None]

            def tile(width=NW):
                def one(i, T, slot, g, j, tt, k0, nk):
                    ph = cur[0]
                    last = None
                    for h, (a, b) in enumerate(halves(nk)):
                        H = half_at(ph, g, h, i)
                        dve.wait_ge(w_hi, H.val(1, 1))
                        ring = (2 * ((ph.H0 // 2 + g) % 2) + h) % 4
                        last = v.tensor_tensor(WL[:, ring, 0:b - a, 0:width], raw[:, slot, a:b, 0:width],
                                               WH[:, ring, 0:b - a, 0:width].bitcast(F32), ALU.subtract)
                        last.then_inc(w_lo, 1)
                return one

            def ada(what, i, arg):
                ph = cur[0]
                ada_acc, ada_row, ada_brow = ada_place(ph.name)
                a = At(ph.A0, 1, i)
                if what == "row":
                    dve.wait_ge(ada_red, a.val(1, 1))
                    dve.wait_ge(ada_b_in, a.val(16, 16))
                    v.tensor_tensor(ada_row[0:1], acc[2][0:1, 0, :], ada_brow[0:1], ALU.add).then_inc(ada_rowed, 1)
                    return
                T, slot, q = arg
                dve.wait_ge(landed[slot], T.val(4, 16 - 4 * slot))
                for kk in range(4):
                    n = 4 * q + kk
                    count = a.val(16, n)
                    if n < 2:
                        if not (isinstance(i, int) and a.val() == 0):
                            dve.wait_ge(ada_red, a.val(1, 0))
                        v.tensor_scalar(ada_acc[:, n % 2], raw[:, slot, kk], cact[:, n:n + 1], None, ALU.mult).then_inc(ada_mac, 1)
                    else:
                        dve.wait_ge(ada_mac, a.val(16, n - 1))
                        v.scalar_tensor_tensor(ada_acc[:, n % 2], raw[:, slot, kk], cact[:, n:n + 1], ada_acc[:, n % 2],
                                               ALU.mult, ALU.add).then_inc(ada_mac, 1)

            def phase(name, epilogue, straight=False, width=NW, side=None, prepared=0, tail=None):
                cur[0] = PH[name]
                products(dve, PH[name], tile(width), epilogue, ada=ada if PH[name].ada else None, straight=straight,
                         side=side, prepared=prepared, tail=tail)

            def ahead(name, count, start=0):
                now, cur[0] = cur[0], PH[name]
                prepare(PH[name], tile(), count, start)
                cur[0] = now

            def rest(ready, g, src=XF, shift=None):
                dve.wait_ge(xh_ready, ready + g + 1)
                if shift is not None:
                    for k in range(4 * g, 4 * g + 4):
                        op = v.scalar_tensor_tensor(XL[:, k], src[:, k], shift[:, k:k + 1], XH[:, k].bitcast(F32), ALU.add, ALU.subtract)
                    op.then_inc(xl_ready, 1)
                    return
                v.tensor_tensor(XL[:, 4 * g:4 * g + 4], src[:, 4 * g:4 * g + 4], XH[:, 4 * g:4 * g + 4].bitcast(F32),
                                ALU.subtract).then_inc(xl_ready, 1)

            def fill(n, g, gain=None):
                dve.wait_ge(sem("turned"), 4 * TURN[n] + g + 1)
                src = acc[TURN_PAIRS[n][g % 2]][:, :, :].rearrange("p a (b s) -> p (a b) s", b=2)
                if gain is None:
                    v.tensor_copy(XF[:, 4 * g:4 * g + 4], src).then_inc(sem("xf_filled"), 1)
                else:
                    v.tensor_tensor(XF[:, 4 * g:4 * g + 4], src, bc(gain[:, 4 * g:4 * g + 4], [P, 4, S]), ALU.mult).then_inc(sem("xf_filled"), 1)

            def norm_mean(n):
                dve.wait_ge(sem("norm_squares"), 8 * (n + 1))
                v.tensor_reduce(stat[:, 12:14], stat[:, 0:8].rearrange("p (t c) -> p t c", t=NT), AX.X, ALU.add).then_inc(sem("norm_sum"), 1)
                dve.wait_ge(sem("norm_sum"), n + 1)
                v.tensor_scalar(stat[:, 8:10], stat[:, 12:14], 1.0 / D, EPS, ALU.mult, ALU.add).then_inc(sem("norm_mean"), 1)

            def norm_tail(n, ready, shift=None):
                dve.wait_ge(sem("norm_root"), n + 1)
                v.reciprocal(stat[:, 12:14], stat[:, 10:12]).then_inc(sem("norm_inverse"), 1)
                dve.wait_ge(sem("norm_inverse"), n + 1)
                v.tensor_copy(root_wide, bc(stat[:, 12:14], [P, NT, P])).then_inc(sem("norm_rows"), 1)
                dve.wait_ge(sem("norm_spread"), n + 1)
                by_token = acc[2][:, 1, 0:S].unsqueeze(1).broadcast_to([P, 4, S])
                for g in range(4):
                    x = XF[:, 4 * g:4 * g + 4]
                    dve.wait_ge(sem("xf_filled"), 4 * TURN[n] + g + 1)
                    v.tensor_tensor(x, x, by_token, ALU.mult).then_inc(sem("acts"), 1)
                    if g:
                        rest(ready, g - 1, shift=shift)
                rest(ready, 3, shift=shift)

            dve.wait_ge(sem("bias_in"), 32)
            v.tensor_copy(at(76, 768)[0:32].rearrange("p (h q) -> p h q", h=6), bc(at(32, 6)[0:32], [32, 6, P])).then_inc(sem("bias_wide"), 1)
            dve.wait_ge(sem("cols_in"), 16)
            for g in range(4):
                fill(0, g, col("g_mem"))
            norm_mean(0)
            ahead("mem", 1)
            norm_tail(0, 0)
            dve.wait_ge(sem("small_set"), 2)
            dve.wait_ge(sem("cols_in"), 16)
            for dst, name, n, s in ((0, "g_qa", 6, SCALE), (6, "g_ka", 6, 1.0), (20, "g_qc", 4, SCALE), (24, "g_kc", 4, 1.0)):
                v.tensor_scalar(gq[:, dst:dst + n], col(name).broadcast_to([P, n]), s, None, ALU.mult).then_inc(sem("head_gain"), 1)
            v.tensor_scalar(gq[:, 12:18], one1.broadcast_to([P, 6]), SCALE, None, ALU.mult).then_inc(sem("head_gain"), 1)

            def bias_masks():
                dve.wait_ge(sem("bias_back"), 16 * 12)
                dve.wait_ge(sem("mask_in"), 16)
                mk = at(36, 6 * S).rearrange("p (t g s) -> p t g s", t=2, g=3)
                for j in range(2):
                    for tt in range(NT):
                        v.tensor_tensor(BI[:, j, tt], BI[:, j, tt], mk[:, tt], ALU.add).then_inc(sem("bias_ready"), 1)

            def to_tokens(dst):
                def epilogue(i, j, p, used):
                    dve.wait_ge(mm_half, chunk_done(cur[0], j, i))
                    v.tensor_copy(dst(i, j, 1), acc[p][:, 1, :]).then_inc(acc_used[p], 1)
                return epilogue
            dve.wait_ge(sem("c_ready"), 1)
            dve.wait_ge(xl_ready, 4)
            def mem_side(i, j, t):
                n = 4 * j + t
                if n in (3, 5, 7):
                    fill(1, (n - 3) // 2, col("g_mix"))
                if n == 6:
                    bias_masks()
            phase("mem", to_tokens(lambda i, j, tt: (KC, VC)[j][:, tt, :]), straight=True, prepared=1, side=mem_side,
                  tail=lambda: ahead("qkv", 1))

            norm_mean(1)
            fill(1, 3, col("g_mix"))
            norm_tail(1, READY["mem"])
            def by_head(rows):
                return rows.rearrange("p t (h d) -> p t h d", d=HD)

            def heads_mean(s):
                done_at, rows, h0 = HEADS[s]
                z = by_head(rows)
                n = rows.shape[2] // HD
                if s:
                    c = PH["qkv"].C0 + done_at
                    dve.wait_ge(acc_used[c % 2], 2 * (c // 2 + 1))
                    dve.wait_ge(sem("hd_sum"), s)
                sq = X[:, 1, 0:2 * n * HD].rearrange("p (t h d) -> p t h d", t=NT, h=n)
                v.tensor_tensor(sq, z, z, ALU.mult).then_inc(sem("hd_sq"), 1)
                dve.wait_ge(sem("hd_sq"), s + 1)
                stats = HEAD_STATS[:, :, h0:h0 + n]
                v.tensor_reduce(stats, sq, AX.X, ALU.add).then_inc(sem("hd_sum"), 1)
                dve.wait_ge(sem("hd_sum"), s + 1)
                v.tensor_scalar(stats, stats, 1.0 / HD, EPS, ALU.mult, ALU.add).then_inc(sem("heads_mean"), 1)

            def heads_scale(s):
                _, rows, h0 = HEADS[s]
                n = rows.shape[2] // HD
                stats = HEAD_STATS[:, :, h0:h0 + n]
                dve.wait_ge(sem("heads_root"), s + 1)
                v.reciprocal(stats, stats).then_inc(sem("heads_inverse"), 1)
                dve.wait_ge(sem("heads_inverse"), s + 1)
                z = by_head(rows)
                v.tensor_tensor(z, z, stats.unsqueeze(3).broadcast_to([P, NT, n, HD]), ALU.mult).then_inc(sem("heads_scaled"), 1)

            def rope_gain(s, gain):
                z = by_head(HEADS[s][1])
                n = HEADS[s][1].shape[2] // HD
                dve.wait_ge(sem("heads_scaled"), s + 1)
                dve.wait_ge(sem("rope_in"), 48)
                v.tensor_tensor(z, z, gain.unsqueeze(1).unsqueeze(1).broadcast_to([P, NT, n, HD]), ALU.mult).then_inc(sem("rope_gain"), 1)

            def rope_heads(tt):
                rope = ROPE[:, 0:256].rearrange("p (t c f) -> p t c f", t=2, c=2)
                z = Z[:, tt, 2304:3328].rearrange("p (h f c) -> p c h f", h=8, c=2)
                x0, x1 = z[:, 0], z[:, 1]
                cs = rope[:, tt, 0].unsqueeze(1).broadcast_to([P, 8, 64])
                sn = rope[:, tt, 1].unsqueeze(1).broadcast_to([P, 8, 64])
                w = [at(2 + 2 * k, 512).rearrange("p (h f) -> p h f", h=8) for k in range(4)]
                if tt:
                    dve.wait_ge(sem("roped"), 2)
                else:
                    dve.wait_ge(sem("rope_gain"), 2)
                for k, (a, b) in enumerate(((x0, cs), (x1, sn), (x0, sn), (x1, cs))):
                    v.tensor_tensor(w[k], a, b, ALU.mult).then_inc(sem("rope_part"), 1)
                dve.wait_ge(sem("rope_part"), 4 * tt + 4)
                v.tensor_tensor(x0, w[0], w[1], ALU.subtract).then_inc(sem("roped"), 1)
                v.tensor_tensor(x1, w[2], w[3], ALU.add).then_inc(sem("roped"), 1)

            def heads_fetch(n):
                g = HEAD_GROUPS[n]
                dve.wait_ge(sem("heads_turned"), n + 1)
                v.tensor_tensor(QK[:, 4 * g:4 * g + 4], acc[HEAD_PAIR[n]][:, :, :].rearrange("p a (b s) -> p (a b) s", b=2),
                                bc(gq[:, 4 * g:4 * g + 4], [P, 4, S]), ALU.mult).then_inc(sem("heads_ready"), 1)

            def heads_side(i, j, t):
                c = 2 * i + j
                for s, start in enumerate(HEAD_TILE):
                    if 4 * c + t == start:
                        heads_mean(s)
                    if 4 * c + t == start + 2:
                        heads_scale(s)
                if t == 3 and 1 <= c <= 4:
                    if c == 1:
                        dve.wait_ge(ada_stored, 16)
                        dve.wait_ge(sem("head_gain"), 5)
                    heads_fetch(c - 1)
                if t == 3 and c in (6, 7):
                    rope_gain(c - 2, ROPE[:, 256:384] if c == 6 else ROPE[:, 384:512])
            phase("qkv", None, straight=True,
                  side=heads_side, prepared=1)
            heads_mean(6)
            def finish1(job):
                b, probs = job % 3, probs1(job)
                dve.wait_ge(sem("attn1_exp"), 2 * job + 2)
                r = asum1[:, 2 * b:2 * b + 2]
                v.reciprocal(r, r).then_inc(sem("attn1_inverse"), 1)
                dve.wait_ge(sem("attn1_inverse"), job + 1)
                v.tensor_tensor(probs, probs, bc(r, [P, NT, 768 if job < 2 else 256]), ALU.mult).then_inc(sem("attn1_probs"), 1)

            def out1(job):
                dve.wait_ge(sem("attn1_mm"), job + 1)
                v.tensor_copy(XF[:, JOB_OUT[job]], acc[3][:, 1, 0:S]).then_inc(sem("attn1_out"), 1)

            def top1(job):
                b = job % 3
                mx = amax1[:, 2 * b:2 * b + 2]
                for tt in range(NT):
                    u = 2 * job + tt
                    dve.wait_ge(sem("attn1_scores"), u + 1)
                    if job < 2:
                        sc = probs1(job)[:, tt]
                        v.tensor_tensor(sc, acc[tt][:, :, :].rearrange("p a s -> p (a s)")[:, 0:768],
                                        BI[:, job, tt].rearrange("p g s -> p (g s)"), ALU.add).then_inc(sem("attn1_biased"), 1)
                        dve.wait_ge(sem("attn1_biased"), u + 1)
                    else:
                        sc = acc[tt][:, 0, 0:256]
                    v.tensor_reduce(mx[:, tt:tt + 1], sc, AX.X, ALU.max).then_inc(sem("attn1_top"), 1)
                dve.wait_ge(sem("attn1_top"), 2 * job + 2)
                v.tensor_scalar(mx, mx, -1.0, None, ALU.mult).then_inc(sem("attn1_max"), 1)

            top1(0)
            heads_scale(6)
            top1(1)
            heads_fetch(4)
            for job in range(12):
                if job == 1:
                    dve.wait_ge(ada_stored, 16 * (PH["qkv"].A0 + PH["qkv"].iters))
                    rope_heads(0)
                if job == 2:
                    rope_heads(1)
                if job == 6:
                    ahead("gates", 1)
                finish1(job)
                if job >= 2 and job != 4:
                    out1(job - 2)
                if job == 3:
                    out1(2)
                    heads_fetch(5)
                    heads_fetch(6)
                if job + 2 < 12:
                    top1(job + 2)
            out1(10)
            out1(11)
            phase("gates", None, prepared=1, tail=lambda: [ahead("branch", 1)] + [rest(READY["gates"], g) for g in range(3)])

            def branch_epilogue(i, j, p, used):
                dve.wait_ge(mm_half, chunk_done(cur[0], j, i))
                gate = SG[:, :, D * j + NW * i:D * j + NW * i + NW]
                dst = M[:, :, NW * i:NW * i + NW]
                if j == 0:
                    v.tensor_tensor(dst, acc[p][:, :, :], gate, ALU.mult).then_inc(acc_used[p], 2)
                    return
                v.tensor_tensor(gate, acc[p][:, :, :], gate, ALU.mult).then_inc(acc_used[p], 2)
                dve.wait_ge(acc_used[p], used.val(2, 2))
                v.tensor_tensor(dst, dst, gate, ALU.add).then_inc(sem("merging1"), 1)
                dve.wait_ge(sem("merging1"), 2 * i + j)

            def merged_fill(n):
                def side(i, j, t):
                    if i and (j, t) == (2, 0):
                        fill(n, i - 1)
                return side
            phase("branch", branch_epilogue, straight=True, prepared=1, side=merged_fill("m1"),
                  tail=lambda: [ahead("w_o", 1), rest(READY["branch"], 0), rest(READY["branch"], 1)])

            def residual(name, gain=None):
                def epilogue(i, j, p, used):
                    dve.wait_ge(mm_half, chunk_done(cur[0], j, i))
                    x = X[:, :, bass.ds(i * (2 * NW) + j * NW, NW)]
                    if gain is not None:
                        tmp = at(88, 2 * NW).rearrange("p (t n) -> p t n", t=NT)
                        gb = gain(i, j)
                        if not (isinstance(i, int) and i == 0 and j == 0):
                            dve.wait_ge(sem(name), i * 2 + j)
                        v.tensor_tensor(tmp, acc[p][:, :, :], gb, ALU.mult).then_inc(acc_used[p], 2)
                        dve.wait_ge(acc_used[p], used.val(2, 2))
                        v.tensor_tensor(x, x, tmp, ALU.add).then_inc(sem(name), 1)
                        return
                    v.tensor_tensor(x, x, acc[p][:, :, :], ALU.add).then_inc(acc_used[p], 2)
                return epilogue
            dve.wait_ge(sem("x_again"), 16)

            def residual_fill(n, gain):
                def side(i, j, t):
                    c = 2 * i + j - 1
                    if t == 3 and c >= 0:
                        fill(n, c, gain)
                return side

            def w_o_side(i, j, t):
                if (i, j, t) == (0, 0, 1):
                    rest(READY["branch"], 2)
                    fill("m1", 3)
                    rest(READY["branch"], 3)
                residual_fill(2, col("g_ffn"))(i, j, t)
            phase("w_o", residual("x1_ready"), straight=True, side=w_o_side, prepared=1,
                  tail=lambda: ahead("ffn_in", 1))
            norm_mean(2)
            fill(2, 3, col("g_ffn"))
            norm_tail(2, READY["w_o"])

            def hidden(p, i, j, used):
                dve.wait_ge(mm_half, chunk_done(cur[0], j, i))
                src = acc[p][:, :, :].rearrange("p a (b s) -> p (a b) s", b=2)
                v.tensor_tensor(AT[:, bass.ds(i * 4, 4), :], GT, src, ALU.mult).then_inc(acc_used[p], 2)

            def swiglu(i, j, p, used):
                if j == 0:
                    return
                dve.wait_ge(acc_used[1 - p], pair_of(PH["ffn_in"], 0, i)[1].val(2, 2))
                hidden(p, i, j, used)

            def k_weights(ph, j, i):
                for h in range(2):
                    ring = (ph.H0 + 2 * j + h) % 4
                    dve.wait_ge(w_hi, At(ph.H0 + 2 * j + h, 8, i).val(1, 1))
                    v.tensor_tensor(WL[:, ring], raw[:, j, 2 * h:2 * h + 2], WH[:, ring].bitcast(F32), ALU.subtract).then_inc(w_lo, 1)
            phase("ffn_in", swiglu, prepared=1, tail=lambda: k_weights(PH["ffn_out"], 0, 0))

            def k_outer(name, base):
                ph = PH[name]

                def body(i, first):
                    for j in range(4):
                        dve.wait_ge(sem("hidden_rounded"), At(base + j, 4, i).val(1, 1))
                        v.tensor_tensor(XL[:, j:j + 1], AT[:, bass.ds(i * 4 + j, 1), :], XH[:, j:j + 1].bitcast(F32), ALU.subtract).then_inc(sem("hidden_rest"), 1)
                        if not (first and j == 0):
                            k_weights(ph, j, i)
                run(dve, ph, body)

            dve.wait_ge(sem("mod_turned"), 1)
            v.tensor_copy(mod, acc[2][:, 1, 0:64]).then_inc(sem("mod_copied"), 1)
            dve.wait_ge(sem("mod_copied"), 1)
            for n, g in ((0, "norm1_g_2"), (2, "norm2_g_2")):
                m = mod[:, 16 * n:16 * n + 16]
                v.scalar_tensor_tensor(m, m, 1.0, col(g), ALU.add, ALU.mult).then_inc(sem("mod_ready"), 1)
            dve.wait_ge(sem("mod_ready"), 2)
            k_outer("ffn_out", 0)
            ahead("lru_x", 1)
            for n in range(4):
                dve.wait_ge(mm_half, PH["ffn_out"].H0 + PH["ffn_out"].hpi * PH["ffn_out"].iters - (n < 2))
                v.tensor_tensor(X[:, :, NW * n:NW * n + NW], X[:, :, NW * n:NW * n + NW], acc[n][:, :, :], ALU.add).then_inc(sem("x2_ready"), 1)
            for g in range(3):
                fill(3, g, mod[:, 0:16])
            norm_mean(3)
            fill(3, 3, mod[:, 0:16])
            norm_tail(3, READY["ffn_in"], mod[:, 16:32])

            def to_features(dst, scale=1.0):
                def epilogue(i, j, p, used):
                    dve.wait_ge(mm_half, chunk_done(cur[0], j, i))
                    src = acc[p][:, 1, :].rearrange("p (b s) -> p b s", b=2)
                    if scale != 1.0:
                        v.tensor_scalar(dst(i, j, 1), src, scale, None, ALU.mult).then_inc(acc_used[p], 1)
                    else:
                        v.tensor_copy(dst(i, j, 1), src).then_inc(acc_used[p], 1)
                return epilogue
            phase("lru_x", to_features(lambda i, j, b: LX[:, bass.ds(i * 8 + (4 * j + 2 * b), 2), :]), prepared=1,
                  tail=lambda: ahead("lru_y", 1))

            cw = col("lru_conv_w_2")

            def lru_conv(b, tap):
                UT = UT2[b % 2]
                if tap == 0:
                    dve.wait_ge(acc_used[0], 2 * c_end("lru_x", 0))
                    dve.wait_ge(acc_used[1], 2 * c_end("lru_x", 1))
                    if b >= 2:
                        dve.wait_ge(sem("lru_out"), b - 1)
                for n in range(4):
                    k = 4 * b + n
                    if tap == 0:
                        v.tensor_scalar(UT[:, n], LX[:, k], cw[:, 48 + k:49 + k], col("lru_conv_b_2")[:, k:k + 1],
                                        ALU.mult, ALU.add).then_inc(sem("conv_tap"), 1)
                    else:
                        dve.wait_ge(sem("conv_tap"), 16 * b + 4 * (tap - 1) + n + 1)
                        v.scalar_tensor_tensor(UT[:, n, tap:S], LX[:, k, 0:S - tap], cw[:, 16 * (3 - tap) + k:16 * (3 - tap) + k + 1],
                                               UT[:, n, tap:S], ALU.mult, ALU.add).then_inc(sem("conv_tap"), 1)

            def lru_side(n):
                if n == 4:
                    v.tensor_scalar(lamc[:, 16:32], col("lru_lambda_2"), 0.0, None, ALU.min).then_inc(sem("lam_min"), 1)
                    dve.wait_ge(sem("lam_min"), 1)
                    dve.wait_ge(sem("lam_log"), 1)
                    v.tensor_tensor(lamc[:, 0:16], lamc[:, 0:16], lamc[:, 16:32], ALU.subtract).then_inc(sem("lam_sub"), 1)
                    dve.wait_ge(sem("lam_sub"), 1)
                    v.tensor_scalar(lamc[:, 0:16], lamc[:, 0:16], 8.0, None, ALU.mult).then_inc(sem("lam_ready"), 1)
                    dve.wait_ge(sem("lam_ready"), 1)
                if n in (38, 39, 41, 42):
                    m, half = (0, n - 38) if n < 40 else (1, n - 41)
                    kv, pos = ((KC2, "cmp_pos_k_2"), (VC2, "cmp_pos_v_2"))[m]
                    c = PH["kv2"].C0 + m
                    dve.wait_ge(acc_used[c % 2], 2 * (c // 2 + 1))
                    v.tensor_tensor(BLOCKS[:, m, half].rearrange("p (w l) -> p w l", l=16), kv[:, :, :].rearrange("p g (w l) -> p (g w) l", l=16),
                                    col(pos)[:, 16 * half:16 * half + 16].unsqueeze(1).broadcast_to([P, 64, 16]),
                                    ALU.add).then_inc(sem("cmp_blocks"), 1)
                for b in range(4):
                    IT, UT, AA = IT2[b % 2], UT2[b % 2], LX[:, 4 * b:4 * b + 4]
                    step = n - 8 * b
                    if 0 <= step < 4:
                        lru_conv(b, step)
                    if step == 6:
                        dve.wait_ge(sem("lru_r"), 8 * b + 8)
                        v.tensor_tensor(RT, RT, bc(lamc[:, 4 * b:4 * b + 4], [P, 4, S]), ALU.mult).then_inc(sem("lru_scaled"), 1)
                        v.tensor_tensor(IT, IT, UT, ALU.mult).then_inc(sem("lru_iu"), 1)
                    if step == 8:
                        dve.wait_ge(sem("lru_tanh"), b + 1)
                        dve.wait_ge(sem("lru_a"), 2 * b + 2)
                        v.scalar_tensor_tensor(TT, UT, 1.0, TT, ALU.add, ALU.mult).then_inc(sem("lru_one_minus"), 1)
                    if step == 10:
                        dve.wait_ge(sem("lru_iu"), b + 1)
                        dve.wait_ge(sem("lru_sqrt"), b + 1)
                        v.tensor_tensor(IT, IT, TT, ALU.mult).then_inc(sem("lru_b"), 1)
                    if step == 12:
                        dve.wait_ge(sem("lru_b"), b + 1)
                        for m in range(4):
                            v.tensor_tensor_scan(UT[:, m], AA[:, m], IT[:, m], 0.0, ALU.mult, ALU.add).then_inc(sem("lru_h"), 1)
                    if step == 13:
                        dve.wait_ge(sem("lru_h"), 4 * b + 4)
                        dve.wait_ge(sem("lru_gelu"), b + 1)
                        v.tensor_tensor(AA, UT, LY[:, 4 * b:4 * b + 4], ALU.mult).then_inc(sem("lru_out"), 1)

            def under(name):
                return lambda i, j, t: lru_side(SIDE0[name] + 8 * i + 4 * j + t)
            phase("lru_y", to_features(lambda i, j, b: LY[:, 8 * i + 4 * j + 2 * b:8 * i + 4 * j + 2 * b + 2]), straight=True,
                  side=under("lru_y"), prepared=1, tail=lambda: ahead("q2", 1))
            phase("q2", to_features(lambda i, j, b: Q2[:, 8 * i + 4 * j + 2 * b:8 * i + 4 * j + 2 * b + 2], SCALE), straight=True,
                  side=under("q2"), prepared=1, tail=lambda: ahead("kv2", 1))
            dve.wait_ge(ada_stored, 16 * ADA_CHUNKS)
            kv_dst = [(KC2, 0), (VC2, 0), (KS2, 0), (VS2, 1), (KW2, 0), (VW2, 1)]

            def kv_epilogue(i, j, p, used):
                dst, token = kv_dst[2 * i + j]
                if token:
                    to_tokens(lambda i, j, tt: dst[:, tt, :])(i, j, p, used)
                else:
                    to_features(lambda i, j, b: dst[:, 2 * b:2 * b + 2, :])(i, j, p, used)
            phase("kv2", kv_epilogue, straight=True, side=under("kv2"), prepared=1)
            phase("g48", None, width=48)
            dve.wait_ge(sem("mask2_in"), 16)
            dve.wait_ge(sem("gates48_turned"), 1)
            v.tensor_copy(G48[:, :, :], acc[3][:, 0, 0:96].rearrange("p (t n) -> p t n", t=NT)).then_inc(sem("gates48_kept"), 1)
            dve.wait_ge(sem("gates48_kept"), 1)
            dve.wait_ge(sem("lru_out"), 4)
            mk = X[:, 0, 0:2 * 527].rearrange("p (t n) -> p t n", t=2)
            stats2 = smx.rearrange("p (b w t g) -> p b w t g", b=3, w=2, t=2)
            wide2 = P2[:, :, :, 0:512].rearrange("p b t (g s) -> p b t g s", g=2)

            def mask2(job):
                bb = job % 3
                if job >= 3:
                    dve.wait_ge(sem("attn2_turned"), job - 2)
                for tt in range(NT):
                    dve.wait_ge(sem("attn2_scores"), 2 * job + tt + 1)
                    v.tensor_tensor(P2[:, bb, tt], acc[tt][:, :, :].rearrange("p a s -> p (a s)")[:, 0:527], mk[:, tt], ALU.add).then_inc(sem("attn2_masked"), 1)
                dve.wait_ge(sem("attn2_masked"), 2 * job + 2)
                v.tensor_reduce(stats2[:, bb, 0, :, 1:3], wide2[:, bb], AX.X, ALU.max).then_inc(sem("attn2_top"), 1)
                v.tensor_reduce(stats2[:, bb, 0, :, 0:1], P2[:, bb, :, 512:527].unsqueeze(2), AX.X, ALU.max).then_inc(sem("attn2_top"), 1)
                dve.wait_ge(sem("attn2_top"), 2 * job + 2)
                top = smx[:, 12 * bb:12 * bb + 6]
                v.tensor_scalar(top, top, -1e25, -1.0, ALU.max, ALU.mult).then_inc(sem("attn2_max"), 1)

            def finish2(job):
                bb = job % 3
                dve.wait_ge(sem("attn2_exp"), 6 * job + 6)
                r = smx[:, 12 * bb + 6:12 * bb + 12]
                v.tensor_scalar(r, r, 1e-30, None, ALU.max).then_inc(sem("attn2_guard"), 1)
                dve.wait_ge(sem("attn2_guard"), job + 1)
                v.reciprocal(r, r).then_inc(sem("attn2_inverse"), 1)
                dve.wait_ge(sem("attn2_inverse"), job + 1)
                rs = stats2[:, bb, 1]
                v.tensor_tensor(rs, rs, G48[:, :, 3 * job:3 * job + 3], ALU.mult).then_inc(sem("attn2_gated"), 1)
                dve.wait_ge(sem("attn2_gated"), job + 1)
                for tt in range(NT):
                    w = wide2[:, bb, tt]
                    v.tensor_tensor(w, w, bc(rs[:, tt, 1:3], [P, 2, S]), ALU.mult).then_inc(sem("attn2_probs"), 1)
                c = P2[:, bb, :, 512:527]
                v.tensor_tensor(c, c, rs[:, :, 0:1].broadcast_to([P, NT, 15]), ALU.mult).then_inc(sem("attn2_probs"), 1)

            def out2(job):
                dve.wait_ge(sem("attn2_mm"), job + 1)
                v.tensor_copy(Q2[:, job], acc[3][:, 1, 0:S]).then_inc(sem("attn2_out"), 1)

            mask2(0)
            mask2(1)
            for job in range(16):
                if job == 13:
                    ahead("gates2", 2)
                finish2(job)
                if job >= 2:
                    out2(job - 2)
                if job + 2 < 16:
                    mask2(job + 2)
            out2(14)
            out2(15)
            phase("gates2", None, prepared=2,
                  tail=lambda: [ahead("proj_a", 1)] + [rest(READY["mix2"], g, Q2) for g in range(4)])

            def proj_epilogue(second):
                def epilogue(i, j, p, used):
                    dve.wait_ge(mm_half, chunk_done(cur[0], j, i))
                    a = SG2[:, :, bass.ds(i * (2 * NW) + j * NW, NW)]
                    if not second:
                        v.tensor_tensor(a, acc[p][:, :, :], a, ALU.mult).then_inc(acc_used[p], 2)
                        return
                    b = SG2[:, :, bass.ds(i * (2 * NW) + (j * NW + D), NW)]
                    v.tensor_tensor(b, acc[p][:, :, :], b, ALU.mult).then_inc(acc_used[p], 2)
                    dve.wait_ge(acc_used[p], used.val(2, 2))
                    v.tensor_tensor(a, a, b, ALU.add).then_inc(sem("merging2"), 1)
                return epilogue
            phase("proj_a", proj_epilogue(False), prepared=1,
                  tail=lambda: [ahead("proj_b", 1)] + [rest(READY["proj_a"], g, LX) for g in range(4)])
            phase("proj_b", proj_epilogue(True), straight=True, prepared=1,
                  side=lambda i, j, t: fill("m2", 2 * i + j - 1) if t == 3 and 2 * i + j else None,
                  tail=lambda: [ahead("w_out", 1), rest(READY["proj_b"], 0), rest(READY["proj_b"], 1)])
            dve.wait_ge(sem("x_back"), 16)
            dve.wait_ge(sem("g1_in"), 16)

            def w_out_side(i, j, t):
                if (i, j, t) == (0, 0, 1):
                    rest(READY["proj_b"], 2)
                    fill("m2", 3)
                    rest(READY["proj_b"], 3)
                residual_fill(4, mod[:, 32:48])(i, j, t)
            phase("w_out", residual("x3_ready", gain=lambda i, j: at(80, D)[:, bass.ds(i * (2 * NW) + j * NW, NW)].unsqueeze(1).broadcast_to([P, NT, NW])),
                  straight=True, side=w_out_side, prepared=1, tail=lambda: ahead("ffn_up", 1))
            norm_mean(4)
            fill(4, 3, mod[:, 32:48])
            norm_tail(4, READY["w_out"], mod[:, 48:64])
            fcw, fcb = col("ffn_conv_w_2"), col("ffn_conv_b_2")

            def convolve(i, p, used, part):
                src = acc[p][:, :, :].rearrange("p a (b s) -> p (a b) s", b=2)
                ms = (2 * part, 2 * part + 1)
                for m in ms:
                    v.tensor_scalar(CV[:, m], src[:, m], fcw[:, bass.ds(i * 4 + (m + 96), 1)], fcb[:, bass.ds(i * 4 + m, 1)],
                                    ALU.mult, ALU.add).then_inc(sem("up_tap"), 1)
                for tap in (1, 2):
                    for m in ms:
                        before = 6 * part + 2 * (tap - 1) + m % 2 + 1
                        last = (part, tap, m % 2) == (1, 2, 1)
                        dve.wait_ge(sem("up_tap"), i * 11 + (11 if last else before))
                        op = v.scalar_tensor_tensor(CV[:, m, tap:S], src[:, m, 0:S - tap], fcw[:, bass.ds(i * 4 + (m + 48 * (2 - tap)), 1)],
                                                    CV[:, m, tap:S], ALU.mult, ALU.add)
                        if last:
                            op.then_inc(acc_used[p], 2)
                        else:
                            op.then_inc(sem("up_tap"), 1)

            def up_epilogue(i, j, p, used):
                dve.wait_ge(mm_half, chunk_done(cur[0], j, i))
                if j == 1:
                    dve.wait_ge(sem("gate_ready"), i + 1)
                    hidden(p, i, j, used)
                else:
                    convolve(i, p, used, 0)

            def up_side(i, j, t):
                if (j, t) == (1, 1):
                    convolve(i, *pair_of(cur[0], 0, i), 1)
            phase("ffn_up", up_epilogue, side=up_side, prepared=1, tail=lambda: k_weights(PH["ffn_down"], 0, 0))
            k_outer("ffn_down", KF1)
            dve.wait_ge(sem("g2_in"), 16)
            dve.wait_ge(sem("final_g_in"), 16)
            for n in range(4):
                dve.wait_ge(mm_half, PH["ffn_down"].H0 + PH["ffn_down"].hpi * PH["ffn_down"].iters - (n < 2))
                if n >= 2:
                    dve.wait_ge(sem("x4_ready"), n - 1)
                tmp = at(72 + 4 * (n % 2), NT * NW).rearrange("p (t n) -> p t n", t=NT)
                g2 = at(0, D)[:, NW * n:NW * n + NW].unsqueeze(1).broadcast_to([P, NT, NW])
                v.tensor_tensor(tmp, acc[n][:, :, :], g2, ALU.mult).then_inc(sem("down2_gated"), 1)
                dve.wait_ge(sem("down2_gated"), n + 1)
                x = X[:, :, NW * n:NW * n + NW]
                v.tensor_tensor(x, x, tmp, ALU.add).then_inc(sem("x4_ready"), 1)
            norm_mean(5)
            dve.wait_ge(sem("norm_root"), 6)
            v.reciprocal(stat[:, 12:14], stat[:, 10:12]).then_inc(sem("norm_inverse"), 1)
            dve.wait_ge(sem("norm_inverse"), 6)
            for n in range(2 * NT):
                tt, half = n // 2, slice(D // 2 * (n % 2), D // 2 * (n % 2 + 1))
                v.scalar_tensor_tensor(XN[:, tt, half], X[:, tt, half], stat[:, 12 + tt:13 + tt], at(8, D)[:, half],
                                       ALU.mult, ALU.mult).then_inc(sem("final"), 1)

        @block.tensor
        def _(pe):
            def product_phase(name, modes, straight=False, width=NW, side=None, fresh=None):
                ph = PH[name]

                def body(i, first):
                    g = 0
                    for n, b in enumerate(ph.body):
                        if b[0] == "a":
                            continue
                        _, j, tt, k0, nk = b
                        p, used = pair_of(ph, j, i)
                        mode = modes(i, j) if callable(modes) else modes
                        if tt == 0 and not (isinstance(i, int) and used.val() == 0):
                            pe.wait_ge(acc_used[p], used.val(2, 0))
                        lasttile = tt == len(ph.chunks[j]) - 1
                        if first and fresh is not None:
                            pe.wait_ge(xl_ready, fresh + (k0 + nk - 1) // 4 + 1)
                        for h, (a, e) in enumerate(halves(nk)):
                            H = half_at(ph, g, h, i)
                            ring = (ph.H0 + 2 * g + h) % 4
                            pe.wait_ge(w_lo, H.val(1, 1))
                            mm = None
                            for k in range(a, e):
                                kx = k0 + k
                                start, stop_ = tt == 0 and k == 0, lasttile and k == nk - 1
                                if mode == "tokens":
                                    for s in range(NT):
                                        o = acc[p][:, s, 0:width]
                                        xh, xl = XH[:, kx, s * P:(s + 1) * P], XL[:, kx, s * P:(s + 1) * P]
                                        wh, wl = WH[:, ring, k - a, 0:width], WL[:, ring, k - a, 0:width]
                                        pe.matmul(o, xh, wh, start=start, stop=False)
                                        pe.matmul(o, xh, wl, start=False, stop=False)
                                        mm = pe.matmul(o, xl, wh, start=False, stop=stop_)
                                elif width == NW:
                                    for m in range(4):
                                        o = acc[p][:, m // 2, (m % 2) * S:(m % 2 + 1) * S]
                                        wh = WH[:, ring, k - a, m * P:(m + 1) * P]
                                        wl = WL[:, ring, k - a, m * P:(m + 1) * P]
                                        pe.matmul(o, wh, XH[:, kx], start=start and m % 2 == 0, stop=False, skip_group_check=True)
                                        pe.matmul(o, wh, XL[:, kx], start=False, stop=False, skip_group_check=True)
                                        mm = pe.matmul(o, wl, XH[:, kx], start=False, stop=stop_, skip_group_check=True)
                                else:
                                    o, wh, wl = acc[p][0:width, 0, 0:S], WH[:, ring, k - a, 0:width], WL[:, ring, k - a, 0:width]
                                    pe.matmul(o, wh, XH[:, kx], start=start, stop=False)
                                    pe.matmul(o, wh, XL[:, kx], start=False, stop=False)
                                    mm = pe.matmul(o, wl, XH[:, kx], start=False, stop=stop_)
                            mm.then_inc(mm_half, 1)
                        g += 1
                        if side:
                            side(i, j, tt)
                    if ph.ada:
                        ada_acc = ada_place(name)[0]
                        a = At(ph.A0, 1, i)
                        pe.wait_ge(ada_mac, a.val(16, 16))
                        if not (isinstance(i, int) and a.val() == 0):
                            pe.wait_ge(ada_rowed, a.val())
                        for q in range(2):
                            mm = pe.matmul(acc[2][0:1, 0, :], one1, ada_acc[:, q], start=q == 0, stop=q == 1)
                        mm.then_inc(ada_red, 1)
                if straight:
                    for i in range(ph.iters):
                        body(i, i == 0)
                else:
                    run(pe, ph, body)

            def turn(n, g, src):
                pairs = TURN_PAIRS[n]
                if g >= (1 if pairs[0] == pairs[1] else 2):
                    pe.wait_ge(sem("xf_filled"), 4 * TURN[n] + g - (0 if pairs[0] == pairs[1] else 1))
                for k in range(4):
                    for tt in range(NT):
                        o = acc[pairs[g % 2]][:, k // 2, (k % 2) * S + tt * P:(k % 2) * S + (tt + 1) * P]
                        mm = pe.transpose(o, src[:, tt, (4 * g + k) * P:(4 * g + k + 1) * P], ident[:, :])
                mm.then_inc(sem("turned"), 1)

            def spread(n):
                pe.wait_ge(sem("norm_rows"), n + 1)
                pe.wait_ge(sem("xf_filled"), 4 * TURN[n] + 4)
                for tt in range(NT):
                    mm = pe.matmul(acc[2][:, 1, tt * P:(tt + 1) * P], root_wide[:, tt], ident[:, :], start=True, stop=True)
                mm.then_inc(sem("norm_spread"), 1)

            pe.wait_ge(sem("ident_in"), 16)
            pe.wait_ge(sem("mem_in"), 16)
            for g in range(4):
                turn(0, g, X)
            pe.wait_ge(sem("bias_wide"), 1)
            for h in range(6):
                if h >= 4:
                    pe.wait_ge(sem("bias_row"), h - 3)
                pe.matmul(acc[h % 2][:, h // 2 % 2, :], at(76, 768)[0:32, P * h:P * h + P], at(33, 512)[0:32],
                          start=True, stop=True).then_inc(sem("bias_mm"), 1)
            spread(0)
            def turn_x(i, j, t):
                n = 4 * j + t
                if n % 2:
                    if n == 1:
                        pe.wait_ge(sem("x_in"), 16)
                    turn(1, n // 2, X)
            pe.wait_ge(sem("bias_row"), 6)
            product_phase("mem", "tokens", straight=True, fresh=0, side=turn_x)
            pe.wait_ge(ada_rowed, 1)
            spread(1)
            HC = [P * h for h in range(12)] + [2304 + P * h for h in range(8)] + [3584 + P * h for h in range(4)]

            def turn_heads(n):
                g, pair = HEAD_GROUPS[n], HEAD_PAIR[n]
                if n == 4:
                    pe.wait_ge(ada_rowed, 5)
                if 0 < n < 4:
                    pe.wait_ge(sem("heads_ready"), n)
                pe.wait_ge(sem("heads_scaled"), (1, 2, 3, 4, 7, 7, 7)[n])
                if n >= 5:
                    pe.wait_ge(sem("roped"), 4)
                for k in range(4):
                    for tt in range(NT):
                        rows = KC[:, tt, P * k:P * k + P] if g == 6 else Z[:, tt, HC[4 * g + k]:HC[4 * g + k] + P]
                        mm = pe.transpose(acc[pair][:, k // 2, (k % 2) * S + tt * P:(k % 2) * S + (tt + 1) * P], rows, ident[:, :])
                mm.then_inc(sem("heads_turned"), 1)

            product_phase("qkv", "tokens", straight=True, fresh=READY["mem"],
                          side=lambda i, j, t: turn_heads(2 * i + j - 1) if t == 0 and 1 <= 2 * i + j <= 4 else None)
            for p in range(2):
                pe.wait_ge(acc_used[p], 2 * c_end("qkv", p))
            pe.wait_ge(sem("heads_ready"), 4)
            pe.wait_ge(sem("bias_ready"), 4)

            def keys1(job):
                if job < 2:
                    return [(2 * g + job, 6 + 2 * g + job, lambda kt, h=2 * g + job: Z[:, kt, 1536 + P * h:1536 + P * h + P])
                            for g in range(3)]
                if job < 6:
                    h = job - 2
                    return [(20 + h, 24 + h, lambda kt: VC[:, kt, P * h:P * h + P])]
                h = job - 6
                return [(12 + h, 18 + h // 3, lambda kt: Z[:, kt, 3328 + P * (h // 3):3328 + P * (h // 3) + P])]

            def scores1(job):
                for tt in range(NT):
                    if job >= 1:
                        pe.wait_ge(sem("attn1_exp"), 2 * (job - 1) + tt + 1)
                    for g, (q, k, _) in enumerate(keys1(job)):
                        mm = pe.matmul(acc[tt][:, g // 2, (g % 2) * S:(g % 2 + 1) * S], QK[:, q, tt * P:(tt + 1) * P], QK[:, k],
                                       start=True, stop=True)
                    mm.then_inc(sem("attn1_scores"), 1)

            def turn1(job):
                pe.wait_ge(sem("attn1_probs"), job + 1)
                if job:
                    pe.wait_ge(sem("attn1_pt"), pt_count(job - 1))
                for g in range(len(keys1(job))):
                    for kt in range(NT):
                        n = 2 * g + kt
                        for tt in range(NT):
                            o = acc[2 + n // 4][:, (n % 4) // 2, (n % 2) * S + tt * P:(n % 2) * S + (tt + 1) * P]
                            mm = pe.transpose(o, probs1(job)[:, tt, S * g + P * kt:S * g + P * kt + P], ident[:, :])
                mm.then_inc(sem("attn1_turned"), 1)

            def values1(job):
                segs = keys1(job)
                pe.wait_ge(sem("attn1_pt"), pt_count(job))
                if job:
                    pe.wait_ge(sem("attn1_out"), job)
                for g, (_, _, value) in enumerate(segs):
                    for kt in range(NT):
                        n = 2 * g + kt
                        mm = pe.matmul(acc[3][:, 1, 0:S], value(kt), PT1[:, job % 2, n], start=n == 0, stop=n == 2 * len(segs) - 1)
                mm.then_inc(sem("attn1_mm"), 1)

            def pt_count(job):
                return 2 * min(job + 1, 2) + max(job - 1, 0)

            scores1(0)
            scores1(1)
            turn_heads(4)
            pe.wait_ge(sem("heads_ready"), 5)
            scores1(2)
            for job in range(12):
                turn1(job)
                if job:
                    values1(job - 1)
                if job == 3:
                    pe.wait_ge(sem("attn1_pt"), pt_count(3))
                    turn_heads(5)
                    pe.wait_ge(sem("attn1_out"), 3)
                    turn_heads(6)
                    pe.wait_ge(sem("heads_ready"), 7)
                if job + 3 < 12:
                    scores1(job + 3)
            values1(11)
            pe.wait_ge(sem("attn1_out"), 12)
            product_phase("gates", "tokens")

            def merged_turn(i, j, t):
                if i and (j, t) == (1, 0):
                    pe.wait_ge(sem("merging1"), 2 * i)
                    if i == 1:
                        pe.wait_ge(ada_rowed, 11)
                    turn("m1", i - 1, M)
            product_phase("branch", "tokens", straight=True, fresh=READY["gates"], side=merged_turn)

            def residual_turn(n):
                def side(i, j, t):
                    c = 2 * i + j - 1
                    if t == 1 and c >= 0:
                        C = PH["w_o" if n == 2 else "w_out"].C0 + c
                        pe.wait_ge(acc_used[C % 2], 2 * (C // 2 + 1))
                        if n == 4:
                            pe.wait_ge(sem("x3_ready"), c + 1)
                        turn(n, c, X)
                return side

            def w_o_side(i, j, t):
                if (i, j, t) == (0, 0, 0):
                    pe.wait_ge(sem("merging1"), 8)
                    turn("m1", 3, M)
                residual_turn(2)(i, j, t)
            product_phase("w_o", "tokens", straight=True, fresh=READY["branch"], side=w_o_side)
            residual_turn(2)(2, 0, 1)
            pe.wait_ge(ada_rowed, 13)
            spread(2)
            product_phase("ffn_in", "features", fresh=READY["w_o"])

            def k_outer(name, base):
                ph = PH[name]
                for p in range(2):
                    pe.wait_ge(acc_used[p], 2 * c_end(before[name], p))

                def body(i, first):
                    for j in range(4):
                        pe.wait_ge(sem("hidden_rest"), At(base + j, 4, i).val(1, 1))
                        for h in range(2):
                            H = At(ph.H0 + 2 * j + h, 8, i)
                            ring = (ph.H0 + 2 * j + h) % 4
                            pe.wait_ge(w_lo, H.val(1, 1))
                            for nn in range(2):
                                for s in range(NT):
                                    o = acc[2 * h + nn][:, s, :]
                                    xh, xl = XH[:, j, s * P:(s + 1) * P], XL[:, j, s * P:(s + 1) * P]
                                    st = first and j == 0
                                    pe.matmul(o, xh, WH[:, ring, nn], start=st, stop=False, skip_group_check=True)
                                    pe.matmul(o, xh, WL[:, ring, nn], start=False, stop=False, skip_group_check=True)
                                    mm = pe.matmul(o, xl, WH[:, ring, nn], start=False, stop=True, skip_group_check=True)
                            mm.then_inc(mm_half, 1)
                run(pe, ph, body)
            before = {"ffn_out": "ffn_in", "ffn_down": "ffn_up"}
            pe.wait_ge(ada_rowed, ADA_CHUNKS)
            pe.wait_ge(sem("mod_in"), 64)
            pe.transpose(acc[2][:, 1, 0:64], at(88, P)[0:64], ident[0:64, 0:64]).then_inc(sem("mod_turned"), 1)
            pe.wait_ge(sem("mod_copied"), 1)
            k_outer("ffn_out", 0)
            for g in range(4):
                pe.wait_ge(sem("x2_ready"), g + 1)
                turn(3, g, X)
            spread(3)
            product_phase("lru_x", "features", fresh=READY["ffn_in"])

            def lru_gate_products(b, n):
                k = 4 * b + n
                pe.wait_ge(sem("lru_w_in"), 32)
                pe.wait_ge(sem("conv_tap"), 16 * b + 12 + n + 1)
                if k >= 2:
                    pe.wait_ge(sem("lru_r"), 2 * (k - 1))
                pe.matmul(acc[2 + k % 2][:, 0, 0:S], X[:, 0, P * k:P * k + P], UT2[b % 2][:, n], start=True, stop=True)
                pe.matmul(acc[2 + k % 2][:, 0, S:2 * S], X[:, 1, P * k:P * k + P], UT2[b % 2][:, n], start=True, stop=True).then_inc(sem("lru_gates"), 1)

            def compress(m, part):
                if part == 0:
                    pe.wait_ge(sem("cmp_blocks"), 2 * m + 2)
                    pe.wait_ge(sem(f"cmp_in{m}"), 16)
                for l in range(8 * part, 8 * part + 8):
                    half = l // 16
                    rows = BLOCKS[:, m, half].rearrange("p (g w l) -> p g w l", g=4, l=16)[:, :, half:half + 15, l % 16]
                    mm = pe.matmul(acc[2 + m][:, 1, 0:60].rearrange("p (g w) -> p g w", g=4), W1[m][:, P * l:P * l + P], rows,
                                   start=l == 0, stop=l == 31)
                if part == 3:
                    mm.then_inc(sem("cmp_hid"), 1)

            def lru_side(n):
                for b in range(4):
                    if n - 8 * b in (3, 4):
                        lru_gate_products(b, 2 * (n - 8 * b - 3))
                        lru_gate_products(b, 2 * (n - 8 * b - 3) + 1)
                if 42 <= n < 50:
                    compress((n - 42) // 4, (n - 42) % 4)
                if n == 52:
                    pe.wait_ge(sem("cmp2_in"), 32)
                    pe.wait_ge(sem("cmp_gelu"), 2)
                    pe.matmul(acc[2][:, 1, 64:124], CMP_W2[:, 0], CMP_HID[:, 0, 0:60], start=True, stop=True).then_inc(sem("cmp_done"), 1)
                    for g in range(4):
                        mm = pe.matmul(acc[3][0:15, 1, P * g:P * g + P], CMP_HID[:, 1, 15 * g:15 * g + 15], CMP_W2[:, 1], start=True, stop=True)
                    mm.then_inc(sem("cmp_done"), 1)

            def under(name):
                return lambda i, j, t: lru_side(SIDE0[name] + 8 * i + 4 * j + t)
            product_phase("lru_y", "features", straight=True, side=under("lru_y"))
            product_phase("q2", "features", straight=True, side=under("q2"))
            product_phase("kv2", lambda i, j: ("features", "features", "features", "tokens", "features", "tokens")[2 * i + j],
                          straight=True, side=under("kv2"))
            product_phase("g48", "features", width=48)
            for p in range(2):
                pe.wait_ge(acc_used[p], 2 * c_end("g48", p))
            pe.wait_ge(sem("cmp_kept"), 2)
            for tt in range(NT):
                mm = pe.transpose(acc[3][:, 0, 48 * tt:48 * tt + 48], GATE_ROWS[:, P * tt:P * tt + P], ident[0:48, 0:48])
            mm.then_inc(sem("gates48_turned"), 1)

            def scores2(job):
                kv = job // 4
                for tt in range(NT):
                    if job >= 1:
                        pe.wait_ge(sem("attn2_masked"), 2 * (job - 1) + tt + 1)
                    q = Q2[:, job, tt * P:(tt + 1) * P]
                    pe.matmul(acc[tt][:, 0, 0:S], q, KS2[:, kv], start=True, stop=True)
                    pe.matmul(acc[tt][:, 0, S:2 * S], q, KW2[:, kv], start=True, stop=True)
                    pe.matmul(acc[tt][:, 1, 0:15], q, KCMP[:, 15 * kv:15 * kv + 15], start=True, stop=True).then_inc(sem("attn2_scores"), 1)

            def turn2(job):
                bb = job % 3
                pe.wait_ge(sem("attn2_probs"), 3 * job + 3)
                if job == 0:
                    pe.wait_ge(sem("gates48_kept"), 1)
                if job:
                    pe.wait_ge(sem("attn2_pt"), 2 * job)
                for g in range(2):
                    for kt in range(NT):
                        n = 2 * g + kt
                        for tt in range(kt, NT):
                            pe.transpose(acc[2][:, n // 2, (n % 2) * S + tt * P:(n % 2) * S + (tt + 1) * P],
                                         P2[:, bb, tt, S * g + P * kt:S * g + P * kt + P], ident[:, :])
                for tt in range(NT):
                    mm = pe.transpose(acc[3][0:15, 0, tt * P:(tt + 1) * P], P2[:, bb, tt, 512:527], ident[:, :])
                mm.then_inc(sem("attn2_turned"), 1)

            def values2(job):
                kv, bb = job // 4, job % 2
                pe.wait_ge(sem("attn2_pt"), 2 * job + 2)
                if job:
                    pe.wait_ge(sem("attn2_out"), job)
                o = acc[3][:, 1, 0:S]
                for n, values in ((0, VS2), (2, VW2)):
                    for kt in range(NT):
                        pe.matmul(o[:, P * kt:S], values[:, kt, P * kv:P * kv + P], PT2[:, bb, n + kt, P * kt:S], start=(n, kt) == (0, 0), stop=False)
                pe.matmul(o, VCMP[0:15, P * kv:P * kv + P], PC2[0:15, bb], start=False, stop=True).then_inc(sem("attn2_mm"), 1)

            for job in range(3):
                scores2(job)
            for job in range(16):
                turn2(job)
                if job:
                    values2(job - 1)
                if job + 3 < 16:
                    scores2(job + 3)
            values2(15)
            pe.wait_ge(sem("attn2_out"), 16)
            product_phase("gates2", "tokens")
            product_phase("proj_a", "tokens", fresh=READY["mix2"])

            def turn_merged(i, j, t):
                c = 2 * i + j - 1
                if t == 1 and c >= 0:
                    pe.wait_ge(sem("merging2"), c + 1)
                    turn("m2", c, SG2)
            product_phase("proj_b", "tokens", fresh=READY["proj_a"], straight=True, side=turn_merged)

            def w_out_side(i, j, t):
                if (i, j, t) == (0, 0, 0):
                    turn_merged(2, 0, 1)
                residual_turn(4)(i, j, t)
            product_phase("w_out", "tokens", straight=True, fresh=READY["proj_b"], side=w_out_side)
            residual_turn(4)(2, 0, 1)
            spread(4)
            product_phase("ffn_up", "features", fresh=READY["w_out"])
            k_outer("ffn_down", KF1)


def _bucket(rel):
    nb, max_dist = 16, 1024
    n = np.abs(rel)
    large = nb // 2 + (np.log(np.maximum(n, 1).astype(np.float32) / np.float32(nb // 2))
                       / np.float32(np.log(max_dist / (nb // 2))) * np.float32(nb - nb // 2)).astype(np.int32)
    return np.where(rel > 0, nb, 0) + np.where(n < nb // 2, n, np.minimum(large, nb - 1))


def _constants():
    pos = np.arange(S)
    diff = np.arange(-255, 256)
    one_hot = np.zeros((32, 512), np.float32)
    one_hot[_bucket(diff), diff + 255] = 1.0
    rel = pos[None, :] - pos[:, None]
    ok = [np.abs(rel) <= 64] + [(rel % dil == 0) & (np.abs(rel) // dil <= 64) for dil in (4, 16)]
    masks_a = np.stack([np.where(m, 0.0, NEG) for m in ok]).astype(np.float32)
    masks_a = masks_a.reshape(3, NT, P, S).transpose(2, 1, 0, 3).reshape(P, -1)
    causal = np.where(rel <= 0, 0.0, NEG)
    ends = np.arange(15) * 16 + 31
    cmp = np.where(ends[None, :] <= pos[:, None], 0.0, NEG)
    masks_2 = np.concatenate([causal, causal, cmp], 1).astype(np.float32)
    masks_2 = masks_2.reshape(NT, P, 527).transpose(1, 0, 2).reshape(P, -1)
    inv = np.float32(10000.0) ** (-np.arange(32, dtype=np.float32) / np.float32(32))
    r, c = (pos // 64).astype(np.float32), (pos % 64).astype(np.float32)
    ang = np.concatenate([r[:, None] * inv, c[:, None] * inv], 1).astype(np.float32)
    rope = np.stack([np.cos(ang), np.sin(ang)], 1).astype(np.float32)
    rope = rope.reshape(NT, P, 2, 64).transpose(1, 0, 2, 3).reshape(P, -1)
    return {"identity": np.eye(P, dtype=np.float32), "one_hot": one_hot, "masks_a": masks_a, "masks_2": masks_2,
            "rope": rope}


_AS_IS = ["rel_bias"]
_FIRST = ["w_in", "g_qb", "g_kb", "w_mem_kv", "w_br_a", "w_br_b", "w_br_c", "w_o", "w_ffn_in", "w_ffn_out",
          "ada_w_2", "w_in_2", "cmp_w1_k_2", "cmp_w2_k_2", "cmp_w1_v_2", "cmp_w2_v_2", "lru_wa_2", "lru_wi_2",
          "proj_a_2", "proj_b_2", "w_out_2", "ffn_up_2", "ffn_down_2", "x", "mem"]


def _inputs(inputs):
    a = {n: np.ascontiguousarray(inputs[n]) for n in _AS_IS}
    a |= {n: np.ascontiguousarray(inputs[n][0]) for n in _FIRST}
    a["g_qb"], a["g_kb"] = a["g_qb"].reshape(HD), a["g_kb"].reshape(HD)
    a["ada_b_2"] = np.ascontiguousarray(inputs["ada_b_2"]).reshape(1, -1)
    a["final_g_2"] = np.ascontiguousarray(inputs["final_g_2"]).reshape(-1)
    a["vectors"] = np.ascontiguousarray(np.concatenate(
        [np.asarray(inputs[n]).reshape(-1, P) for n, _ in VECTORS]).T)
    a |= _constants()
    return a


def build(nc, a):
    t = {n: nc.dram_tensor(f"in_{n}", v.shape, mybir.dt.from_np(v.dtype), kind="ExternalInput").ap()
         for n, v in a.items()}
    out = nc.dram_tensor("out_0", (S, D), F32, kind="ExternalOutput").ap()
    two_block_program(nc, t, out)


def kernel(**inputs):
    import concourse.bacc as bacc
    from concourse.bass_utils import run_bass_kernel_spmd

    a = _inputs(inputs)
    nc = bacc.Bacc("TRN2", target_bir_lowering=False, num_devices=1)
    build(nc, a)
    r = run_bass_kernel_spmd(nc, [{f"in_{n}": v for n, v in a.items()}], core_ids=[0])
    return r.results[0]["out_0"].reshape(1, S, D)
```
